# Optimizing a Trainium2 kernel written in Bass

```python
import math
import jax, jax.numpy as jnp
from jax import lax
import numpy as np

D_MODEL = 1024
BATCH = 1
SEQ = 1024
DEPTH = 1

PLE_DIM = 256
EPS = 1e-6
GN_EPS = 1e-5
NEG = -1e30

RET_HEADS = 8
RET_DV = D_MODEL // RET_HEADS
RET_DK = RET_DV // 2
RET_CHUNK = 128

NSA_HEADS = 16
NSA_GROUPS = 2
NSA_HPG = NSA_HEADS // NSA_GROUPS
NSA_DV = D_MODEL // NSA_HEADS
NSA_DK = 3 * NSA_DV // 2
CMP_LEN = 32
CMP_STRIDE = 16
SEL_LEN = 64
SEL_TOPN = 16
WINDOW = 512
NSA_Q_BLOCK = 32

D_FF = -(-8 * D_MODEL // (3 * 256)) * 256

IN_SPLITS = (
    RET_HEADS * RET_DK,
    RET_HEADS * RET_DK,
    RET_HEADS * RET_DV,
    RET_HEADS * RET_DV,
    NSA_HEADS * NSA_DK,
    NSA_GROUPS * NSA_DK,
    NSA_GROUPS * NSA_DV,
    NSA_GROUPS * NSA_DK,
    NSA_GROUPS * NSA_DV,
    NSA_GROUPS * NSA_DK,
    NSA_GROUPS * NSA_DV,
    3 * NSA_HEADS,
    2 * D_MODEL,
)
IN_TOTAL = sum(IN_SPLITS)

kernel_name = "hybrid_retention_nsa_block"

def rms(x):
    xf = x.astype(jnp.float32)
    return (xf * lax.rsqrt(jnp.mean(xf * xf, axis=-1, keepdims=True) + EPS)).astype(x.dtype)

def rms_norm(x, g):
    xf = x.astype(jnp.float32)
    y = xf * lax.rsqrt(jnp.mean(xf * xf, axis=-1, keepdims=True) + EPS)
    return (y * g.astype(jnp.float32)).astype(x.dtype)

def retention(q, k, v):
    B_, S, H, dk = q.shape
    dv = v.shape[-1]
    n_chunks = S // RET_CHUNK
    qf = q.astype(jnp.float32)
    kf = k.astype(jnp.float32) * (dk ** -0.5)
    vf = v.astype(jnp.float32)

    def to_chunks(t):
        return t.reshape(B_, n_chunks, RET_CHUNK, H, t.shape[-1]).transpose(1, 0, 3, 2, 4)

    qc, kc, vc = to_chunks(qf), to_chunks(kf), to_chunks(vf)
    log_g = jnp.log1p(-(2.0 ** (-5.0 - jnp.arange(H, dtype=jnp.float32))))
    idx = jnp.arange(RET_CHUNK, dtype=jnp.float32)
    diff = idx[:, None] - idx[None, :]
    dmat = jnp.exp(log_g[:, None, None] * jnp.maximum(diff, 0.0)) * (diff >= 0)
    xi = jnp.exp(log_g[:, None] * (idx + 1.0))
    zeta = jnp.exp(log_g[:, None] * (RET_CHUNK - 1.0 - idx))
    chunk_decay = jnp.exp(log_g * RET_CHUNK)

    def step(R, inp):
        qi, ki, vi = inp
        inner = jnp.einsum('bhcd,bhsd->bhcs', qi, ki) * dmat[None]
        o = (jnp.einsum('bhcs,bhse->bhce', inner, vi)
             + jnp.einsum('bhcd,bhde->bhce', qi, R) * xi[None, :, :, None])
        R = (R * chunk_decay[None, :, None, None]
             + jnp.einsum('bhsd,bhse->bhde', ki * zeta[None, :, :, None], vi))
        return R, o

    R0 = jnp.zeros((B_, H, dk, dv), jnp.float32)
    _, o = lax.scan(step, R0, (qc, kc, vc))
    return o.transpose(1, 0, 3, 2, 4).reshape(B_, S, H, dv)

def group_norm_heads(o, g):
    mu = jnp.mean(o, axis=-1, keepdims=True)
    var = jnp.mean(jnp.square(o - mu), axis=-1, keepdims=True)
    y = (o - mu) * lax.rsqrt(var + GN_EPS)
    B_, S, H, dv = o.shape
    return y.reshape(B_, S, H * dv) * g.astype(jnp.float32)

def compress_blocks(src, pe, w1, w2):
    B_, S, G, d = src.shape
    n_cmp = (S - CMP_LEN) // CMP_STRIDE + 1
    idx = jnp.arange(n_cmp)[:, None] * CMP_STRIDE + jnp.arange(CMP_LEN)[None, :]
    blocks = src[:, idx] + pe[:, None, :]
    blocks = blocks.transpose(0, 3, 1, 2, 4).reshape(B_, G, n_cmp, CMP_LEN * d)
    return jax.nn.gelu(blocks @ w1) @ w2

def masked_softmax(s, mask):
    s = jnp.where(mask, s.astype(jnp.float32), NEG)
    return jax.nn.softmax(s, axis=-1) * mask

def gather_blocks(blocks, idx):
    return blocks[idx]

def nsa_attention(q, k_c, v_c, k_s, v_s, k_w, v_w, gates,
                  pe_k, w1_k, w2_k, pe_v, w1_v, w2_v):
    B_, S, H, dk = q.shape
    G, hpg, dv = NSA_GROUPS, NSA_HPG, NSA_DV
    scale = dk ** -0.5
    slopes = (2.0 ** (-8.0 * (jnp.arange(H, dtype=jnp.float32) + 1.0) / H)).reshape(G, hpg)
    sl = slopes[None, :, :, None, None]

    k_cmp = compress_blocks(k_c, pe_k, w1_k, w2_k)
    v_cmp = compress_blocks(v_c, pe_v, w1_v, w2_v)
    n_cmp = k_cmp.shape[2]
    cmp_start = jnp.arange(n_cmp) * CMP_STRIDE
    cmp_end = cmp_start + CMP_LEN - 1

    n_sel = S // SEL_LEN
    topn = min(SEL_TOPN, n_sel)
    sel_start = jnp.arange(n_sel) * SEL_LEN
    overlap = ((cmp_start[:, None] < sel_start[None, :] + SEL_LEN)
               & (cmp_start[:, None] + CMP_LEN > sel_start[None, :])).astype(jnp.float32)
    ks_blocks = k_s.reshape(B_, n_sel, SEL_LEN, G, dk).transpose(0, 3, 1, 2, 4)
    vs_blocks = v_s.reshape(B_, n_sel, SEL_LEN, G, dv).transpose(0, 3, 1, 2, 4)

    kw_pad = jnp.pad(k_w.transpose(0, 2, 1, 3), ((0, 0), (0, 0), (WINDOW, 0), (0, 0)))
    vw_pad = jnp.pad(v_w.transpose(0, 2, 1, 3), ((0, 0), (0, 0), (WINDOW, 0), (0, 0)))

    n_q = S // NSA_Q_BLOCK
    q_chunks = q.reshape(B_, n_q, NSA_Q_BLOCK, G, hpg, dk).transpose(1, 0, 3, 4, 2, 5)
    g_chunks = gates.reshape(B_, n_q, NSA_Q_BLOCK, 3, G, hpg).transpose(1, 3, 0, 4, 5, 2)
    c_ids = jnp.arange(n_q, dtype=jnp.int32)

    def one_block(inp):
        c, qg, gg = inp
        t = c * NSA_Q_BLOCK + jnp.arange(NSA_Q_BLOCK)
        tf = t.astype(jnp.float32)

        s_c = jnp.einsum('bghtd,bgnd->bghtn', qg, k_cmp) * scale
        s_c = s_c - sl * (tf[:, None] - cmp_end[None, :].astype(jnp.float32))
        valid_c = cmp_end[None, :] <= t[:, None]
        p_c = masked_softmax(s_c, valid_c)
        o_c = jnp.einsum('bghtn,bgne->bghte', p_c, v_cmp.astype(jnp.float32))

        imp = jnp.einsum('bgtn,nj->bgtj', jnp.sum(p_c, axis=2), overlap)
        blk = jnp.arange(n_sel)
        cur = t // SEL_LEN
        valid_s = sel_start[None, :] <= t[:, None]
        forced = (blk[None, :] == 0) | (blk[None, :] == cur[:, None]) | (blk[None, :] == cur[:, None] - 1)
        score = jnp.where(forced, 1e6, jnp.where(valid_s, imp, -1e6))
        _, sel = lax.top_k(score, topn)
        k_g = jax.vmap(jax.vmap(gather_blocks))(ks_blocks, sel).reshape(B_, G, NSA_Q_BLOCK, topn * SEL_LEN, dk)
        v_g = jax.vmap(jax.vmap(gather_blocks))(vs_blocks, sel).reshape(B_, G, NSA_Q_BLOCK, topn * SEL_LEN, dv)
        pos_s = (sel[..., None] * SEL_LEN + jnp.arange(SEL_LEN)).reshape(B_, G, NSA_Q_BLOCK, topn * SEL_LEN)
        s_s = jnp.einsum('bghtd,bgtkd->bghtk', qg, k_g) * scale
        s_s = s_s - sl * (tf[None, None, None, :, None] - pos_s[:, :, None].astype(jnp.float32))
        valid_sel = (pos_s <= t[None, None, :, None])[:, :, None]
        p_s = masked_softmax(s_s, valid_sel)
        o_s = jnp.einsum('bghtk,bgtke->bghte', p_s, v_g.astype(jnp.float32))

        start = c * NSA_Q_BLOCK
        k_win = lax.dynamic_slice_in_dim(kw_pad, start, NSA_Q_BLOCK + WINDOW, axis=2)
        v_win = lax.dynamic_slice_in_dim(vw_pad, start, NSA_Q_BLOCK + WINDOW, axis=2)
        pos_w = start - WINDOW + jnp.arange(NSA_Q_BLOCK + WINDOW)
        s_w = jnp.einsum('bghtd,bgkd->bghtk', qg, k_win) * scale
        s_w = s_w - sl * (tf[:, None] - pos_w[None, :].astype(jnp.float32))
        valid_w = (pos_w[None, :] <= t[:, None]) & (pos_w[None, :] > t[:, None] - WINDOW) & (pos_w[None, :] >= 0)
        p_w = masked_softmax(s_w, valid_w)
        o_w = jnp.einsum('bghtk,bgke->bghte', p_w, v_win.astype(jnp.float32))

        gf = gg.astype(jnp.float32)[..., None]
        return gf[0] * o_c + gf[1] * o_s + gf[2] * o_w

    out = lax.map(one_block, (c_ids, q_chunks, g_chunks))
    out = out.transpose(1, 0, 4, 2, 3, 5).reshape(B_, S, H * dv)
    return out.astype(q.dtype)

def setup_inputs(seed: int = 0) -> dict:
    key = jax.random.key(seed)
    ks = jax.random.split(key, 20)
    f32 = jnp.float32

    def w(k, shape, fan_in):
        return jax.random.normal(k, shape, f32) * (fan_in ** -0.5)

    def gain(k, shape):
        return 1.0 + 0.05 * jax.random.normal(k, shape, f32)

    return {
        "x": jax.random.normal(ks[0], (BATCH, SEQ, D_MODEL), f32),
        "p": jax.random.normal(ks[1], (DEPTH, BATCH, SEQ, PLE_DIM), f32),
        "norm_mix_pre": gain(ks[2], (DEPTH, D_MODEL)),
        "norm_mix_post": gain(ks[3], (DEPTH, D_MODEL)),
        "norm_ffn_pre": gain(ks[4], (DEPTH, D_MODEL)),
        "norm_ffn_post": gain(ks[5], (DEPTH, D_MODEL)),
        "w_in": w(ks[6], (DEPTH, D_MODEL, IN_TOTAL), D_MODEL),
        "ret_gn_g": gain(ks[7], (DEPTH, RET_HEADS * RET_DV)),
        "cmp_pe_k": 0.1 * jax.random.normal(ks[8], (DEPTH, CMP_LEN, NSA_DK), f32),
        "cmp_w1_k": w(ks[9], (DEPTH, CMP_LEN * NSA_DK, NSA_DK), CMP_LEN * NSA_DK),
        "cmp_w2_k": w(ks[10], (DEPTH, NSA_DK, NSA_DK), NSA_DK),
        "cmp_pe_v": 0.1 * jax.random.normal(ks[11], (DEPTH, CMP_LEN, NSA_DV), f32),
        "cmp_w1_v": w(ks[12], (DEPTH, CMP_LEN * NSA_DV, NSA_DV), CMP_LEN * NSA_DV),
        "cmp_w2_v": w(ks[13], (DEPTH, NSA_DV, NSA_DV), NSA_DV),
        "w_out": w(ks[14], (DEPTH, D_MODEL, D_MODEL), D_MODEL),
        "w_ffn_in": w(ks[15], (DEPTH, D_MODEL, 2 * D_FF), D_MODEL),
        "w_ffn_out": w(ks[16], (DEPTH, D_FF, D_MODEL), D_FF),
        "w_ple": w(ks[17], (DEPTH, PLE_DIM, D_MODEL), PLE_DIM),
        "w_ple_gate": w(ks[18], (DEPTH, D_MODEL, D_MODEL), D_MODEL),
    }

def reference(x, p, norm_mix_pre, norm_mix_post, norm_ffn_pre, norm_ffn_post, w_in, ret_gn_g,
              cmp_pe_k, cmp_w1_k, cmp_w2_k, cmp_pe_v, cmp_w1_v, cmp_w2_v,
              w_out, w_ffn_in, w_ffn_out, w_ple, w_ple_gate):
    B_, S, _ = x.shape
    offsets = [int(o) for o in np.cumsum(IN_SPLITS)[:-1]]
    for i in range(DEPTH):
        h = rms_norm(x, norm_mix_pre[i])
        proj = h @ w_in[i]
        (r_q, r_k, r_v, r_g, n_q, kc, vc, ks_, vs_, kw, vw, n_g, m_g) = jnp.split(proj, offsets, axis=-1)

        ret = retention(r_q.reshape(B_, S, RET_HEADS, RET_DK),
                        r_k.reshape(B_, S, RET_HEADS, RET_DK),
                        r_v.reshape(B_, S, RET_HEADS, RET_DV))
        ret = (jax.nn.silu(r_g.astype(jnp.float32)) * group_norm_heads(ret, ret_gn_g[i])).astype(x.dtype)

        nsa = nsa_attention(
            n_q.reshape(B_, S, NSA_HEADS, NSA_DK),
            kc.reshape(B_, S, NSA_GROUPS, NSA_DK), vc.reshape(B_, S, NSA_GROUPS, NSA_DV),
            ks_.reshape(B_, S, NSA_GROUPS, NSA_DK), vs_.reshape(B_, S, NSA_GROUPS, NSA_DV),
            kw.reshape(B_, S, NSA_GROUPS, NSA_DK), vw.reshape(B_, S, NSA_GROUPS, NSA_DV),
            jax.nn.sigmoid(n_g).reshape(B_, S, 3, NSA_HEADS),
            cmp_pe_k[i], cmp_w1_k[i], cmp_w2_k[i], cmp_pe_v[i], cmp_w1_v[i], cmp_w2_v[i])

        g_a, g_b = jnp.split(jax.nn.sigmoid(m_g), 2, axis=-1)
        mix = (g_a * ret + g_b * nsa) @ w_out[i]
        x = x + rms_norm(mix, norm_mix_post[i])

        h = rms_norm(x, norm_ffn_pre[i])
        u, v = jnp.split(h @ w_ffn_in[i], 2, axis=-1)
        f = (jax.nn.silu(u) * v) @ w_ffn_out[i]
        x = x + rms_norm(f, norm_ffn_post[i])

        gate = jax.nn.sigmoid(rms(x) @ w_ple_gate[i])
        x = x + gate * (p[i] @ w_ple[i])
    return x


_drawn_inputs = setup_inputs


def setup_inputs(seed=0):
    import zlib

    import numpy as np

    out = dict(_drawn_inputs(seed))
    spreads = {}
    factors = {'cmp_pe_k': 8.0}
    for name, (base, spread) in spreads.items():
        noise = np.random.default_rng([zlib.crc32(name.encode()), seed]).standard_normal(out[name].shape)
        drawn = base * np.exp(spread * noise) if base else spread * noise
        out[name] = __import__('jax').numpy.asarray(drawn.astype(out[name].dtype))
    for name, factor in factors.items():
        out[name] = (out[name] * factor).astype(out[name].dtype)
    return out
```

```python
from contextlib import ExitStack

import numpy as np
import concourse.bass as bass
from concourse import mybir

F32 = mybir.dt.float32
F32R = mybir.dt.float32r
ALU = mybir.AluOpType
ACT = mybir.ActivationFunctionType

P = 128
SEQ, DM = 1024, 1024
NT, NK = SEQ // P, DM // P
HALF = 512
EPS, GN_EPS = 1e-6, 1e-5
RH, RDK, RDV = 8, 64, 128
NH, NG, DK, DV = 16, 2, 96, 64
HPG = NH // NG
CMP_LEN, CMP_STRIDE = 32, 16
NCMP = (SEQ - CMP_LEN) // CMP_STRIDE + 1
NB = SEQ // CMP_STRIDE
WINDOW = 512
WB = WINDOW // P
DFF = 2816
NF = DFF // P
PLE = 256
BIG = 1e30

C_RQ = 0
C_RK = C_RQ + RH * RDK
C_RV = C_RK + RH * RDK
C_RG = C_RV + RH * RDV
C_NQ = C_RG + RH * RDV
C_KC = C_NQ + NH * DK
C_VC = C_KC + NG * DK
C_KS = C_VC + NG * DV
C_VS = C_KS + NG * DK
C_KW = C_VS + NG * DV
C_VW = C_KW + NG * DK
C_NGATE = C_VW + NG * DV
C_MA = C_NGATE + 3 * NH
C_MB = C_MA + DM

_PARTS = [("slope", NH), ("qscale", NH), ("valid", 1), ("xi", RH), ("zeta", RH), ("decay", RH // 2),
          ("ident", P), ("dsel", SEQ), ("dwin", WINDOW + P), ("dcmp", NB + (NT - 1) * 8), ("dmat", RH * P)]
CONST_AT, _n = {}, 0
for _name, _w in _PARTS:
    CONST_AT[_name] = (_n, _n + _w)
    _n += _w
CONST_W = _n
SMALL_W = CONST_AT["ident"][0]


def shape_constants():
    c = np.zeros((P, CONST_W), np.float64)

    def put(name, value):
        a, b = CONST_AT[name]
        c[:, a:b] = value

    q = np.arange(P)[:, None]
    put("ident", np.eye(P))
    d = q + (SEQ - P) - np.arange(SEQ)[None, :]
    put("dsel", np.where(d >= 0, d, BIG))
    d = q + WINDOW - np.arange(WINDOW + P)[None, :]
    put("dwin", np.where((d >= 0) & (d < WINDOW), d, BIG))
    v = np.arange(NB + (NT - 1) * 8)[None, :] - (NT - 1) * 8
    d = q - CMP_STRIDE * v - (CMP_LEN - 1)
    put("dcmp", np.where(d >= 0, d, BIG))
    slope = 2.0 ** (-8.0 * (np.arange(NH) + 1.0) / NH)
    put("slope", slope[None, :])
    put("qscale", -(DK ** -0.5) / slope[None, :])
    put("valid", q >= CMP_LEN - 1)
    log_g = np.log1p(-(2.0 ** (-5.0 - np.arange(RH))))
    s, t = np.arange(P)[:, None, None], np.arange(P)[None, None, :]
    dmat = np.where(t >= s, np.exp(-log_g[None, :, None] * (s + 1.0)) * RDK ** -0.5, 0.0)
    put("dmat", np.broadcast_to(dmat, (P, RH, P)).reshape(P, RH * P))
    put("xi", np.exp(log_g[None, :] * (q + 1.0)))
    put("zeta", np.exp(log_g[None, :] * (P - 1.0 - q)) * RDK ** -0.5)
    decay = np.exp(log_g * P)
    put("decay", np.where(q < RDK, decay[None, 0::2], decay[None, 1::2]))
    return c.astype(np.float32)


def above_zero(engine, sem, value):
    if not (isinstance(value, int) and value <= 0):
        engine.wait_ge(sem, value)


class Core:

    def const(self, name):
        a, b = CONST_AT[name]
        return self.small[:, a:b]


def setup(nc, ctx, K):
    def sb(name, shape, dt=F32):
        return ctx.enter_context(nc.sbuf_tensor(name, shape, dt))

    sem = nc.alloc_semaphore
    K.own = []

    def phase_sem(name):
        K.own.append(nc.alloc_semaphore(name))
        return K.own[-1]

    def renew():
        nc.clear_and_free_semaphores(K.own)
        K.own = []
        nc.all_engine_barrier()

    K.sem, K.renew = phase_sem, renew

    K.nc = nc
    K.ps = ctx.enter_context(nc.psum_tensor("ps", [P, 8, 512], F32))
    K.stage = [sb(f"stage{s}", [P, 1024]) for s in range(2)]
    K.w_hi = [sb(f"w_hi{s}", [P, 1024], F32R) for s in range(2)]
    K.w_lo = [sb(f"w_lo{s}", [P, 1024], F32R) for s in range(2)]
    K.ident = sb("ident", [P, P])
    K.landed = [sem(f"w_landed{s}") for s in range(2)]
    K.hi_made = [sem(f"w_hi_made{s}") for s in range(2)]
    K.lo_made = [sem(f"w_lo_made{s}") for s in range(2)]
    K.w_used = [sem(f"w_used{s}") for s in range(2)]


def load_unit(sp, K, s, n, src, width):
    above_zero(sp, K.hi_made[s], n)
    above_zero(sp, K.lo_made[s], n)
    dst = K.stage[s][:, 0:src.shape[1] * width].rearrange("p (k c) -> p k c", c=width)
    sp.dma_start(dst, src).then_inc(K.landed[s], 16)


def split_hi(act, K, s, n, r, size, dst=None):
    act.wait_ge(K.landed[s], 16 * n + 16)
    if dst is None:
        above_zero(act, K.w_used[s], r)
        dst = K.w_hi[s][:, 0:size]
    K.nc.scalar.activation(dst, K.stage[s][:, 0:size], ACT.Copy).then_inc(K.hi_made[s], 1)


def split_lo(dve, K, s, n, size, dst=None, hi=None):
    dve.wait_ge(K.hi_made[s], n + 1)
    dst = K.w_lo[s][:, 0:size] if dst is None else dst
    hi = K.w_hi[s][:, 0:size] if hi is None else hi
    K.nc.vector.tensor_tensor(dst, K.stage[s][:, 0:size], hi.bitcast(F32), ALU.subtract).then_inc(K.lo_made[s], 1)


def mm3(nc, out, a, b, start, stop):
    nc.tensor.matmul(out, a[0], b[0], start=start, stop=False)
    nc.tensor.matmul(out, a[0], b[1], start=False, stop=False)
    return nc.tensor.matmul(out, a[1], b[0], start=False, stop=stop)


def project_half(K, bank, s, width, half, act_hi, act_lo):
    for k in range(NK):
        cols = slice(k * width, (k + 1) * width)
        toks = slice(half * HALF, (half + 1) * HALF)
        last = mm3(K.nc, K.ps[0:width, bank, :], (K.w_hi[s][:, cols], K.w_lo[s][:, cols]),
                   (act_hi[:, k, toks], act_lo[:, k, toks]), k == 0, k == NK - 1)
    return last


class NormTranspose:
    def __init__(self, K, ctx, tag, x, xn, hi, lo, gain):
        sem = lambda n: K.sem(f"{tag}_{n}")
        self.K, self.x, self.xn, self.hi, self.lo, self.gain = K, x, xn, hi, lo, gain
        self.ss, self.rstd, self.mhalf = K.ss, K.rstd, K.mhalf
        self.squared, self.rstd_made, self.mean_made = sem("squared"), sem("rstd_made"), sem("mean_made")
        self.scaled, self.turned = sem("scaled"), sem("turned")
        self.hi_out, self.lo_out = sem("hi_out"), sem("lo_out")

    def scalar_stats(self, act, t, spare=None):
        self.K.nc.scalar.activation((self.lo if spare is None else spare)[:, t, :], self.x[:, t, :], ACT.Square,
                                    accum_out=self.ss[:, t:t + 1]).then_inc(self.squared, 1)

    def scalar_out(self, act):
        for n in range(2 * NK):
            h, k = divmod(n, NK)
            act.wait_ge(self.turned, n + 1)
            dst = self.hi[:, k, h * HALF:(h + 1) * HALF]
            src = self.K.ps[:, 4 + n % 4, :]
            if self.gain is None:
                i = self.K.nc.scalar.activation(dst, src, ACT.Copy)
            else:
                i = self.K.nc.scalar.activation(dst, src, ACT.Copy, scale=self.gain[:, k:k + 1])
            i.then_inc(self.hi_out, 1)

    def pool(self, pool):
        nc = self.K.nc
        for t in range(NT):
            pool.wait_ge(self.squared, t + 1)
            c = slice(t, t + 1)
            nc.gpsimd.tensor_scalar(self.ss[:, c], self.ss[:, c], 1.0 / DM, EPS, ALU.mult, ALU.add)\
                .then_inc(self.mean_made, 1)
            pool.wait_ge(self.mean_made, t + 1)
            nc.gpsimd.tensor_tensor(self.rstd[:, c], self.ss[:, c], self.mhalf[:, 0:1], ALU.pow)\
                .then_inc(self.rstd_made, 1)

    def vector(self, dve):
        nc = self.K.nc
        for t in range(NT):
            dve.wait_ge(self.rstd_made, t + 1)
            nc.vector.tensor_scalar(self.xn[:, t, :], self.x[:, t, :], self.rstd[:, t:t + 1], None, ALU.mult)\
                .then_inc(self.scaled, 1)
        for n in range(2 * NK):
            h, k = divmod(n, NK)
            dve.wait_ge(self.hi_out, n + 1)
            toks = slice(h * HALF, (h + 1) * HALF)
            src, hi = self.K.ps[:, 4 + n % 4, :], self.hi[:, k, toks].bitcast(F32)
            if self.gain is None:
                i = nc.vector.tensor_tensor(self.lo[:, k, toks], src, hi, ALU.subtract)
            else:
                i = nc.vector.scalar_tensor_tensor(out=self.lo[:, k, toks], in0=src, scalar=self.gain[:, k:k + 1],
                                                   in1=hi, op0=ALU.mult, op1=ALU.subtract)
            i.then_inc(self.lo_out, 1)

    def tensor(self, pe):
        for n in range(2 * NK):
            h, k = divmod(n, NK)
            pe.wait_ge(self.scaled, 4 * h + 4)
            above_zero(pe, self.lo_out, n - 3)
            for t in range(4):
                last = self.K.nc.tensor.transpose(self.K.ps[:, 4 + n % 4, t * P:(t + 1) * P],
                                                  self.xn[:, 4 * h + t, k * P:(k + 1) * P], self.K.ident[:])
            last.then_inc(self.turned, 1)


def w_in_unit(W, c0, width):
    return W.rearrange("(k p) n -> p k n", p=P)[:, :, c0:c0 + width]


def phase_norm1(K, ctx, A, first_units):
    nc = K.nc
    x = ctx.enter_context(nc.sbuf_tensor("x_in", [P, NT, DM], F32))
    x_landed = [K.sem(f"x_landed{t}") for t in range(NT)]
    c_landed = K.sem("c_landed")
    one = K.sem("mhalf_set")
    N = NormTranspose(K, ctx, "n1", x, x, K.h_hi, K.h_lo, K.gains[:, 0, :])
    xv = A["x"][0].rearrange("(t p) d -> p t d", p=P)

    with nc.Block() as block:
        @block.sync
        def _(sp):
            for t in range(NT):
                sp.dma_start(x[:, t, :], xv[:, t, :]).then_inc(x_landed[t], 16)
            for s, (c0, width) in enumerate(first_units):
                load_unit(sp, K, s, 0, w_in_unit(A["w_in"][0], c0, width), width)

        @block.scalar
        def _(act):
            a, b = CONST_AT["ident"]
            act.dma_start(K.ident[:], A["consts"][:, a:b]).then_inc(c_landed, 16)
            act.dma_start(K.small[:], A["consts"][:, 0:SMALL_W]).then_inc(c_landed, 16)
            act.dma_start(K.gains[:], A["gains"]).then_inc(c_landed, 16)
            for t in range(NT):
                act.wait_ge(x_landed[t], 16)
                N.scalar_stats(act, t)
            act.wait_ge(c_landed, 48)
            N.scalar_out(act)

        @block.gpsimd
        def _(pool):
            nc.gpsimd.memset(K.mhalf[:, 0:4], -0.5).then_inc(one, 1)
            nc.gpsimd.memset(K.mhalf[:, 4:16], -1.0).then_inc(one, 1)
            pool.wait_ge(one, 2)
            N.pool(pool)

        @block.vector
        def _(dve):
            dve.wait_ge(c_landed, 48)
            N.vector(dve)

        @block.tensor
        def _(pe):
            pe.wait_ge(c_landed, 48)
            N.tensor(pe)


def kv_units():
    return [("copy", C_KC, DK, ("kc", 0)), ("copy", C_KC + DK, DK, ("kc", 1)), ("copy", C_VC, P, ("vc", 0)),
            ("turn", C_VS, P, "vs"), ("turn", C_VW, P, "vw"), ("turn", C_NGATE, P, "gate"),
            ("split", C_KS, DK, 0), ("split", C_KW, DK, 1),
            ("copy", C_KS + DK, DK, ("kraw", 0)), ("copy", C_KW + DK, DK, ("kraw", 1))]


def phase_kv(K, ctx, A, C, next_units):
    nc = K.nc
    units = kv_units()
    tmp = [ctx.enter_context(nc.sbuf_tensor(f"kv_tmp{i}", [P, SEQ], F32)) for i in range(2)]
    sem = K.sem
    half0 = [sem(f"kv_half0_{s}") for s in range(2)]
    out = [[sem(f"kv_out{s}{h}") for h in range(2)] for s in range(2)]
    k_hi = sem("kv_k_hi")
    turned, turned_out = sem("kv_turned"), sem("kv_turned_out")
    masked = sem("kv_gate_out")
    turns = [u for u, unit in enumerate(units) if unit[0] == "turn"]
    splits = [u for u, unit in enumerate(units) if unit[0] == "split"]
    half_ready = lambda e, u, h: e.wait_ge(half0[u % 2] if h == 0 else K.w_used[u % 2], u // 2 + 1)

    with nc.Block() as block:
        @block.sync
        def _(sp):
            for u in range(2, len(units)):
                load_unit(sp, K, u % 2, u // 2, w_in_unit(A["w_in"][0], units[u][1], units[u][2]), units[u][2])
            for s, (c0, width) in enumerate(next_units):
                load_unit(sp, K, s, len(units) // 2, w_in_unit(A["w_in"][0], c0, width), width)

        @block.scalar
        def _(act):
            split_hi(act, K, 0, 0, 0, NK * units[0][2])
            for u, (kind, c0, width, which) in enumerate(units):
                if u + 1 < len(units):
                    split_hi(act, K, (u + 1) % 2, (u + 1) // 2, (u + 1) // 2, NK * units[u + 1][2])
                s = u % 2
                for h in range(2):
                    half_ready(act, u, h)
                    src, toks = K.ps[0:width, 2 * s + h, :], slice(h * HALF, (h + 1) * HALF)
                    if kind == "copy":
                        dst = C.vc[:, toks] if which[0] == "vc" else source_of(C, which[0])[:, which[1], toks]
                        nc.scalar.activation(dst, src, ACT.Copy).then_inc(out[s][h], 1)
                    elif kind == "split":
                        nc.scalar.activation(C.k_hi[:, which, toks], src, ACT.Copy).then_inc(k_hi, 1)
                    else:
                        i = turns.index(u)
                        above_zero(act, turned, 2 * (i - 1))
                        nc.scalar.activation(tmp[i % 2][:, toks], src, ACT.Sigmoid if which == "gate" else ACT.Copy)\
                            .then_inc(out[s][h], 1)

        @block.vector
        def _(dve):
            def turn_out(u):
                which, i = units[u][3], turns.index(u)
                for h in range(2):
                    dve.wait_ge(turned, 2 * i + h + 1)
                    src = K.ps[:, 4 + 2 * (i % 2) + h, :].rearrange("p (t c) -> p t c", t=4)
                    if which == "gate":
                        nc.vector.tensor_copy(C.gate[:, 4 * h:4 * h + 4, :], src[:, :, 0:3 * NH]).then_inc(turned_out, 1)
                    else:
                        dst = C.vs if which == "vs" else C.vw
                        nc.vector.tensor_copy(dst[:, 4 * h:4 * h + 4, :], src).then_inc(turned_out, 1)

            split_lo(dve, K, 0, 0, NK * units[0][2])
            for u, (kind, c0, width, which) in enumerate(units):
                if u + 1 < len(units):
                    split_lo(dve, K, (u + 1) % 2, (u + 1) // 2, NK * units[u + 1][2])
                s = u % 2
                if kind == "split":
                    for h in range(2):
                        toks = slice(h * HALF, (h + 1) * HALF)
                        dve.wait_ge(k_hi, 2 * splits.index(u) + h + 1)
                        nc.vector.tensor_tensor(C.k_lo[:, which, toks], K.ps[0:width, 2 * s + h, :],
                                                C.k_hi[:, which, toks].bitcast(F32), ALU.subtract).then_inc(out[s][h], 1)
                if u - 1 in turns:
                    turn_out(u - 1)
            dve.wait_ge(turned_out, 2 * len(turns))
            first = C.gate[:, 0, 0:NH]
            nc.vector.tensor_scalar(first, first, K.const("valid"), None, ALU.mult).then_inc(masked, 1)
            dve.wait_ge(masked, 1)

        @block.tensor
        def _(pe):
            for u, (kind, c0, width, which) in enumerate(units):
                s = u % 2
                pe.wait_ge(K.lo_made[s], u // 2 + 1)
                for h in range(2):
                    above_zero(pe, out[s][h], u // 2)
                    project_half(K, 2 * s + h, s, width, h, K.h_hi, K.h_lo)\
                        .then_inc(half0[s] if h == 0 else K.w_used[s], 1)
                if u - 1 in turns:
                    i = turns.index(u - 1)
                    above_zero(pe, turned_out, 2 * (i - 1))
                    for h in range(2):
                        pe.wait_ge(out[(u - 1) % 2][h], (u - 1) // 2 + 1)
                        for t in range(4):
                            last = nc.tensor.transpose(K.ps[:, 4 + 2 * (i % 2) + h, t * P:(t + 1) * P],
                                                       tmp[i % 2][:, (4 * h + t) * P:(4 * h + t + 1) * P], K.ident[:])
                        last.then_inc(turned, 1)


def source_of(C, name):
    return {"kc": C.kc, "kraw": C.kraw}[name]


def phase_compress(K, ctx, A, C):
    nc = K.nc
    sb = lambda n, s, d=F32: ctx.enter_context(nc.sbuf_tensor(n, s, d))
    sem = K.sem
    w1k, w1v = sb("w1k", [DK, CMP_LEN, DK]), sb("w1v", [P, CMP_LEN, DV])
    w2k, w2v = sb("w2k", [DK, DK]), sb("w2v", [DV, DV])
    pek, pev = sb("pek", [DK, CMP_LEN]), sb("pev", [P, CMP_LEN])
    ksrc = [K.mix[0:DK, 2 * i:2 * i + 2, :].rearrange("p g (n l) -> p g n l", l=CMP_STRIDE) for i in range(2)]
    vsrc = [K.mix[:, 4 + i, :].rearrange("p (n l) -> p n l", l=CMP_STRIDE) for i in range(2)]
    gk, gv = sb("gelu_k", [DK, NG * NCMP]), sb("gelu_v", [DV, NG * NCMP])
    loaded, summed, hidden, active = sem("cw_loaded"), sem("cw_summed"), sem("cw_hidden"), sem("cw_active")
    mapped, zeroed, high, written = sem("cw_mapped"), sem("cw_zeroed"), sem("cw_high"), sem("cw_written")
    hid_k = K.ps[0:DK, 0, 0:NG * NCMP]
    hid_v = [K.ps[0:DV, 1, 0:NCMP], K.ps[0:DV, 4, 0:NCMP]]
    out_k, out_v = K.ps[0:DK, 2, 0:NG * NCMP], K.ps[0:NCMP, 3, 0:NG * DV]

    with nc.Block() as block:
        @block.gpsimd
        def _(pool):
            nc.gpsimd.memset(C.kc_hi[:].bitcast(F32), 0.0).then_inc(zeroed, 1)
            nc.gpsimd.memset(C.kc_lo[:].bitcast(F32), 0.0).then_inc(zeroed, 1)

        @block.sync
        def _(sp):
            sp.dma_start(w1k[:], A["cmp_w1_k"][0].rearrange("(l d) j -> d l j", d=DK)).then_inc(loaded, 16)
            for g in range(NG):
                rows = slice(g * DV, (g + 1) * DV)
                sp.dma_start(w1v[rows], A["cmp_w1_v"][0].rearrange("(l d) j -> d l j", d=DV)).then_inc(loaded, 16)
                sp.dma_start(pev[rows], A["pe_v"]).then_inc(loaded, 16)
            sp.dma_start(pek[:], A["pe_k"]).then_inc(loaded, 16)
            sp.dma_start(w2k[:], A["cmp_w2_k"][0]).then_inc(loaded, 16)
            sp.dma_start(w2v[:], A["cmp_w2_v"][0]).then_inc(loaded, 16)

        @block.vector
        def _(dve):
            dve.wait_ge(loaded, 16 * 8)
            for i in range(2):
                part = slice(i * CMP_STRIDE, (i + 1) * CMP_STRIDE)
                for g in range(NG):
                    nc.vector.tensor_tensor(ksrc[i][:, g], C.kc[:, g, :].rearrange("p (n l) -> p n l", l=CMP_STRIDE),
                                            pek[:, part].unsqueeze(1).to_broadcast([DK, NB, CMP_STRIDE]), ALU.add)\
                        .then_inc(summed, 1)
                nc.vector.tensor_tensor(vsrc[i], C.vc[:].rearrange("p (n l) -> p n l", l=CMP_STRIDE),
                                        pev[:, part].unsqueeze(1).to_broadcast([P, NB, CMP_STRIDE]), ALU.add)\
                    .then_inc(summed, 1)
            dve.wait_ge(mapped, 1)
            dve.wait_ge(high, 1)
            nc.vector.tensor_tensor(C.kc_lo[:, :, 0:NCMP], out_k.rearrange("p (g n) -> p g n", g=NG),
                                    C.kc_hi[:, :, 0:NCMP].bitcast(F32), ALU.subtract).then_inc(written, 1)
            dve.wait_ge(mapped, 2)
            nc.vector.tensor_copy(C.vcmp[0:NCMP, :, :], out_v.rearrange("p (g n) -> p g n", g=NG)).then_inc(written, 1)

        @block.tensor
        def _(pe):
            pe.wait_ge(summed, 6)
            for l in range(CMP_LEN):
                i, c = divmod(l, CMP_STRIDE)
                last = nc.tensor.matmul(hid_k.rearrange("p (g n) -> p g n", g=NG), w1k[:, l, :],
                                        ksrc[i][:, :, i:i + NCMP, c], start=(l == 0), stop=(l == CMP_LEN - 1))
            last.then_inc(hidden, 1)
            for g in range(NG):
                rows = slice(g * DV, (g + 1) * DV)
                for l in range(CMP_LEN):
                    i, c = divmod(l, CMP_STRIDE)
                    last = nc.tensor.matmul(hid_v[g], w1v[rows, l, :],
                                            vsrc[i][rows, i:i + NCMP, c], start=(l == 0), stop=(l == CMP_LEN - 1))
            last.then_inc(hidden, 1)
            pe.wait_ge(active, 1)
            nc.tensor.matmul(out_k, w2k[:], gk[:], start=True, stop=True).then_inc(mapped, 1)
            pe.wait_ge(active, 3)
            for g in range(NG):
                last = nc.tensor.matmul(out_v[:, g * DV:(g + 1) * DV], gv[:, g * NCMP:(g + 1) * NCMP], w2v[:],
                                        start=True, stop=True)
            last.then_inc(mapped, 1)

        @block.scalar
        def _(act):
            act.wait_ge(hidden, 1)
            nc.scalar.activation(gk[:], hid_k, ACT.Gelu_apprx_tanh).then_inc(active, 1)
            act.wait_ge(hidden, 2)
            for g in range(NG):
                nc.scalar.activation(gv[:, g * NCMP:(g + 1) * NCMP], hid_v[g], ACT.Gelu_apprx_tanh).then_inc(active, 1)
            act.wait_ge(mapped, 1)
            act.wait_ge(zeroed, 2)
            nc.scalar.activation(C.kc_hi[:, :, 0:NCMP], out_k.rearrange("p (g n) -> p g n", g=NG), ACT.Copy)\
                .then_inc(high, 1)


def laid_out(inputs):
    column = lambda a: np.asarray(a)[0].reshape(NK, P).T
    gains = np.stack([column(inputs[n]) for n in ("norm_mix_pre", "norm_ffn_pre", "ret_gn_g")], axis=1)
    return {"consts": shape_constants(), "gains": np.ascontiguousarray(gains),
            "pe_k": np.ascontiguousarray(np.asarray(inputs["cmp_pe_k"])[0].T),
            "pe_v": np.ascontiguousarray(np.asarray(inputs["cmp_pe_v"])[0].T)}



STEPS = [(0, i) for i in range(NT)] + [(1, i) for i in reversed(range(NT))]
NS = len(STEPS)
CMP, SEL, WIN = 0, 1, 2
E_WIN, E_CMP, E_SEL = 0, WINDOW + P, WINDOW + P + NB
E_W = E_SEL + SEQ


def key_blocks(i):
    first = max(0, i - WB)
    return ([(WIN, b, E_WIN + (b - first) * P) for b in range(first, i + 1)] + [(CMP, 0, E_CMP)]
            + [(SEL, b, E_SEL + b * P) for b in range(i + 1)])


def batches(i):
    blocks = key_blocks(i)
    return [blocks[n:n + 4] for n in range(0, len(blocks), 4)]


BEFORE = [sum(len(batches(i)) for _, i in STEPS[:s]) for s in range(NS + 1)]
PER_PAIR = BEFORE[NS]
assert PER_PAIR % 2 == 0
Q_AT = {1: (1, 0), 3: (1, 1), 12: (0, 0), 14: (0, 1)}
SPLIT_AT = {5: 0, 10: 1}
LAST_PAIR = NH // 2 - 1


def phase_attention(K, ctx, A, C, n0, next_units):
    nc = K.nc
    sb = lambda n, s, d=F32: ctx.enter_context(nc.sbuf_tensor(n, s, d))
    sem = K.sem
    dsel, dwin, dcmp = sb("d_sel", [P, SEQ]), sb("d_win", [P, WINDOW + P]), sb("d_cmp", [P, NB + (NT - 1) * 8])
    q_hi = [sb(f"q_hi{i}", [DK, SEQ], F32R) for i in range(2)]
    q_lo = [sb(f"q_lo{i}", [DK, SEQ], F32R) for i in range(2)]
    E = sb("probs", [P, 2, E_W])
    ET = sb("probs_t", [P, 2, 512])
    o_nat = sb("o_nat", [P, NT, P])
    o_part = sb("o_part", [P, 2, DV])
    least, total = sb("least", [P, 2, 3]), sb("total", [P, 2, 3])
    inv, weight = sb("inv_total", [P, 2, 3]), sb("weight", [P, 2, 3])
    slope, qscale, gate = sb("slope", [P, 2]), sb("q_scale", [P, 2]), sb("pair_gate", [P, NT, 3, 2])
    d_landed = sem("d_landed")
    q_half0, q_high, q_out = sem("q_half0"), sem("q_high"), sem("q_out")
    sB, sA = sem("win_scores"), sem("sel_scores")
    nB, nA = sem("win_biased"), sem("sel_biased")
    eB, eA = sem("win_probs"), sem("sel_probs")
    turned, pv = sem("probs_turned"), sem("values_added")
    copied = [sem("probs_copied0"), sem("probs_copied1")]
    scaled, weighted, merged = sem("inv_made"), sem("weights_made"), sem("merged")
    part = sem("o_part_made")
    o_turned, o_out = sem("o_turned"), [sem("o_out0"), sem("o_out1")]
    slope_set, pair_set, gate_set = sem("slope_set"), sem("pair_set"), sem("gate_set")
    k_moved_hi, k_moved = sem("k_moved_hi"), sem("k_moved")
    psA = K.ps[:, 0:2, :].rearrange("p b n -> p (b n)")
    psB = K.ps[:, 2:4, :].rearrange("p b n -> p (b n)")
    O = K.ps[:, 6, 0:3 * DV].rearrange("p (b e) -> p b e", b=3)
    PQ = K.ps[0:DK, 7, :]
    wv = A["w_in"][0].rearrange("(k p) n -> p k n", p=P)

    def per_pair(engine, body):
        body(0, 0)
        with engine.Fori(1, LAST_PAIR // 2 + 1) as j:
            body(j, 0)
        with engine.Fori(LAST_PAIR // 2 + 1, LAST_PAIR) as j:
            body(j, 1)
        body(LAST_PAIR, 1)

    def last(j):
        return isinstance(j, int) and j == LAST_PAIR

    with nc.Block() as block:
        @block.sync
        def _(sp):
            for name, dst in (("dsel", dsel), ("dwin", dwin), ("dcmp", dcmp)):
                a, b = CONST_AT[name]
                sp.dma_start(dst[:], A["consts"][:, a:b]).then_inc(d_landed, 16)

            def body(j, g):
                if last(j):
                    for s, (c0, width) in enumerate(next_units):
                        load_unit(sp, K, s, n0 + NH // 2, w_in_unit(A["w_in"][0], c0, width), width)
                    return
                for s in range(2):
                    c0 = j * (2 * DK) + (C_NQ + (2 + s) * DK)
                    load_unit(sp, K, s, j + (n0 + 1), wv[:, :, bass.ds(c0, DK)], DK)
            per_pair(nc.sync, body)

        @block.scalar
        def _(act):
            def q_high_part(c, s, h, n, scale):
                act.wait_ge(q_half0 if h == 0 else K.w_used[s], (c if h == 0 else n) + 1)
                nc.scalar.activation(q_hi[s][:, h * HALF:(h + 1) * HALF], PQ, ACT.Copy, scale=scale).then_inc(q_high, 1)

            def copy_out(t, j, s):
                for k, batch in enumerate(batches(STEPS[s][1])):
                    if (BEFORE[s] + k) % 2:
                        b = j * PER_PAIR + (BEFORE[s] + k)
                        act.wait_ge(turned, b + 1)
                        above_zero(act, pv, b - 1)
                        w = len(batch) * P
                        nc.scalar.activation(ET[:, 1, 0:w], K.ps[:, 5, 0:w], ACT.Copy).then_inc(copied[1], 1)

            for s in range(2):
                split_hi(act, K, s, n0, n0, NK * DK)
            for h in range(2):
                q_high_part(0, 0, h, n0, K.const("qscale")[0:DK, 0:1])

            def body(j, g):
                for s, (hh, i) in enumerate(STEPS):
                    t, slot = j * NS + s, s % 2
                    w, wide = (min(i, WB) + 1) * P, (i + 1) * P
                    act.wait_ge(nB, t + 1)
                    for br, at, size in ((WIN, E_WIN, w), (CMP, E_CMP, NB)):
                        m = nc.scalar.activation(E[:, slot, at:at + size], E[:, slot, at:at + size], ACT.Exp,
                                                 bias=least[:, slot, br:br + 1], scale=-1.0,
                                                 accum_out=total[:, slot, br:br + 1])
                    m.then_inc(eB, 1)
                    if s:
                        copy_out(t - 1, j, s - 1)
                    act.wait_ge(nA, t + 1)
                    nc.scalar.activation(E[:, slot, E_SEL:E_SEL + wide], E[:, slot, E_SEL:E_SEL + wide], ACT.Exp,
                                         bias=least[:, slot, SEL:SEL + 1], scale=-1.0,
                                         accum_out=total[:, slot, SEL:SEL + 1]).then_inc(eA, 1)
                    if s in Q_AT and not (last(j) and Q_AT[s][0] == 0):
                        qs, h = Q_AT[s]
                        act.wait_ge(pair_set, j + 1)
                        q_high_part(j * 2 + (1 if qs else 2), qs, h, j + (n0 if qs else n0 + 1), qscale[0:DK, 1 - qs:2 - qs])
                    if s in SPLIT_AT and not last(j):
                        r = SPLIT_AT[s]
                        split_hi(act, K, r, j + (n0 + 1), j + (n0 + 1), NK * DK)
                copy_out(None, j, NS - 1)
                act.wait_ge(o_turned, j * 2 + 1)
                nc.scalar.activation(K.mix[:, bass.ds(j, 1), 0:HALF].rearrange("p a n -> p (a n)"), K.ps[:, 4, :],
                                     ACT.Copy).then_inc(o_out[0], 1)

            body(0, 0)
            with nc.scalar.Fori(1, 4) as j:
                body(j, 0)
            act.wait_ge(sA, 4 * NS)
            nc.scalar.activation(C.k_hi[:], C.kraw[:], ACT.Copy).then_inc(k_moved_hi, 1)
            with nc.scalar.Fori(4, 7) as j:
                body(j, 1)
            body(LAST_PAIR, 1)

        @block.gpsimd
        def _(pool):
            def body(j, g):
                above_zero(pool, q_out, j * 4 + 2)
                n = 1 if last(j) else 2
                nc.gpsimd.tensor_copy(qscale[:, 0:n], K.const("qscale")[:, bass.ds(j * 2 + 1, n)]).then_inc(pair_set, 1)
                above_zero(pool, weighted, j * NS)
                src = C.gate[:].rearrange("p i (b h) -> p i b h", b=3)[:, :, :, bass.ds(j * 2, 2)]
                nc.gpsimd.tensor_copy(gate[:], src).then_inc(gate_set, 1)
                pool.wait_ge(gate_set, j + 1)
                for s, (hh, i) in enumerate(STEPS):
                    t, slot = j * NS + s, s % 2
                    pool.wait_ge(eA, t + 1)
                    nc.gpsimd.tensor_tensor(inv[:, slot, :], total[:, slot, :], K.mhalf[:, 4:7], ALU.pow).then_inc(scaled, 1)
                    pool.wait_ge(scaled, t + 1)
                    above_zero(pool, merged, t - 1)
                    nc.gpsimd.tensor_tensor(weight[:, slot, :], inv[:, slot, :], gate[:, i, :, hh], ALU.mult)\
                        .then_inc(weighted, 1)
            per_pair(nc.gpsimd, body)

        @block.vector
        def _(dve):
            def q_low_part(c, s, h, scale):
                dve.wait_ge(q_high, c + 1)
                toks = slice(h * HALF, (h + 1) * HALF)
                nc.vector.scalar_tensor_tensor(out=q_lo[s][:, toks], in0=PQ, scalar=scale, in1=q_hi[s][:, toks].bitcast(F32),
                                               op0=ALU.mult, op1=ALU.subtract).then_inc(q_out, 1)

            def copy_out(j, s):
                for k, batch in enumerate(batches(STEPS[s][1])):
                    if (BEFORE[s] + k) % 2 == 0:
                        b = j * PER_PAIR + (BEFORE[s] + k)
                        dve.wait_ge(turned, b + 1)
                        above_zero(dve, pv, b - 1)
                        w = len(batch) * P
                        nc.vector.tensor_copy(ET[:, 0, 0:w], K.ps[:, 4, 0:w]).then_inc(copied[0], 1)

            def merge(j, s):
                hh, i = STEPS[s]
                t, slot = j * NS + s, s % 2
                dve.wait_ge(pv, j * PER_PAIR + BEFORE[s + 1])
                dve.wait_ge(weighted, t + 1)
                w = [weight[:, slot, br:br + 1] for br in range(3)]
                nc.vector.tensor_scalar(o_part[:, 0, :], O[:, 0, :], w[0], None, ALU.mult).then_inc(part, 1)
                dve.wait_ge(part, t * 2 + 1)
                nc.vector.scalar_tensor_tensor(out=o_part[:, 1, :], in0=O[:, 1, :], scalar=w[1], in1=o_part[:, 0, :],
                                               op0=ALU.mult, op1=ALU.add).then_inc(part, 1)
                dve.wait_ge(part, t * 2 + 2)
                nc.vector.scalar_tensor_tensor(out=o_nat[:, i, hh * DV:(hh + 1) * DV], in0=O[:, 2, :], scalar=w[2],
                                               in1=o_part[:, 1, :], op0=ALU.mult, op1=ALU.add).then_inc(merged, 1)

            for s in range(2):
                split_lo(dve, K, s, n0, NK * DK)
            nc.vector.tensor_copy(slope[:], K.const("slope")[:, 0:2]).then_inc(slope_set, 1)
            for h in range(2):
                q_low_part(h, 0, h, K.const("qscale")[0:DK, 0:1])
            dve.wait_ge(d_landed, 48)

            def body(j, g):
                dve.wait_ge(slope_set, j + 1)
                for s, (hh, i) in enumerate(STEPS):
                    t, slot = j * NS + s, s % 2
                    w, wide = (min(i, WB) + 1) * P, (i + 1) * P
                    dve.wait_ge(sB, t + 1)
                    above_zero(dve, turned, j * PER_PAIR + (BEFORE[s - 1] if s else BEFORE[NS - 1] - PER_PAIR))
                    nc.vector.nop(nofuse=True)
                    for br, at, size, src, d in ((WIN, E_WIN, w, 0, dwin[:, WINDOW + P - w:]),
                                                 (CMP, E_CMP, NB, WINDOW + P, dcmp[:, (NT - 1 - i) * 8:(NT - 1 - i) * 8 + NB])):
                        m = nc.vector.tensor_tensor_reduce(E[:, slot, at:at + size], psB[:, src:src + size], d,
                                                           slope[:, hh:hh + 1], 3e38, ALU.add, ALU.min,
                                                           least[:, slot, br:br + 1])
                    m.then_inc(nB, 1)
                    dve.wait_ge(sA, t + 1)
                    nc.vector.nop(nofuse=True)
                    nc.vector.tensor_tensor_reduce(E[:, slot, E_SEL:E_SEL + wide], psA[:, 0:wide], dsel[:, SEQ - wide:],
                                                   slope[:, hh:hh + 1], 3e38, ALU.add, ALU.min,
                                                   least[:, slot, SEL:SEL + 1]).then_inc(nA, 1)
                    if s:
                        copy_out(j, s - 1)
                    if s in Q_AT and not (last(j) and Q_AT[s][0] == 0):
                        qs, h = Q_AT[s]
                        q_low_part(j * 4 + (2 + list(Q_AT).index(s)), qs, h, qscale[0:DK, 1 - qs:2 - qs])
                    if s in SPLIT_AT and not last(j):
                        split_lo(dve, K, SPLIT_AT[s], j + (n0 + 1), NK * DK)
                    if s:
                        merge(j, s - 1)
                copy_out(j, NS - 1)
                merge(j, NS - 1)
                dve.wait_ge(nA, j * NS + NS)
                nc.vector.tensor_scalar(slope[:], slope[:], 0.5, None, ALU.mult).then_inc(slope_set, 1)
                dve.wait_ge(o_turned, j * 2 + 2)
                nc.vector.tensor_scalar(K.mix[:, bass.ds(j, 1), HALF:SEQ].rearrange("p a n -> p (a n)"), K.ps[:, 5, :],
                                        1.0, None, ALU.mult).then_inc(o_out[1], 1)

            body(0, 0)
            with nc.vector.Fori(1, 4) as j:
                body(j, 0)
            dve.wait_ge(k_moved_hi, 1)
            nc.vector.tensor_tensor(C.k_lo[:], C.kraw[:], C.k_hi[:].bitcast(F32), ALU.subtract).then_inc(k_moved, 1)
            with nc.vector.Fori(4, 7) as j:
                body(j, 1)
            body(LAST_PAIR, 1)

        @block.tensor
        def _(pe):
            def q_half(c, s, h, n):
                pe.wait_ge(K.lo_made[s], n + 1)
                above_zero(pe, q_out, c)
                project_half(K, 7, s, DK, h, K.h_hi, K.h_lo).then_inc(q_half0 if h == 0 else K.w_used[s], 1)

            def scores(j, s, g):
                hh, i = STEPS[s]
                t = j * NS + s
                w, wide = (min(i, WB) + 1) * P, (i + 1) * P
                mine = (q_hi[hh][:, i * P:(i + 1) * P], q_lo[hh][:, i * P:(i + 1) * P])
                above_zero(pe, nB, t)
                for a in range(0, w, 512):
                    b = min(w, a + 512)
                    keys = slice((i + 1) * P - w + a, (i + 1) * P - w + b)
                    mm3(nc, psB[:, a:b], mine, (C.k_hi[:, 1, keys], C.k_lo[:, 1, keys]), True, True)
                mm3(nc, psB[:, WINDOW + P:WINDOW + P + NB], mine, (C.kc_hi[:, g, :], C.kc_lo[:, g, :]), True, True)\
                    .then_inc(sB, 1)
                above_zero(pe, nA, t)
                for a in range(0, wide, 512):
                    b = min(wide, a + 512)
                    m = mm3(nc, psA[:, a:b], mine, (C.k_hi[:, 0, a:b], C.k_lo[:, 0, a:b]), True, True)
                m.then_inc(sA, 1)

            def turn(j, s, k, blocks, fresh):
                n = BEFORE[s] + k
                t = j * NS + s
                if k == 0:
                    pe.wait_ge(eB, t + 1)
                if fresh:
                    pe.wait_ge(eA, t + 1)
                above_zero(pe, copied[n % 2], j * (PER_PAIR // 2) + n // 2)
                if n < 2:
                    above_zero(pe, o_out[n % 2], j)
                nc.tensor.nop(nofuse=True)
                for c, (br, b, at) in enumerate(blocks):
                    rows = NB if br == CMP else P
                    m = nc.tensor.transpose(K.ps[0:rows, 4 + n % 2, c * P:(c + 1) * P],
                                            E[:, s % 2, at:at + rows], K.ident[:])
                m.then_inc(turned, 1)

            def values(j, s, k, blocks, g):
                n = BEFORE[s] + k
                hh, i = STEPS[s]
                pe.wait_ge(copied[n % 2], j * (PER_PAIR // 2) + (n // 2 + 1))
                if k == 0:
                    above_zero(pe, merged, j * NS + s)
                for c, (br, b, at) in enumerate(blocks):
                    first = b == (max(0, i - WB) if br == WIN else 0)
                    rows = NCMP if br == CMP else P
                    v = C.vcmp[0:NCMP, g, :] if br == CMP else (C.vs if br == SEL else C.vw)[:, b, g * DV:(g + 1) * DV]
                    m = nc.tensor.matmul(O[:, br, :], ET[0:rows, n % 2, c * P:(c + 1) * P], v, start=first,
                                         stop=(br == CMP or b == i))
                m.then_inc(pv, 1)

            def outputs(j, s, g):
                parts = batches(STEPS[s][1])
                seen = [any(x[0] == SEL for x in part) for part in parts]
                for k in range(len(parts) + 1):
                    if k < len(parts):
                        turn(j, s, k, parts[k], seen[k] and not any(seen[:k]))
                    if k:
                        values(j, s, k - 1, parts[k - 1], g)

            for h in range(2):
                q_half(h, 0, h, n0)

            def body(j, g):
                for s in range(NS):
                    if s == 0:
                        pe.wait_ge(q_out, j * 4 + 2)
                    if s == NT:
                        pe.wait_ge(q_out, j * 4 + 4)
                    scores(j, s, g)
                    if s in Q_AT and not (last(j) and Q_AT[s][0] == 0):
                        qs, h = Q_AT[s]
                        q_half(j * 4 + (2 + list(Q_AT).index(s)), qs, h, j + (n0 if qs else n0 + 1))
                    if s:
                        outputs(j, s - 1, g)
                outputs(j, NS - 1, g)
                pe.wait_ge(merged, j * NS + NS)
                for half in range(2):
                    pe.wait_ge(copied[half], (j + 1) * (PER_PAIR // 2))
                    for i in range(4):
                        m = nc.tensor.transpose(K.ps[:, 4 + half, i * P:(i + 1) * P], o_nat[:, 4 * half + i, :], K.ident[:])
                    m.then_inc(o_turned, 1)

            body(0, 0)
            with nc.tensor.Fori(1, 4) as j:
                body(j, 0)
            pe.wait_ge(k_moved, 1)
            with nc.tensor.Fori(4, 7) as j:
                body(j, 1)
            body(LAST_PAIR, 1)



def half_stream(K, ctx, tag):
    sem = lambda n: K.sem(f"{tag}_{n}")
    half0 = [sem(f"half0_{s}") for s in range(2)]
    out = [[sem(f"out{s}{h}") for h in range(2)] for s in range(2)]
    return half0, out


def phase_gate_nsa(K, ctx, A, n0, next_units):
    nc = K.nc
    half0, out = half_stream(K, ctx, "gb")
    sig = [[ctx.enter_context(nc.sbuf_tensor(f"gb_sig{s}{h}", [P, HALF], F32)) for h in range(2)] for s in range(2)]
    gated = [[K.sem(f"gb_gated{s}{h}") for h in range(2)] for s in range(2)]
    wv = A["w_in"][0].rearrange("(k p) n -> p k n", p=P)
    pairs = NK // 2

    def per_pair(engine, body):
        body(0)
        with engine.Fori(1, pairs) as r:
            body(r)

    with nc.Block() as block:
        @block.sync
        def _(sp):
            with nc.sync.Fori(0, pairs - 1) as r:
                for s in range(2):
                    load_unit(sp, K, s, r + (n0 + 1), wv[:, :, bass.ds(r * (2 * P) + (C_MB + (2 + s) * P), P)], P)
            for s, (c0, width) in enumerate(next_units):
                load_unit(sp, K, s, n0 + pairs, w_in_unit(A["w_in"][0], c0, width), width)

        @block.scalar
        def _(act):
            split_hi(act, K, 0, n0, n0, 1024)

            def body(r):
                for s in range(2):
                    split_hi(act, K, 1 - s, r + (n0 + s), r + (n0 + s), 1024)
                    for h in range(2):
                        act.wait_ge(half0[s] if h == 0 else K.w_used[s], r + (1 if h == 0 else n0 + 1))
                        above_zero(act, gated[s][h], r)
                        nc.scalar.activation(sig[s][h][:], K.ps[:, 2 * s + h, :], ACT.Sigmoid).then_inc(out[s][h], 1)
            per_pair(nc.scalar, body)

        @block.vector
        def _(dve):
            split_lo(dve, K, 0, n0, 1024)

            def body(r):
                for s in range(2):
                    split_lo(dve, K, 1 - s, r + (n0 + s), 1024)
                    for h in range(2):
                        dve.wait_ge(out[s][h], r + 1)
                        m = K.mix[:, bass.ds(r * 2 + s, 1), h * HALF:(h + 1) * HALF].rearrange("p a n -> p (a n)")
                        nc.vector.tensor_tensor(m, m, sig[s][h][:], ALU.mult).then_inc(gated[s][h], 1)
            per_pair(nc.vector, body)

        @block.tensor
        def _(pe):
            def body(r):
                for s in range(2):
                    pe.wait_ge(K.lo_made[s], r + (n0 + 1))
                    for h in range(2):
                        above_zero(pe, out[s][h], r)
                        project_half(K, 2 * s + h, s, P, h, K.h_hi, K.h_lo)\
                            .then_inc(half0[s] if h == 0 else K.w_used[s], 1)
            per_pair(nc.tensor, body)


HH = RH // 2
RP = HH // 2


def ret_units(half):
    return ([("q", C_RQ + (half * RP + i) * P, i) for i in range(RP)] + [("k", C_RK + (half * RP + i) * P, i) for i in range(RP)]
            + [("v", C_RV + (half * HH + i) * P, i) for i in range(HH)])


def phase_ret_project(K, ctx, A, R, half, n0, next_units):
    nc = K.nc
    units = ret_units(half)
    half0, out = half_stream(K, ctx, f"rp{half}")
    sem = lambda n: K.sem(f"rp{half}_{n}")
    tmp = [ctx.enter_context(nc.sbuf_tensor(f"ret{half}_tmp{i}", [P, SEQ], F32)) for i in range(2)]
    turned, turned_out = sem("turned"), sem("turned_out")
    turns = [u for u, unit in enumerate(units) if unit[0] in "kv"]

    def turn_source(u):
        kind, _, i = units[u]
        return R.k[:, i, :] if kind == "k" else tmp[i % 2][:]

    with nc.Block() as block:
        @block.sync
        def _(sp):
            for u in range(2, len(units)):
                load_unit(sp, K, u % 2, n0 + u // 2, w_in_unit(A["w_in"][0], units[u][1], P), P)
            for s, (c0, width) in enumerate(next_units):
                load_unit(sp, K, s, n0 + len(units) // 2, w_in_unit(A["w_in"][0], c0, width), width)

        @block.scalar
        def _(act):
            for u, (kind, c0, i) in enumerate(units):
                s, n = u % 2, n0 + (u + 1) // 2
                split_hi(act, K, (u + 1) % 2, n, n, 1024)
                for h in range(2):
                    act.wait_ge(half0[s] if h == 0 else K.w_used[s], u // 2 + 1 + (0 if h == 0 else n0))
                    toks = slice(h * HALF, (h + 1) * HALF)
                    if kind == "v":
                        above_zero(act, turned, 2 * (turns.index(u) - 1) if i >= 2 else 0)
                        dst = tmp[i % 2][:, toks]
                    else:
                        dst = (R.q if kind == "q" else R.k)[:, i, toks]
                    nc.scalar.activation(dst, K.ps[:, 2 * s + h, :], ACT.Copy).then_inc(out[s][h], 1)

        @block.vector
        def _(dve):
            def turn_out(u):
                kind, _, i = units[u]
                t = turns.index(u)
                for h in range(2):
                    dve.wait_ge(turned, 2 * t + h + 1)
                    src = K.ps[:, 4 + 2 * (t % 2) + h, :].rearrange("p (t c) -> p t c", t=4)
                    if kind == "v":
                        nc.vector.tensor_copy(R.v[:, 4 * h:4 * h + 4, i, :], src).then_inc(turned_out, 1)
                    else:
                        for a in range(2):
                            head = half * HH + 2 * i + a
                            nc.vector.tensor_scalar(R.kz[:, 4 * h:4 * h + 4, i, a * RDK:(a + 1) * RDK],
                                                    src[:, :, a * RDK:(a + 1) * RDK],
                                                    K.const("zeta")[:, head:head + 1], None, ALU.mult).then_inc(turned_out, 1)

            for u in range(len(units)):
                n = n0 + (u + 1) // 2
                split_lo(dve, K, (u + 1) % 2, n, 1024)
                if u - 1 in turns:
                    turn_out(u - 1)
            turn_out(len(units) - 1)

        @block.tensor
        def _(pe):
            counts = [0]
            for u in turns:
                counts.append(counts[-1] + (4 if units[u][0] == "k" else 2))

            def turn(u):
                t = turns.index(u)
                above_zero(pe, turned_out, counts[max(0, t - 1)])
                for h in range(2):
                    pe.wait_ge(out[u % 2][h], u // 2 + 1)
                    for i in range(4):
                        last = nc.tensor.transpose(K.ps[:, 4 + 2 * (t % 2) + h, i * P:(i + 1) * P],
                                                   turn_source(u)[:, (4 * h + i) * P:(4 * h + i + 1) * P], K.ident[:])
                    last.then_inc(turned, 1)

            for u in range(len(units)):
                s = u % 2
                pe.wait_ge(K.lo_made[s], n0 + u // 2 + 1)
                for h in range(2):
                    above_zero(pe, out[s][h], u // 2)
                    project_half(K, 2 * s + h, s, P, h, K.h_hi, K.h_lo).then_inc(half0[s] if h == 0 else K.w_used[s], 1)
                if u - 1 in turns:
                    turn(u - 1)
            turn(len(units) - 1)


def phase_ret_chunks(K, ctx, A, R, half):
    nc = K.nc
    sb = lambda n, s: ctx.enter_context(nc.sbuf_tensor(f"rc{half}_{n}", s, F32))
    sem = lambda n: K.sem(f"rc{half}_{n}")
    dmat = sb("dmat", [P, HH, P])
    inner = sb("inner", [P, 2, HH, P])
    state = sb("state", [P, RP, RDV])
    o, y = sb("o", [P, 2, HH, P]), sb("y", [P, 2, HH, P])
    stats, mv, rstd = sb("stats", [P, 2, HH, 6]), sb("mv", [P, 2, HH, 2]), sb("rstd", [P, 2, HH])
    d_landed, scores, decayed, summed, updated = sem("d_landed"), sem("scores"), sem("decayed"), sem("summed"), sem("updated")
    state_set, scaled, stat, agg = sem("state_set"), sem("scaled"), sem("stat"), sem("agg")
    var_eps, inv_std, normed, turned, turned_out = sem("var_eps"), sem("inv_std"), sem("normed"), sem("turned"), sem("turned_out")
    heads = [(a, a // 2, (a % 2) * RDK) for a in range(HH)]
    score_bank = lambda n, a: K.ps[:, 2 * (n % 2) + a % 2, (a // 2) * P:(a // 2 + 1) * P]
    o_bank = lambda a: K.ps[:, 4 + a % 2, (a // 2) * P:(a // 2 + 1) * P]
    gain = K.gains[:, 2, :]

    with nc.Block() as block:
        @block.sync
        def _(sp):
            a, b = CONST_AT["dmat"]
            w = (b - a) // 2
            sp.dma_start(dmat[:], A["consts"][:, a + half * w:a + (half + 1) * w].rearrange("p (h n) -> p h n", n=P))\
                .then_inc(d_landed, 16)

        @block.tensor
        def _(pe):
            def score(n):
                above_zero(pe, decayed, 2 * (n - 1))
                toks = slice(n * P, (n + 1) * P)
                for a, pair, row in sorted(heads, key=lambda x: x[2]):
                    rows = slice(row, row + RDK)
                    m = nc.tensor.matmul(score_bank(n, a), R.k[rows, pair, toks], R.q[rows, pair, toks], start=True, stop=True)
                m.then_inc(scores, 1)

            def turn(n):
                pe.wait_ge(normed, HH * (n + 1))
                above_zero(pe, turned_out, HH * n)
                for a in range(HH):
                    m = nc.tensor.transpose(K.ps[:, 7, a * P:(a + 1) * P], y[:, n % 2, a, :], K.ident[:])
                m.then_inc(turned, 1)

            score(0)
            for n in range(NT):
                toks = slice(n * P, (n + 1) * P)
                if n + 1 < NT:
                    score(n + 1)
                pe.wait_ge(decayed, 2 * (n + 1))
                above_zero(pe, scaled, 2 * n)
                if n:
                    pe.wait_ge(state_set, RP * n)
                for a, pair, row in sorted(heads, key=lambda x: x[2]):
                    rows = slice(row, row + RDK)
                    m = nc.tensor.matmul(o_bank(a), inner[:, n % 2, a, :], R.v[:, n, a, :], start=True, stop=(n == 0))
                    if n:
                        m = nc.tensor.matmul(o_bank(a), R.q[rows, pair, toks], state[rows, pair, :], start=False, stop=True)
                m.then_inc(summed, 1)
                if n + 1 < NT:
                    for a, pair, row in heads:
                        m = nc.tensor.matmul(K.ps[row:row + RDK, 6, pair * RDV:(pair + 1) * RDV],
                                             R.kz[:, n, pair, row:row + RDK], R.v[:, n, a, :], start=True, stop=True)
                    m.then_inc(updated, 1)
                if n:
                    turn(n - 1)
            turn(NT - 1)

        @block.vector
        def _(dve):
            def norm(n):
                for a in range(HH):
                    dve.wait_ge(scaled, 2 * (n + 1))
                    nc.vector.bn_stats(stats[:, n % 2, a, :], o[:, n % 2, a, :]).then_inc(stat, 1)
                for a in range(HH):
                    dve.wait_ge(stat, HH * n + a + 1)
                    nc.vector.bn_aggr(mv[:, n % 2, a, :], stats[:, n % 2, a, :]).then_inc(agg, 1)

            def normalise(n):
                dve.wait_ge(inv_std, n + 1)
                above_zero(dve, turned, n - 1)
                for a in range(HH):
                    nc.vector.tensor_scalar(y[:, n % 2, a, :], o[:, n % 2, a, :], mv[:, n % 2, a, 0:1],
                                            rstd[:, n % 2, a:a + 1], ALU.subtract, ALU.mult).then_inc(normed, 1)

            dve.wait_ge(d_landed, 16)
            for n in range(NT):
                dve.wait_ge(scores, n + 1)
                for odd in range(2):
                    nc.vector.tensor_tensor(inner[:, n % 2, odd::2, :],
                                            K.ps[:, 2 * (n % 2) + odd, 0:RP * P].rearrange("p (a c) -> p a c", c=P),
                                            dmat[:, odd::2, :], ALU.mult).then_inc(decayed, 1)
                dve.wait_ge(summed, n + 1)
                for odd in range(2):
                    xi = K.const("xi")[:, half * HH + odd:(half + 1) * HH:2].unsqueeze(2).to_broadcast([P, RP, P])
                    nc.vector.tensor_tensor(o[:, n % 2, odd::2, :],
                                            K.ps[:, 4 + odd, 0:RP * P].rearrange("p (a c) -> p a c", c=P), xi, ALU.mult)\
                        .then_inc(scaled, 1)
                if n + 1 < NT:
                    dve.wait_ge(updated, n + 1)
                    for pair in range(RP):
                        src = K.ps[:, 6, pair * RDV:(pair + 1) * RDV]
                        if n == 0:
                            nc.vector.tensor_copy(state[:, pair, :], src).then_inc(state_set, 1)
                        else:
                            c = half * RP + pair
                            nc.vector.scalar_tensor_tensor(out=state[:, pair, :], in0=state[:, pair, :],
                                                           scalar=K.const("decay")[:, c:c + 1], in1=src,
                                                           op0=ALU.mult, op1=ALU.add).then_inc(state_set, 1)
                norm(n)
                if n:
                    normalise(n - 1)
            normalise(NT - 1)

        @block.gpsimd
        def _(pool):
            for n in range(NT):
                pool.wait_ge(agg, HH * (n + 1))
                above_zero(pool, normed, HH * (n - 1))
                nc.gpsimd.tensor_scalar(rstd[:, n % 2, :], mv[:, n % 2, :, 1], GN_EPS, None, ALU.add).then_inc(var_eps, 1)
                pool.wait_ge(var_eps, n + 1)
                nc.gpsimd.tensor_tensor(rstd[:, n % 2, :], rstd[:, n % 2, :], K.mhalf[:, 0:HH], ALU.pow).then_inc(inv_std, 1)

        @block.scalar
        def _(act):
            for n in range(NT):
                act.wait_ge(turned, n + 1)
                for a in range(HH):
                    head = half * HH + a
                    nc.scalar.activation(R.out[:, a, n * P:(n + 1) * P], K.ps[:, 7, a * P:(a + 1) * P], ACT.Copy,
                                         scale=gain[:, head:head + 1]).then_inc(turned_out, 1)


def phase_gate_ret(K, ctx, A, R, half, n0, next_units):
    nc = K.nc
    half0, out = half_stream(K, ctx, f"gr{half}")
    sb = lambda n: [ctx.enter_context(nc.sbuf_tensor(f"gr{half}_{n}{h}", [P, HALF], F32)) for h in range(2)]
    sem = lambda n: [K.sem(f"gr{half}_{n}{h}") for h in range(2)]
    silu, sig = sb("silu"), sb("sig")
    silu_sig, sig_made, added = sem("silu_sig"), sem("sig_made"), sem("added")
    by_ret, by_sig = sem("by_ret"), sem("by_sig")
    wv = A["w_in"][0].rearrange("(k p) n -> p k n", p=P)
    first = [C_RG + half * HH * P, C_MA + half * HH * P]

    def per_head(engine, body):
        body(0)
        with engine.Fori(1, HH) as r:
            body(r)

    with nc.Block() as block:
        @block.sync
        def _(sp):
            with nc.sync.Fori(0, HH - 1) as r:
                for s in range(2):
                    load_unit(sp, K, s, r + (n0 + 1), wv[:, :, bass.ds(r * P + (first[s] + P), P)], P)
            for s, (src, width) in enumerate(next_units):
                load_unit(sp, K, s, n0 + HH, src, width)

        @block.scalar
        def _(act):
            def body(r):
                for s in range(2):
                    split_hi(act, K, 1 - s, r + (n0 + s), r + (n0 + s), 1024)
                    for h in range(2):
                        act.wait_ge(half0[s] if h == 0 else K.w_used[s], r + (1 if h == 0 else n0 + 1))
                        above_zero(act, added[h], r)
                        if s == 0:
                            nc.scalar.activation(silu[h][:], K.ps[:, h, :], ACT.Sigmoid).then_inc(silu_sig[h], 1)
                        else:
                            nc.scalar.activation(sig[h][:], K.ps[:, 2 + h, :], ACT.Sigmoid).then_inc(out[1][h], 1)
            per_head(nc.scalar, body)

        @block.vector
        def _(dve):
            def body(r):
                for s in range(2):
                    split_lo(dve, K, 1 - s, r + (n0 + s), 1024)
                    for h in range(2):
                        toks = slice(h * HALF, (h + 1) * HALF)
                        if s == 0:
                            dve.wait_ge(silu_sig[h], r + 1)
                            nc.vector.tensor_tensor(silu[h][:], K.ps[:, h, :], silu[h][:], ALU.mult).then_inc(out[0][h], 1)
                            dve.wait_ge(out[0][h], r + 1)
                            ret = R.out[:, bass.ds(r, 1), toks].rearrange("p a n -> p (a n)")
                            nc.vector.tensor_tensor(silu[h][:], silu[h][:], ret, ALU.mult).then_inc(by_ret[h], 1)
                        else:
                            dve.wait_ge(by_ret[h], r + 1)
                            dve.wait_ge(out[1][h], r + 1)
                            nc.vector.tensor_tensor(sig[h][:], sig[h][:], silu[h][:], ALU.mult).then_inc(by_sig[h], 1)
                            dve.wait_ge(by_sig[h], r + 1)
                            m = K.mix[:, bass.ds(r + half * HH, 1), toks].rearrange("p a n -> p (a n)")
                            nc.vector.tensor_tensor(m, m, sig[h][:], ALU.add).then_inc(added[h], 1)
            per_head(nc.vector, body)

        @block.tensor
        def _(pe):
            def body(r):
                for s in range(2):
                    pe.wait_ge(K.lo_made[s], r + (n0 + 1))
                    for h in range(2):
                        above_zero(pe, out[s][h], r)
                        project_half(K, 2 * s + h, s, P, h, K.h_hi, K.h_lo)\
                            .then_inc(half0[s] if h == 0 else K.w_used[s], 1)
            per_head(nc.tensor, body)



def wide_unit(W, m, ch):
    return W.rearrange("(k p) n -> p k n", p=P)[:, 2 * m:2 * m + 2, ch * HALF:(ch + 1) * HALF]


MIX_UNITS = [(ch, m) for ch in range(2) for m in range(NK // 2)]


def phase_mix_out(K, ctx, A, y, n0, next_units):
    nc = K.nc
    m_hi = ctx.enter_context(nc.sbuf_tensor("m_hi", [P, NK, SEQ], F32R))
    m_lo = ctx.enter_context(nc.sbuf_tensor("m_lo", [P, NK, SEQ], F32R))
    sem = K.sem
    m_high, m_made, done, out = sem("m_high"), sem("m_made"), sem("mo_done"), sem("mo_out")

    with nc.Block() as block:
        @block.sync
        def _(sp):
            for u in range(2, len(MIX_UNITS)):
                ch, m = MIX_UNITS[u]
                load_unit(sp, K, u % 2, n0 + u // 2, wide_unit(A["w_out"][0], m, ch), HALF)
            for s, (src, width) in enumerate(next_units):
                load_unit(sp, K, s, n0 + len(MIX_UNITS) // 2, src, width)

        @block.scalar
        def _(act):
            for u in range(len(MIX_UNITS)):
                if u < 4:
                    for k in (2 * u, 2 * u + 1):
                        nc.scalar.activation(m_hi[:, k, :], K.mix[:, k, :], ACT.Copy).then_inc(m_high, 1)
                n = n0 + (u + 1) // 2
                split_hi(act, K, (u + 1) % 2, n, n, 1024)

        @block.vector
        def _(dve):
            for u, (ch, m) in enumerate(MIX_UNITS):
                if u < 4:
                    for k in (2 * u, 2 * u + 1):
                        dve.wait_ge(m_high, k + 1)
                        nc.vector.tensor_tensor(m_lo[:, k, :], K.mix[:, k, :], m_hi[:, k, :].bitcast(F32), ALU.subtract)\
                            .then_inc(m_made, 1)
                split_lo(dve, K, (u + 1) % 2, n0 + (u + 1) // 2, 1024)
                if m == NK // 2 - 1:
                    for t in range(NT):
                        if t < NT - 1:
                            dve.wait_ge(done, ch * (NT - 1) + t + 1)
                        else:
                            dve.wait_ge(K.w_used[u % 2], n0 + u // 2 + 1)
                        nc.vector.tensor_copy(y[:, t, ch * HALF:(ch + 1) * HALF], K.ps[:, t, :]).then_inc(out, 1)

        @block.tensor
        def _(pe):
            for u, (ch, m) in enumerate(MIX_UNITS):
                s = u % 2
                pe.wait_ge(K.lo_made[s], n0 + u // 2 + 1)
                if ch == 0:
                    pe.wait_ge(m_made, 2 * m + 2)
                for t in range(NT):
                    toks = slice(t * P, (t + 1) * P)
                    if m == 0 and ch:
                        pe.wait_ge(out, t + 1)
                    for kk in range(2):
                        k, cols = 2 * m + kk, slice(kk * HALF, (kk + 1) * HALF)
                        last = mm3(nc, K.ps[:, t, :], (m_hi[:, k, toks], m_lo[:, k, toks]),
                                   (K.w_hi[s][:, cols], K.w_lo[s][:, cols]), k == 0, k == NK - 1)
                    if t == NT - 1:
                        last.then_inc(K.w_used[s], 1)
                    elif m == NK // 2 - 1:
                        last.then_inc(done, 1)


def phase_residual(K, ctx, A, tag, y, x, gain_row, hi, lo, gain, x_dram):
    nc = K.nc
    sem = lambda n: K.sem(f"{tag}_{n}")
    row = ctx.enter_context(nc.sbuf_tensor(f"{tag}_gain", [P, DM], F32))
    ss, rstd = (ctx.enter_context(nc.sbuf_tensor(f"{tag}_{n}", [P, NT], F32)) for n in ("ss", "rstd"))
    row_landed = sem("row_landed")
    x_landed = [sem(f"x_landed{t}") for t in range(NT)] if x_dram is not None else None
    squared, mean_made, rstd_made, scaled, added = sem("squared"), sem("mean_made"), sem("rstd_made"), sem("scaled"), sem("added")
    N = NormTranspose(K, ctx, f"{tag}n", x, y, hi, lo, gain)

    with nc.Block() as block:
        @block.sync
        def _(sp):
            sp.dma_start(row[:], gain_row.partition_broadcast(P)).then_inc(row_landed, 16)
            if x_dram is not None:
                for t in range(NT):
                    sp.dma_start(x[:, t, :], x_dram[:, t, :]).then_inc(x_landed[t], 16)

        @block.scalar
        def _(act):
            for t in range(NT + 2):
                if t < NT:
                    nc.scalar.activation(lo[:, t, :], y[:, t, :], ACT.Square, accum_out=ss[:, t:t + 1]).then_inc(squared, 1)
                if t >= 2:
                    act.wait_ge(added, t - 1)
                    N.scalar_stats(act, t - 2, hi)
            N.scalar_out(act)

        @block.gpsimd
        def _(pool):
            for t in range(NT):
                c = slice(t, t + 1)
                pool.wait_ge(squared, t + 1)
                nc.gpsimd.tensor_scalar(ss[:, c], ss[:, c], 1.0 / DM, EPS, ALU.mult, ALU.add).then_inc(mean_made, 1)
                pool.wait_ge(mean_made, t + 1)
                nc.gpsimd.tensor_tensor(rstd[:, c], ss[:, c], K.mhalf[:, 0:1], ALU.pow).then_inc(rstd_made, 1)
            N.pool(pool)

        @block.vector
        def _(dve):
            dve.wait_ge(row_landed, 16)
            for t in range(NT):
                dve.wait_ge(rstd_made, t + 1)
                nc.vector.scalar_tensor_tensor(out=y[:, t, :], in0=y[:, t, :], scalar=rstd[:, t:t + 1], in1=row[:],
                                               op0=ALU.mult, op1=ALU.mult).then_inc(scaled, 1)
                dve.wait_ge(scaled, t + 1)
                if x_dram is not None:
                    dve.wait_ge(x_landed[t], 16)
                nc.vector.tensor_tensor(x[:, t, :], x[:, t, :], y[:, t, :], ALU.add).then_inc(added, 1)
            N.vector(dve)

        @block.tensor
        def _(pe):
            N.tensor(pe)


FPI = 2
FIT = NF // FPI


def ffn_units(A, c):
    win = A["w_ffn_in"][0].rearrange("(k p) n -> p k n", p=P)
    units = []
    for b in range(FPI):
        for part in range(2):
            units.append((win[:, :, bass.ds(c * (FPI * P) + (b * P + part * DFF), P)], P))
    for b in range(FPI):
        units.append((A["w_ffn_out"][0][bass.ds(c * (FPI * P) + b * P, P), :].unsqueeze(1), DM))
    return units


def phase_ffn(K, ctx, A, h_hi, h_lo, total, n0, next_units):
    nc = K.nc
    a_hi = ctx.enter_context(nc.sbuf_tensor("a_hi", [P, FPI, SEQ], F32R))
    a_lo = ctx.enter_context(nc.sbuf_tensor("a_lo", [P, FPI, SEQ], F32R))
    gate = [ctx.enter_context(nc.sbuf_tensor(f"ffn_gate{h}", [P, HALF], F32)) for h in range(2)]
    sem = K.sem
    half0 = [sem(f"ffn_half0_{s}") for s in range(2)]
    sig = [sem(f"ffn_sig{h}") for h in range(2)]
    u_out = [sem(f"ffn_u_out{h}") for h in range(2)]
    v_out = [sem(f"ffn_v_out{h}") for h in range(2)]
    high = [sem(f"ffn_high{h}") for h in range(2)]
    made = [sem(f"ffn_made{h}") for h in range(2)]
    done, out = sem("ffn_done"), sem("ffn_out")
    NU = 3 * FPI
    PER = NU // 2
    NO = 2 * NT

    def per_iteration(engine, body):
        body(0)
        with engine.Fori(1, FIT) as c:
            body(c)

    def half_ready(e, s, c, b, h):
        e.wait_ge(half0[s] if h == 0 else K.w_used[s], c * 2 + (b + 1) if h == 0 else c * PER + (n0 + b + 1))

    with nc.Block() as block:
        @block.sync
        def _(sp):
            def body(c, skip=0):
                for u, (src, width) in enumerate(ffn_units(A, c)):
                    if u >= skip:
                        load_unit(sp, K, u % 2, c * PER + (n0 + u // 2), src, width)
            body(0, skip=2)
            with nc.sync.Fori(1, FIT) as c:
                body(c)
            for s, (src, width) in enumerate(next_units):
                load_unit(sp, K, s, n0 + FIT * PER, src, width)

        @block.scalar
        def _(act):
            def body(c):
                for u in range(NU):
                    s, b = u % 2, u // 2
                    n = c * PER + (n0 + (u + 1) // 2)
                    split_hi(act, K, 1 - s, n, n, 1024)
                    if b == FPI:
                        continue
                    for h in range(2):
                        toks = slice(h * HALF, (h + 1) * HALF)
                        if s == 0:
                            half_ready(act, 0, c, b, h)
                            above_zero(act, made[h], c * 2 + b)
                            nc.scalar.activation(gate[h][:], K.ps[:, h, :], ACT.Sigmoid).then_inc(sig[h], 1)
                        else:
                            act.wait_ge(v_out[h], c * 2 + (b + 1))
                            nc.scalar.activation(a_hi[:, b, toks], gate[h][:], ACT.Copy).then_inc(high[h], 1)
            per_iteration(nc.scalar, body)

        @block.vector
        def _(dve):
            def body(c):
                for u in range(NU):
                    s, b = u % 2, u // 2
                    n = c * PER + (n0 + (u + 1) // 2)
                    if u < NU - 1:
                        split_lo(dve, K, 1 - s, n, 1024)
                    if b == FPI:
                        continue
                    for h in range(2):
                        toks = slice(h * HALF, (h + 1) * HALF)
                        if s == 0:
                            dve.wait_ge(sig[h], c * 2 + (b + 1))
                            nc.vector.tensor_tensor(gate[h][:], K.ps[:, h, :], gate[h][:], ALU.mult).then_inc(u_out[h], 1)
                        else:
                            half_ready(dve, 1, c, b, h)
                            dve.wait_ge(u_out[h], c * 2 + (b + 1))
                            nc.vector.tensor_tensor(gate[h][:], K.ps[:, 2 + h, :], gate[h][:], ALU.mult).then_inc(v_out[h], 1)
                            dve.wait_ge(high[h], c * 2 + (b + 1))
                            nc.vector.tensor_tensor(a_lo[:, b, toks], gate[h][:], a_hi[:, b, toks].bitcast(F32),
                                                    ALU.subtract).then_inc(made[h], 1)
                for o in range(NO):
                    t, ch = divmod(o, 2)
                    if o < NO - 1:
                        dve.wait_ge(done, c * (NO - 1) + (o + 1))
                    else:
                        dve.wait_ge(K.w_used[1], c * PER + (n0 + PER))
                    dst, src = total[:, t, ch * HALF:(ch + 1) * HALF], K.ps[:, 4 + o % 4, :]
                    if isinstance(c, int) and c == 0:
                        nc.vector.tensor_copy(dst, src).then_inc(out, 1)
                    else:
                        nc.vector.tensor_tensor(dst, src, dst, ALU.add).then_inc(out, 1)
                split_lo(dve, K, 0, c * PER + (n0 + PER), 1024)
            per_iteration(nc.vector, body)

        @block.tensor
        def _(pe):
            def body(c):
                for u in range(2 * FPI):
                    s, b = u % 2, u // 2
                    pe.wait_ge(K.lo_made[s], c * PER + (n0 + b + 1))
                    for h in range(2):
                        above_zero(pe, (u_out if s == 0 else v_out)[h], c * 2 + b)
                        project_half(K, 2 * s + h, s, P, h, h_hi, h_lo).then_inc(half0[s] if h == 0 else K.w_used[s], 1)
                for s in range(2):
                    pe.wait_ge(K.lo_made[s], c * PER + (n0 + PER))
                for o in range(NO):
                    t, ch = divmod(o, 2)
                    toks, cols = slice(t * P, (t + 1) * P), slice(ch * HALF, (ch + 1) * HALF)
                    if o % NT == 0:
                        pe.wait_ge(made[o // NT], c * 2 + 2)
                    above_zero(pe, out, c * NO + (o - 3))
                    for b in range(FPI):
                        m = mm3(nc, K.ps[:, 4 + o % 4, :], (a_hi[:, b, toks], a_lo[:, b, toks]),
                                (K.w_hi[b][:, cols], K.w_lo[b][:, cols]), b == 0, b == FPI - 1)
                        if o == NO - 1:
                            m.then_inc(K.w_used[b], 1)
                    if o < NO - 1:
                        m.then_inc(done, 1)
            per_iteration(nc.tensor, body)


PLE_UNITS = [(ch, m) for ch in range(2) for m in range(NK // 2 + 1)]


def ple_unit(A, u):
    ch, m = PLE_UNITS[u]
    return (wide_unit(A["w_ple_gate"][0], m, ch) if m < NK // 2 else wide_unit(A["w_ple"][0], 0, ch)), HALF


def phase_ple(K, ctx, A, x, x_hi, x_lo, spare, n0):
    nc = K.nc
    sem = K.sem
    p_in = spare[:, 0:2, :].rearrange("p a (t c) -> p (a t) c", c=PLE)
    p_hi = ctx.enter_context(nc.sbuf_tensor("p_hi", [P, PLE // P, SEQ], F32R))
    p_lo = ctx.enter_context(nc.sbuf_tensor("p_lo", [P, PLE // P, SEQ], F32R))
    sig = ctx.enter_context(nc.sbuf_tensor("ple_sig", [P, NT, HALF], F32))
    p_landed, p_turned, p_high, p_made = sem("p_landed"), sem("p_turned"), sem("p_high"), sem("p_made")
    gated, embedded = sem("ple_gated"), sem("ple_embedded")
    sig_made, scaled, added, stored = sem("ple_sig_made"), sem("ple_scaled"), sem("ple_added"), sem("ple_stored")
    ov = A["out"][0].rearrange("(t p) d -> p t d", p=P)
    G = NK // 2

    with nc.Block() as block:
        @block.sync
        def _(sp):
            sp.dma_start(p_in, A["p"][0, 0].rearrange("(t p) c -> p t c", p=P)).then_inc(p_landed, 16)
            for u in range(2, len(PLE_UNITS)):
                src, width = ple_unit(A, u)
                load_unit(sp, K, u % 2, n0 + u // 2, src, width)
            for n in range(2 * NT):
                ch, t = divmod(n, NT)
                sp.wait_ge(added, n + 1)
                cols = slice(ch * HALF, (ch + 1) * HALF)
                sp.dma_start(ov[:, t, cols], x[:, t, cols]).then_inc(stored, 16)
            sp.wait_ge(stored, 16 * 2 * NT)

        @block.scalar
        def _(act):
            for n in range(4):
                k, h = divmod(n, 2)
                act.wait_ge(p_turned, n + 1)
                nc.scalar.activation(p_hi[:, k, h * HALF:(h + 1) * HALF], K.ps[:, 4 + n, :], ACT.Copy).then_inc(p_high, 1)
            for u, (ch, m) in enumerate(PLE_UNITS):
                if u + 1 < len(PLE_UNITS):
                    n = n0 + (u + 1) // 2
                    split_hi(act, K, (u + 1) % 2, n, n, 1024)
                if m == G - 1:
                    for t in range(NT):
                        if t < NT - 1:
                            act.wait_ge(gated, ch * (NT - 1) + t + 1)
                        else:
                            act.wait_ge(K.w_used[u % 2], n0 + u // 2 + 1)
                        above_zero(act, scaled, (ch - 1) * NT + t + 1)
                        nc.scalar.activation(sig[:, t, :], K.ps[:, t, :], ACT.Sigmoid).then_inc(sig_made, 1)

        @block.vector
        def _(dve):
            for n in range(4):
                k, h = divmod(n, 2)
                dve.wait_ge(p_high, n + 1)
                toks = slice(h * HALF, (h + 1) * HALF)
                nc.vector.tensor_tensor(p_lo[:, k, toks], K.ps[:, 4 + n, :], p_hi[:, k, toks].bitcast(F32), ALU.subtract)\
                    .then_inc(p_made, 1)
            for u, (ch, m) in enumerate(PLE_UNITS):
                if u + 1 < len(PLE_UNITS):
                    split_lo(dve, K, (u + 1) % 2, n0 + (u + 1) // 2, 1024)
                if m == G:
                    for t in range(NT):
                        n = ch * NT + t
                        if t < NT - 1:
                            dve.wait_ge(embedded, ch * (NT - 1) + t + 1)
                        else:
                            dve.wait_ge(K.w_used[u % 2], n0 + u // 2 + 1)
                        dve.wait_ge(sig_made, n + 1)
                        cols = slice(ch * HALF, (ch + 1) * HALF)
                        nc.vector.tensor_tensor(sig[:, t, :], K.ps[:, t, :], sig[:, t, :], ALU.mult).then_inc(scaled, 1)
                        dve.wait_ge(scaled, n + 1)
                        nc.vector.tensor_tensor(x[:, t, cols], x[:, t, cols], sig[:, t, :], ALU.add).then_inc(added, 1)

        @block.tensor
        def _(pe):
            pe.wait_ge(p_landed, 16)
            for n in range(4):
                k, h = divmod(n, 2)
                for t in range(4):
                    last = nc.tensor.transpose(K.ps[:, 4 + n, t * P:(t + 1) * P], p_in[:, 4 * h + t, k * P:(k + 1) * P],
                                               K.ident[:])
                last.then_inc(p_turned, 1)
            for u, (ch, m) in enumerate(PLE_UNITS):
                s = u % 2
                pe.wait_ge(K.lo_made[s], n0 + u // 2 + 1)
                if u == 0 or m == G:
                    pe.wait_ge(p_made, 4)
                a_hi, a_lo = (x_hi, x_lo) if m < G else (p_hi, p_lo)
                for t in range(NT):
                    if m == G:
                        pe.wait_ge(sig_made, ch * NT + t + 1)
                    if m == 0 and ch:
                        pe.wait_ge(scaled, t + 1)
                    toks = slice(t * P, (t + 1) * P)
                    for kk in range(2):
                        k = 2 * m + kk if m < G else kk
                        cols = slice(kk * HALF, (kk + 1) * HALF)
                        last = mm3(nc, K.ps[:, t, :], (a_hi[:, k, toks], a_lo[:, k, toks]),
                                   (K.w_hi[s][:, cols], K.w_lo[s][:, cols]), k == 0, (k == NK - 1) or (m == G and kk == 1))
                    if t == NT - 1:
                        last.then_inc(K.w_used[s], 1)
                    elif m == G - 1:
                        last.then_inc(gated, 1)
                    elif m == G:
                        last.then_inc(embedded, 1)



def layer(nc, A):
    with ExitStack() as ctx:
        K, C = Core(), Core()
        setup(nc, ctx, K)
        small = lambda n, s: ctx.enter_context(nc.sbuf_tensor(n, s, F32))
        K.gains = small("gains", [P, 3, NK])
        K.small = small("consts", [P, SMALL_W])
        K.ss, K.rstd, K.mhalf = small("ss", [P, NT]), small("rstd", [P, NT]), small("mhalf", [P, 16])
        K.mix = ctx.enter_context(nc.sbuf_tensor("mix", [P, NK, SEQ], F32))
        with ExitStack() as proj:
            K.h_hi = proj.enter_context(nc.sbuf_tensor("h_hi", [P, NK, SEQ], F32R))
            K.h_lo = proj.enter_context(nc.sbuf_tensor("h_lo", [P, NK, SEQ], F32R))
            with ExitStack() as c:
                phase_norm1(K, c, A, [(u[1], u[2]) for u in kv_units()[:2]])
            with ExitStack() as attention:
                sb = lambda n, s, d=F32: attention.enter_context(nc.sbuf_tensor(n, s, d))
                C.k_hi, C.k_lo = sb("k_hi", [DK, 2, SEQ], F32R), sb("k_lo", [DK, 2, SEQ], F32R)
                C.kraw = sb("k_next", [DK, 2, SEQ])
                C.vs, C.vw = sb("v_sel", [P, NT, P]), sb("v_win", [P, NT, P])
                C.gate = sb("branch_gate", [P, NT, 3 * NH])
                C.kc_hi, C.kc_lo = sb("kc_hi", [DK, NG, NB], F32R), sb("kc_lo", [DK, NG, NB], F32R)
                C.vcmp = sb("v_cmp", [DV, NG, DV])
                with ExitStack() as c:
                    C.kc = c.enter_context(nc.sbuf_tensor("kc", [DK, NG, SEQ], F32))
                    C.vc = c.enter_context(nc.sbuf_tensor("vc", [P, SEQ], F32))
                    with ExitStack() as c2:
                        phase_kv(K, c2, A, C, [(C_NQ, DK), (C_NQ + DK, DK)])
                    with ExitStack() as c2:
                        phase_compress(K, c2, A, C)
                with ExitStack() as c:
                    phase_attention(K, c, A, C, len(kv_units()) // 2, [(C_MB, P), (C_MB + P, P)])
            n = len(kv_units()) // 2 + NH // 2
            K.renew()
            with ExitStack() as c:
                phase_gate_nsa(K, c, A, n, [(u[1], P) for u in ret_units(0)[:2]])
            n += NK // 2
            with ExitStack() as retention:
                R = Core()
                sb = lambda n, s: retention.enter_context(nc.sbuf_tensor(n, s, F32))
                R.q, R.k = sb("ret_q", [P, RP, SEQ]), sb("ret_k", [P, RP, SEQ])
                R.kz, R.v = sb("ret_kz", [P, NT, RP, P]), sb("ret_v", [P, NT, HH, P])
                R.out = sb("ret_out", [P, HH, SEQ])
                for half in range(2):
                    with ExitStack() as c:
                        phase_ret_project(K, c, A, R, half, n, [(C_RG + half * HH * P, P), (C_MA + half * HH * P, P)])
                    n += len(ret_units(half)) // 2
                    with ExitStack() as c:
                        phase_ret_chunks(K, c, A, R, half)
                    with ExitStack() as c:
                        if half == 0:
                            after = [(w_in_unit(A["w_in"][0], u[1], P), P) for u in ret_units(1)[:2]]
                        else:
                            after = [(wide_unit(A["w_out"][0], m, ch), HALF) for ch, m in MIX_UNITS[:2]]
                        phase_gate_ret(K, c, A, R, half, n, after)
                    n += HH
                K.renew()

        tail = ctx.enter_context(ExitStack())
        y = tail.enter_context(nc.sbuf_tensor("y", [P, NT, DM], F32))
        with ExitStack() as c:
            phase_mix_out(K, c, A, y, n, ffn_units(A, 0)[:2])
        n += len(MIX_UNITS) // 2
        x = K.mix
        h_hi = tail.enter_context(nc.sbuf_tensor("h2_hi", [P, NK, SEQ], F32R))
        h_lo = tail.enter_context(nc.sbuf_tensor("h2_lo", [P, NK, SEQ], F32R))
        xv = A["x"][0].rearrange("(t p) d -> p t d", p=P)
        with ExitStack() as c:
            phase_residual(K, c, A, "r1", y, x, A["norm_mix_post"][0], h_hi, h_lo, K.gains[:, 1, :], xv)
        K.renew()
        with ExitStack() as c:
            phase_ffn(K, c, A, h_hi, h_lo, y, n, [ple_unit(A, 0), ple_unit(A, 1)])
        n += FIT * 3 * FPI // 2
        with ExitStack() as c:
            phase_residual(K, c, A, "r2", y, x, A["norm_ffn_post"][0], h_hi, h_lo, None, None)
        with ExitStack() as c:
            phase_ple(K, c, A, x, h_hi, h_lo, y, n)

_INS = ["x", "p", "norm_mix_pre", "norm_mix_post", "norm_ffn_pre", "norm_ffn_post", "w_in", "ret_gn_g",
        "cmp_pe_k", "cmp_w1_k", "cmp_w2_k", "cmp_pe_v", "cmp_w1_v", "cmp_w2_v",
        "w_out", "w_ffn_in", "w_ffn_out", "w_ple", "w_ple_gate"]


def kernel(**inputs):
    import concourse.bacc as _bacc
    from concourse.bass_utils import run_bass_kernel_spmd as _run

    nc = _bacc.Bacc("TRN2", target_bir_lowering=False, num_devices=1)
    given = {name: np.ascontiguousarray(inputs[name]) for name in _INS}
    given.update(laid_out(inputs))
    arrays, A = {}, {}
    for name, a in given.items():
        arrays[f"in_{name}"] = a
        A[name] = nc.dram_tensor(f"in_{name}", a.shape, mybir.dt.from_np(a.dtype), kind="ExternalInput").ap()
    A["out"] = nc.dram_tensor("out", (1, SEQ, DM), F32, kind="ExternalOutput").ap()
    layer(nc, A)
    return _run(nc, [arrays], core_ids=[0]).results[0]["out"]
```

```python
from contextlib import ExitStack

import numpy as np
import concourse.bass as bass
from concourse import mybir

F32 = mybir.dt.float32
F32R = mybir.dt.float32r
ALU = mybir.AluOpType
ACT = mybir.ActivationFunctionType

P = 128
SEQ, DM = 1024, 1024
NT, NK = SEQ // P, DM // P
HALF = 512
EPS, GN_EPS = 1e-6, 1e-5
RH, RDK, RDV = 8, 64, 128
NH, NG, DK, DV = 16, 2, 96, 64
HPG = NH // NG
CMP_LEN, CMP_STRIDE = 32, 16
NCMP = (SEQ - CMP_LEN) // CMP_STRIDE + 1
NB = SEQ // CMP_STRIDE
WINDOW = 512
WB = WINDOW // P
DFF = 2816
NF = DFF // P
PLE = 256
BIG = 1e30

C_RQ = 0
C_RK = C_RQ + RH * RDK
C_RV = C_RK + RH * RDK
C_RG = C_RV + RH * RDV
C_NQ = C_RG + RH * RDV
C_KC = C_NQ + NH * DK
C_VC = C_KC + NG * DK
C_KS = C_VC + NG * DV
C_VS = C_KS + NG * DK
C_KW = C_VS + NG * DV
C_VW = C_KW + NG * DK
C_NGATE = C_VW + NG * DV
C_MA = C_NGATE + 3 * NH
C_MB = C_MA + DM

_PARTS = [("slope", NH), ("qscale", NH), ("valid", 1), ("xi", RH), ("zeta", RH), ("decay", RH // 2),
          ("ident", P), ("dsel", SEQ), ("dwin", WINDOW + P), ("dcmp", NB + (NT - 1) * 8), ("dmat", RH * P)]
CONST_AT, _n = {}, 0
for _name, _w in _PARTS:
    CONST_AT[_name] = (_n, _n + _w)
    _n += _w
CONST_W = _n
SMALL_W = CONST_AT["ident"][0]


def shape_constants():
    c = np.zeros((P, CONST_W), np.float64)

    def put(name, value):
        a, b = CONST_AT[name]
        c[:, a:b] = value

    q = np.arange(P)[:, None]
    put("ident", np.eye(P))
    d = q + (SEQ - P) - np.arange(SEQ)[None, :]
    put("dsel", np.where(d >= 0, d, BIG))
    d = q + WINDOW - np.arange(WINDOW + P)[None, :]
    put("dwin", np.where((d >= 0) & (d < WINDOW), d, BIG))
    v = np.arange(NB + (NT - 1) * 8)[None, :] - (NT - 1) * 8
    d = q - CMP_STRIDE * v - (CMP_LEN - 1)
    put("dcmp", np.where(d >= 0, d, BIG))
    slope = 2.0 ** (-8.0 * (np.arange(NH) + 1.0) / NH)
    put("slope", slope[None, :])
    put("qscale", -(DK ** -0.5) / slope[None, :])
    put("valid", q >= CMP_LEN - 1)
    log_g = np.log1p(-(2.0 ** (-5.0 - np.arange(RH))))
    s, t = np.arange(P)[:, None, None], np.arange(P)[None, None, :]
    dmat = np.where(t >= s, np.exp(-log_g[None, :, None] * (s + 1.0)) * RDK ** -0.5, 0.0)
    put("dmat", np.broadcast_to(dmat, (P, RH, P)).reshape(P, RH * P))
    put("xi", np.exp(log_g[None, :] * (q + 1.0)))
    put("zeta", np.exp(log_g[None, :] * (P - 1.0 - q)) * RDK ** -0.5)
    decay = np.exp(log_g * P)
    put("decay", np.where(q < RDK, decay[None, 0::2], decay[None, 1::2]))
    return c.astype(np.float32)


def above_zero(engine, sem, value):
    if not (isinstance(value, int) and value <= 0):
        engine.wait_ge(sem, value)


class Core:

    def const(self, name):
        a, b = CONST_AT[name]
        return self.small[:, a:b]


def setup(nc, ctx, K):
    def sb(name, shape, dt=F32):
        return ctx.enter_context(nc.sbuf_tensor(name, shape, dt))

    sem = nc.alloc_semaphore
    K.own = []

    def phase_sem(name):
        K.own.append(nc.alloc_semaphore(name))
        return K.own[-1]

    def renew():
        nc.clear_and_free_semaphores(K.own)
        K.own = []
        nc.all_engine_barrier()

    K.sem, K.renew = phase_sem, renew

    K.nc = nc
    K.ps = ctx.enter_context(nc.psum_tensor("ps", [P, 8, 512], F32))
    K.stage = [sb(f"stage{s}", [P, 1024]) for s in range(2)]
    K.w_hi = [sb(f"w_hi{s}", [P, 1024], F32R) for s in range(2)]
    K.w_lo = [sb(f"w_lo{s}", [P, 1024], F32R) for s in range(2)]
    K.ident = sb("ident", [P, P])
    K.landed = [sem(f"w_landed{s}") for s in range(2)]
    K.hi_made = [sem(f"w_hi_made{s}") for s in range(2)]
    K.lo_made = [sem(f"w_lo_made{s}") for s in range(2)]
    K.w_used = [sem(f"w_used{s}") for s in range(2)]


def load_unit(sp, K, s, n, src, width):
    above_zero(sp, K.hi_made[s], n)
    above_zero(sp, K.lo_made[s], n)
    dst = K.stage[s][:, 0:src.shape[1] * width].rearrange("p (k c) -> p k c", c=width)
    sp.dma_start(dst, src).then_inc(K.landed[s], 16)


def split_hi(act, K, s, n, r, size, dst=None):
    act.wait_ge(K.landed[s], 16 * n + 16)
    if dst is None:
        above_zero(act, K.w_used[s], r)
        dst = K.w_hi[s][:, 0:size]
    K.nc.scalar.activation(dst, K.stage[s][:, 0:size], ACT.Copy).then_inc(K.hi_made[s], 1)


def split_lo(dve, K, s, n, size, dst=None, hi=None):
    dve.wait_ge(K.hi_made[s], n + 1)
    dst = K.w_lo[s][:, 0:size] if dst is None else dst
    hi = K.w_hi[s][:, 0:size] if hi is None else hi
    K.nc.vector.tensor_tensor(dst, K.stage[s][:, 0:size], hi.bitcast(F32), ALU.subtract).then_inc(K.lo_made[s], 1)


def mm3(nc, out, a, b, start, stop):
    nc.tensor.matmul(out, a[0], b[0], start=start, stop=False)
    nc.tensor.matmul(out, a[0], b[1], start=False, stop=False)
    return nc.tensor.matmul(out, a[1], b[0], start=False, stop=stop)


def project_half(K, bank, s, width, half, act_hi, act_lo):
    for k in range(NK):
        cols = slice(k * width, (k + 1) * width)
        toks = slice(half * HALF, (half + 1) * HALF)
        last = mm3(K.nc, K.ps[0:width, bank, :], (K.w_hi[s][:, cols], K.w_lo[s][:, cols]),
                   (act_hi[:, k, toks], act_lo[:, k, toks]), k == 0, k == NK - 1)
    return last


class NormTranspose:
    def __init__(self, K, ctx, tag, x, xn, hi, lo, gain):
        sem = lambda n: K.sem(f"{tag}_{n}")
        self.K, self.x, self.xn, self.hi, self.lo, self.gain = K, x, xn, hi, lo, gain
        self.ss, self.rstd, self.mhalf = K.ss, K.rstd, K.mhalf
        self.squared, self.rstd_made, self.mean_made = sem("squared"), sem("rstd_made"), sem("mean_made")
        self.scaled, self.turned = sem("scaled"), sem("turned")
        self.hi_out, self.lo_out = sem("hi_out"), sem("lo_out")

    def scalar_stats(self, act, t, spare=None):
        self.K.nc.scalar.activation((self.lo if spare is None else spare)[:, t, :], self.x[:, t, :], ACT.Square,
                                    accum_out=self.ss[:, t:t + 1]).then_inc(self.squared, 1)

    def scalar_out(self, act):
        for n in range(2 * NK):
            h, k = divmod(n, NK)
            act.wait_ge(self.turned, n + 1)
            dst = self.hi[:, k, h * HALF:(h + 1) * HALF]
            src = self.K.ps[:, 4 + n % 4, :]
            if self.gain is None:
                i = self.K.nc.scalar.activation(dst, src, ACT.Copy)
            else:
                i = self.K.nc.scalar.activation(dst, src, ACT.Copy, scale=self.gain[:, k:k + 1])
            i.then_inc(self.hi_out, 1)

    def pool(self, pool):
        nc = self.K.nc
        for t in range(NT):
            pool.wait_ge(self.squared, t + 1)
            c = slice(t, t + 1)
            nc.gpsimd.tensor_scalar(self.ss[:, c], self.ss[:, c], 1.0 / DM, EPS, ALU.mult, ALU.add)\
                .then_inc(self.mean_made, 1)
            pool.wait_ge(self.mean_made, t + 1)
            nc.gpsimd.tensor_tensor(self.rstd[:, c], self.ss[:, c], self.mhalf[:, 0:1], ALU.pow)\
                .then_inc(self.rstd_made, 1)

    def vector(self, dve):
        nc = self.K.nc
        for t in range(NT):
            dve.wait_ge(self.rstd_made, t + 1)
            nc.vector.tensor_scalar(self.xn[:, t, :], self.x[:, t, :], self.rstd[:, t:t + 1], None, ALU.mult)\
                .then_inc(self.scaled, 1)
        for n in range(2 * NK):
            h, k = divmod(n, NK)
            dve.wait_ge(self.hi_out, n + 1)
            toks = slice(h * HALF, (h + 1) * HALF)
            src, hi = self.K.ps[:, 4 + n % 4, :], self.hi[:, k, toks].bitcast(F32)
            if self.gain is None:
                i = nc.vector.tensor_tensor(self.lo[:, k, toks], src, hi, ALU.subtract)
            else:
                i = nc.vector.scalar_tensor_tensor(out=self.lo[:, k, toks], in0=src, scalar=self.gain[:, k:k + 1],
                                                   in1=hi, op0=ALU.mult, op1=ALU.subtract)
            i.then_inc(self.lo_out, 1)

    def tensor(self, pe):
        for n in range(2 * NK):
            h, k = divmod(n, NK)
            pe.wait_ge(self.scaled, 4 * h + 4)
            above_zero(pe, self.lo_out, n - 3)
            for t in range(4):
                last = self.K.nc.tensor.transpose(self.K.ps[:, 4 + n % 4, t * P:(t + 1) * P],
                                                  self.xn[:, 4 * h + t, k * P:(k + 1) * P], self.K.ident[:])
            last.then_inc(self.turned, 1)


def w_in_unit(W, c0, width):
    return W.rearrange("(k p) n -> p k n", p=P)[:, :, c0:c0 + width]


def phase_norm1(K, ctx, A, first_units):
    nc = K.nc
    x = ctx.enter_context(nc.sbuf_tensor("x_in", [P, NT, DM], F32))
    x_landed = [K.sem(f"x_landed{t}") for t in range(NT)]
    c_landed = K.sem("c_landed")
    one = K.sem("mhalf_set")
    N = NormTranspose(K, ctx, "n1", x, x, K.h_hi, K.h_lo, K.gains[:, 0, :])
    xv = A["x"][0].rearrange("(t p) d -> p t d", p=P)

    with nc.Block() as block:
        @block.sync
        def _(sp):
            for t in range(NT):
                sp.dma_start(x[:, t, :], xv[:, t, :]).then_inc(x_landed[t], 16)
            for s, (c0, width) in enumerate(first_units):
                load_unit(sp, K, s, 0, w_in_unit(A["w_in"][0], c0, width), width)

        @block.scalar
        def _(act):
            a, b = CONST_AT["ident"]
            act.dma_start(K.ident[:], A["consts"][:, a:b]).then_inc(c_landed, 16)
            act.dma_start(K.small[:], A["consts"][:, 0:SMALL_W]).then_inc(c_landed, 16)
            act.dma_start(K.gains[:], A["gains"]).then_inc(c_landed, 16)
            for t in range(NT):
                act.wait_ge(x_landed[t], 16)
                N.scalar_stats(act, t)
            act.wait_ge(c_landed, 48)
            N.scalar_out(act)

        @block.gpsimd
        def _(pool):
            nc.gpsimd.memset(K.mhalf[:, 0:4], -0.5).then_inc(one, 1)
            nc.gpsimd.memset(K.mhalf[:, 4:16], -1.0).then_inc(one, 1)
            pool.wait_ge(one, 2)
            N.pool(pool)

        @block.vector
        def _(dve):
            dve.wait_ge(c_landed, 48)
            N.vector(dve)

        @block.tensor
        def _(pe):
            pe.wait_ge(c_landed, 48)
            N.tensor(pe)


def kv_units():
    return [("copy", C_KC, DK, ("kc", 0)), ("copy", C_KC + DK, DK, ("kc", 1)), ("copy", C_VC, P, ("vc", 0)),
            ("turn", C_VS, P, "vs"), ("turn", C_VW, P, "vw"), ("turn", C_NGATE, P, "gate"),
            ("split", C_KS, DK, 0), ("split", C_KW, DK, 1),
            ("copy", C_KS + DK, DK, ("kraw", 0)), ("copy", C_KW + DK, DK, ("kraw", 1))]


def phase_kv(K, ctx, A, C, next_units):
    nc = K.nc
    units = kv_units()
    tmp = [ctx.enter_context(nc.sbuf_tensor(f"kv_tmp{i}", [P, SEQ], F32)) for i in range(2)]
    sem = K.sem
    half0 = [sem(f"kv_half0_{s}") for s in range(2)]
    out = [[sem(f"kv_out{s}{h}") for h in range(2)] for s in range(2)]
    k_hi = sem("kv_k_hi")
    turned, turned_out = sem("kv_turned"), sem("kv_turned_out")
    masked = sem("kv_gate_out")
    turns = [u for u, unit in enumerate(units) if unit[0] == "turn"]
    splits = [u for u, unit in enumerate(units) if unit[0] == "split"]
    half_ready = lambda e, u, h: e.wait_ge(half0[u % 2] if h == 0 else K.w_used[u % 2], u // 2 + 1)
    cmp_loaded = sem("cmp_weights_loaded")
    w1k, w1v, w2k, w2v, pek, pev = C.cmp_weights

    with nc.Block() as block:
        @block.gpsimd
        def _(pool):
            pool.dma_start(w1k[:], A["cmp_w1_k"][0].rearrange("(l d) j -> d l j", d=DK)).then_inc(cmp_loaded, 16)
            for g in range(NG):
                rows = slice(g * DV, (g + 1) * DV)
                pool.dma_start(w1v[rows], A["cmp_w1_v"][0].rearrange("(l d) j -> d l j", d=DV)).then_inc(cmp_loaded, 16)
                pool.dma_start(pev[rows], A["pe_v"]).then_inc(cmp_loaded, 16)
            pool.dma_start(pek[:], A["pe_k"]).then_inc(cmp_loaded, 16)
            pool.dma_start(w2k[:], A["cmp_w2_k"][0]).then_inc(cmp_loaded, 16)
            pool.dma_start(w2v[:], A["cmp_w2_v"][0]).then_inc(cmp_loaded, 16)
            pool.wait_ge(cmp_loaded, 16 * 8)

        @block.sync
        def _(sp):
            for u in range(2, len(units)):
                load_unit(sp, K, u % 2, u // 2, w_in_unit(A["w_in"][0], units[u][1], units[u][2]), units[u][2])
            for s, (c0, width) in enumerate(next_units):
                load_unit(sp, K, s, len(units) // 2, w_in_unit(A["w_in"][0], c0, width), width)

        @block.scalar
        def _(act):
            split_hi(act, K, 0, 0, 0, NK * units[0][2])
            for u, (kind, c0, width, which) in enumerate(units):
                if u + 1 < len(units):
                    split_hi(act, K, (u + 1) % 2, (u + 1) // 2, (u + 1) // 2, NK * units[u + 1][2])
                s = u % 2
                for h in range(2):
                    half_ready(act, u, h)
                    src, toks = K.ps[0:width, 2 * s + h, :], slice(h * HALF, (h + 1) * HALF)
                    if kind == "copy":
                        dst = C.vc[:, toks] if which[0] == "vc" else source_of(C, which[0])[:, which[1], toks]
                        nc.scalar.activation(dst, src, ACT.Copy).then_inc(out[s][h], 1)
                    elif kind == "split":
                        nc.scalar.activation(C.k_hi[:, which, toks], src, ACT.Copy).then_inc(k_hi, 1)
                    else:
                        i = turns.index(u)
                        above_zero(act, turned, 2 * (i - 1))
                        nc.scalar.activation(tmp[i % 2][:, toks], src, ACT.Sigmoid if which == "gate" else ACT.Copy)\
                            .then_inc(out[s][h], 1)

        @block.vector
        def _(dve):
            def turn_out(u):
                which, i = units[u][3], turns.index(u)
                for h in range(2):
                    dve.wait_ge(turned, 2 * i + h + 1)
                    src = K.ps[:, 4 + 2 * (i % 2) + h, :].rearrange("p (t c) -> p t c", t=4)
                    if which == "gate":
                        nc.vector.tensor_copy(C.gate[:, 4 * h:4 * h + 4, :], src[:, :, 0:3 * NH]).then_inc(turned_out, 1)
                    else:
                        dst = C.vs if which == "vs" else C.vw
                        nc.vector.tensor_copy(dst[:, 4 * h:4 * h + 4, :], src).then_inc(turned_out, 1)

            split_lo(dve, K, 0, 0, NK * units[0][2])
            for u, (kind, c0, width, which) in enumerate(units):
                if u + 1 < len(units):
                    split_lo(dve, K, (u + 1) % 2, (u + 1) // 2, NK * units[u + 1][2])
                s = u % 2
                if kind == "split":
                    for h in range(2):
                        toks = slice(h * HALF, (h + 1) * HALF)
                        dve.wait_ge(k_hi, 2 * splits.index(u) + h + 1)
                        nc.vector.tensor_tensor(C.k_lo[:, which, toks], K.ps[0:width, 2 * s + h, :],
                                                C.k_hi[:, which, toks].bitcast(F32), ALU.subtract).then_inc(out[s][h], 1)
                if u - 1 in turns:
                    turn_out(u - 1)
            dve.wait_ge(turned_out, 2 * len(turns))
            first = C.gate[:, 0, 0:NH]
            nc.vector.tensor_scalar(first, first, K.const("valid"), None, ALU.mult).then_inc(masked, 1)
            dve.wait_ge(masked, 1)

        @block.tensor
        def _(pe):
            for u, (kind, c0, width, which) in enumerate(units):
                s = u % 2
                pe.wait_ge(K.lo_made[s], u // 2 + 1)
                for h in range(2):
                    above_zero(pe, out[s][h], u // 2)
                    project_half(K, 2 * s + h, s, width, h, K.h_hi, K.h_lo)\
                        .then_inc(half0[s] if h == 0 else K.w_used[s], 1)
                if u - 1 in turns:
                    i = turns.index(u - 1)
                    above_zero(pe, turned_out, 2 * (i - 1))
                    for h in range(2):
                        pe.wait_ge(out[(u - 1) % 2][h], (u - 1) // 2 + 1)
                        for t in range(4):
                            last = nc.tensor.transpose(K.ps[:, 4 + 2 * (i % 2) + h, t * P:(t + 1) * P],
                                                       tmp[i % 2][:, (4 * h + t) * P:(4 * h + t + 1) * P], K.ident[:])
                        last.then_inc(turned, 1)


def source_of(C, name):
    return {"kc": C.kc, "kraw": C.kraw}[name]


def phase_compress(K, ctx, A, C):
    nc = K.nc
    sb = lambda n, s, d=F32: ctx.enter_context(nc.sbuf_tensor(n, s, d))
    sem = K.sem
    w1k, w1v, w2k, w2v, pek, pev = C.cmp_weights
    ksrc = [K.mix[0:DK, 2 * i:2 * i + 2, :].rearrange("p g (n l) -> p g n l", l=CMP_STRIDE) for i in range(2)]
    vtmp = sb("cw_vsrc", [P, 2, SEQ])
    vsrc = [vtmp[:, i, :].rearrange("p (n l) -> p n l", l=CMP_STRIDE) for i in range(2)]
    gk, gv = sb("gelu_k", [DK, NG * NCMP]), sb("gelu_v", [DV, NG * NCMP])
    summed, hidden, active = sem("cw_summed"), sem("cw_hidden"), sem("cw_active")
    mapped, zeroed, high, written = sem("cw_mapped"), sem("cw_zeroed"), sem("cw_high"), sem("cw_written")
    hid_k = K.ps[0:DK, 0, 0:NG * NCMP]
    hid_v = [K.ps[0:DV, 1, 0:NCMP], K.ps[0:DV, 4, 0:NCMP]]
    out_k, out_v = K.ps[0:DK, 2, 0:NG * NCMP], K.ps[0:NCMP, 3, 0:NG * DV]

    with nc.Block() as block:
        @block.gpsimd
        def _(pool):
            nc.gpsimd.memset(C.kc_hi[:].bitcast(F32), 0.0).then_inc(zeroed, 1)
            nc.gpsimd.memset(C.kc_lo[:].bitcast(F32), 0.0).then_inc(zeroed, 1)
            nc.gpsimd.memset(C.vcmp[:].bitcast(F32), 0.0).then_inc(zeroed, 1)

        @block.vector
        def _(dve):
            for i in range(2):
                part = slice(i * CMP_STRIDE, (i + 1) * CMP_STRIDE)
                for g in range(NG):
                    nc.vector.tensor_tensor(ksrc[i][:, g], C.kc[:, g, :].rearrange("p (n l) -> p n l", l=CMP_STRIDE),
                                            pek[:, part].unsqueeze(1).to_broadcast([DK, NB, CMP_STRIDE]), ALU.add)\
                        .then_inc(summed, 1)
            for i in range(2):
                nc.vector.tensor_tensor(vsrc[i], C.vc[:].rearrange("p (n l) -> p n l", l=CMP_STRIDE),
                                        pev[:, i * CMP_STRIDE:(i + 1) * CMP_STRIDE].unsqueeze(1)
                                        .to_broadcast([P, NB, CMP_STRIDE]), ALU.add).then_inc(summed, 1)
            dve.wait_ge(mapped, 1)
            dve.wait_ge(high, 1)
            nc.vector.tensor_tensor(C.kc_lo[:, :, 0:NCMP], out_k.rearrange("p (g n) -> p g n", g=NG),
                                    C.kc_hi[:, :, 0:NCMP].bitcast(F32), ALU.subtract).then_inc(written, 1)
            dve.wait_ge(mapped, 2)
            dve.wait_ge(high, 2)
            nc.vector.tensor_tensor(C.vcmp[0:NCMP, :, DV:2 * DV], out_v.rearrange("p (g n) -> p g n", g=NG),
                                    C.vcmp[0:NCMP, :, 0:DV].bitcast(F32), ALU.subtract).then_inc(written, 1)

        @block.tensor
        def _(pe):
            for l in range(CMP_LEN):
                i, c = divmod(l, CMP_STRIDE)
                if c == 0:
                    pe.wait_ge(summed, 2 * i + 2)
                last = nc.tensor.matmul(hid_k.rearrange("p (g n) -> p g n", g=NG), w1k[:, l, :],
                                        ksrc[i][:, :, i:i + NCMP, c], start=(l == 0), stop=(l == CMP_LEN - 1))
            last.then_inc(hidden, 1)
            for g in range(NG):
                rows = slice(g * DV, (g + 1) * DV)
                for l in range(CMP_LEN):
                    i, c = divmod(l, CMP_STRIDE)
                    if c == 0 and g == 0:
                        pe.wait_ge(summed, 5 + i)
                    last = nc.tensor.matmul(hid_v[g], w1v[rows, l, :],
                                            vsrc[i][rows, i:i + NCMP, c], start=(l == 0), stop=(l == CMP_LEN - 1))
            last.then_inc(hidden, 1)
            pe.wait_ge(active, 1)
            nc.tensor.matmul(out_k, w2k[:], gk[:], start=True, stop=True).then_inc(mapped, 1)
            pe.wait_ge(active, 3)
            for g in range(NG):
                last = nc.tensor.matmul(out_v[:, g * DV:(g + 1) * DV], gv[:, g * NCMP:(g + 1) * NCMP], w2v[:],
                                        start=True, stop=True)
            last.then_inc(mapped, 1)

        @block.scalar
        def _(act):
            act.wait_ge(hidden, 1)
            nc.scalar.activation(gk[:], hid_k, ACT.Gelu_apprx_tanh).then_inc(active, 1)
            act.wait_ge(hidden, 2)
            for g in range(NG):
                nc.scalar.activation(gv[:, g * NCMP:(g + 1) * NCMP], hid_v[g], ACT.Gelu_apprx_tanh).then_inc(active, 1)
            act.wait_ge(mapped, 1)
            act.wait_ge(zeroed, 3)
            nc.scalar.activation(C.kc_hi[:, :, 0:NCMP], out_k.rearrange("p (g n) -> p g n", g=NG), ACT.Copy)\
                .then_inc(high, 1)
            act.wait_ge(mapped, 2)
            nc.scalar.activation(C.vcmp[0:NCMP, :, 0:DV], out_v.rearrange("p (g n) -> p g n", g=NG), ACT.Copy)\
                .then_inc(high, 1)


def laid_out(inputs):
    column = lambda a: np.asarray(a)[0].reshape(NK, P).T
    gains = np.stack([column(inputs[n]) for n in ("norm_mix_pre", "norm_ffn_pre", "ret_gn_g")], axis=1)
    return {"consts": shape_constants(), "gains": np.ascontiguousarray(gains),
            "pe_k": np.ascontiguousarray(np.asarray(inputs["cmp_pe_k"])[0].T),
            "pe_v": np.ascontiguousarray(np.asarray(inputs["cmp_pe_v"])[0].T)}



CMP, SEL, WIN = 0, 1, 2
E_WIN, E_CMP, E_SEL = 0, WINDOW + P, WINDOW + 2 * P
LAST_PAIR = NH // 2 - 1
GP = NH // NG // 2


def key_blocks(i):
    first = max(0, i - WB)
    return ([(WIN, b, E_WIN + (b - first) * P) for b in range(first, i + 1)] + [(CMP, 0, E_CMP)]
            + [(SEL, b, E_SEL + b * P) for b in range(i + 1)])


def batches(i):
    blocks = key_blocks(i)
    return [blocks[n:n + 2] for n in range(0, len(blocks), 2)]


BEFORE = [sum(len(batches(i)) for i in range(s)) for s in range(NT + 1)]
PER_PAIR = BEFORE[NT]
assert PER_PAIR % 2 == 0
ORDER = """
A63- C7- T65- H65- X73- Z70- Q00 Q01 Z71- L64- T66- A64- H66- L65- Y70- S00 S02 T70- Y71- L66- A65- A66- T71-
B00 B02 H70- Q02 L70- T72- F6- H71- G6- A70- H72- L71- X02 X00 S03 B03 L72- T73- Y00 S01 A71- B01 H73- A72-
T74- H74- L73- Q03 L74- X03 T75- X01 q0 A73- Y01 P0 T76- l0 S10 h0 A74- B10 S12 H75- Z00 Z01 C0 Q10 H76- S11
L75- B12 S13 L76- X12 A75- B11 X10 Y10 T00 B13 T01 S20 A76- X11 B20 X13 F7- S22 H00 Q11 H01 k0 S21 B22 L00 Q12
X20 S23 B21 P1 Z10 G7- L01 Z11 X22 Y11 C1 X21 T10 A00 A01 Q13 Y20 H10 T11 L10 F0 B23 q1 P2 T12 Z20 S30 G0 l1
H11 A10 S32 B30 Q20 L11 C2 H12 S31 Z21 T20 h1 A11 L12 T21 X23 X30 H20 B32 Y21 A12 F1 H21 S33 B31 Q21 L20 T22
G1 L21 A20 B33 T23 X32 A21 S40 X31 H22 H23 Y30 P3 X33 L22 L23 Z30 A22 S42 A23 Z31 B40 X40 S41 T30 k1 H30 B42
X42 T31 Q22 Y31 F2 H31 C3 B41 Q23 L30 G2 L31 T32 Y40 A30 X41 P4 H32 S43 A31 L32 q2 T33 T34 A32 H33 Z40 H34 B43
Z41 l2 L33 S50 S52 T40 B50 X43 A33 H40 S51 L34 A34 T41 B52 Q30 Y41 L40 X50 F3 H41 C4 G3 T42 A40 X52 L41 B51
A41 T43 H42 L42 H43 L43 X51 S53 B53 T44 Y50 A42 T45 A43 S60 H44 S62 L44 A44 H45 L45 A45 X53 P5 Z50 B60 Y51 Z51
F4 Q31 T50 C5 B62 G4 T51 X60 H50 S61 H51 S63 L50 A50 L51 T52 X62 T53 A51 H52 Y60 H53 Q32 B61 L52 A52 T54 X61
L53 H54 B63 P6 A53 L54 T55 H55 L55 S70 S72 B70 Z60 Z61 A54 X63 C6 T60 B72 A55 T61 H60 S71 L60 F5 H61 G5 T62
Y61 A60 X72 X70 L61 H62 Q33 B71 T63 L62 A61 H63 S73 q3 X71 L63 l3 T64 B73 P7 A62 H64
"""

SCORES = [(0, WIN), (1, WIN), (0, SEL), (1, SEL)]
Q_UNITS = [(0, 1), (1, 1), (0, 0), (1, 0)]


def entries():
    for word in ORDER.split():
        back = word.endswith("-")
        word = word.rstrip("-")
        yield word[0], int(word[1]), int(word[2:] or 0), back


def phase_attention(K, ctx, A, C, n0, next_units):
    nc = K.nc
    sb = lambda n, s, d=F32: ctx.enter_context(nc.sbuf_tensor(n, s, d))
    sem = K.sem
    dsel, dwin, dcmp = sb("d_sel", [P, SEQ]), sb("d_win", [P, WINDOW + P]), sb("d_cmp", [P, NB + (NT - 1) * 8])
    q_hi = [sb(f"q_hi{i}", [DK, SEQ], F32R) for i in range(2)]
    q_lo = [sb(f"q_lo{i}", [DK, SEQ], F32R) for i in range(2)]
    v_sel, v_win = sb("v_sel", [P, NT, P], F32R), sb("v_win", [P, NT, P], F32R)
    E = [sb("probs0", [P, 2, E_SEL + SEQ - P]), sb("probs1", [P, 2, E_SEL + SEQ])]
    t_hi, t_lo = sb("probs_t_hi", [P, 2, 512], F32R), sb("probs_t_lo", [P, 2, 512], F32R)
    o_low = sb("o_low", [DV, 2 * P])
    least, total = sb("least", [P, 2, 3, 2]), sb("total", [P, 2, 3, 2])
    inv, weight = sb("inv_total", [P, 2, 3, 2]), sb("weight", [P, 2, 3, 2])
    sel_gate = sb("sel_gate", [P, NT, 2])
    slope, qscale = sb("slope", [P, 2]), sb("q_scale", [P, 4])
    d_landed = sem("d_landed")
    q_half0, q_high, q_out = sem("q_half0"), sem("q_high"), sem("q_out")
    s_win, s_sel = sem("win_scores"), sem("sel_scores")
    b_win, b_sel = sem("win_biased"), sem("sel_biased")
    e_win, e_sel = sem("win_probs"), sem("sel_probs")
    i_win, w_win = sem("win_inv"), sem("win_weights")
    i_sel, g_sel = sem("sel_inv"), sem("sel_gates_set")
    c_win, c_cmp, c_sel = sem("win_scaled"), sem("cmp_scaled"), sem("sel_scaled")
    turned, high, low, added = sem("turned"), sem("turned_high"), sem("turned_low"), sem("values_added")
    o_low_out, folded = sem("o_low_out"), sem("folded")
    slope_set, pair_set, zeroed = sem("slope_set"), sem("pair_set"), sem("pad_zeroed")
    k_high, k_split = sem("group_high"), sem("group_split")
    ps_sel = K.ps[:, 0:2, :].rearrange("p b n -> p (b n)")
    ps_win = K.ps[:, 2:4, :].rearrange("p b n -> p (b n)")
    O, PQ = K.ps[:, 6, 0:2 * P], K.ps[0:DK, 7, :]
    wv = A["w_in"][0].rearrange("(k p) n -> p k n", p=P)
    gates = C.gate[:].rearrange("p i (b h) -> p i b h", b=3)
    both = lambda ap: ap.rearrange("p t (g e) -> p t g e", g=NG)

    def is_last(j):
        return isinstance(j, int) and j == LAST_PAIR

    def pairs(engine, g, take):
        def body(j, first=False):
            for step, t, n, back in entries():
                if not (back and first):
                    one(step, t, n, j - 1 if back else j)

        def one(step, t, n, pair):
            if not (is_last(pair) and ((step in "Qql" and t >= 2) or step in "hk")):
                take(step, t, n, pair)

        body(GP * g, True)
        if g == NG - 1:
            with engine.Fori(GP * g + 1, LAST_PAIR) as j:
                body(j)
            body(LAST_PAIR)
        else:
            with engine.Fori(GP * g + 1, GP * g + GP) as j:
                body(j)
        for step, t, n, back in entries():
            if back:
                one(step, t, n, GP * (g + 1) - 1)

    def at(j, per, n):
        return j * per + n

    def batch_no(pair, step, k, extra=0):
        return at(pair, PER_PAIR, BEFORE[step] + k + extra)

    def sizes(i):
        return (min(i, WB) + 1) * P, (i + 1) * P

    with nc.Block() as block:
        @block.sync
        def _(sp):
            for name, dst in (("dsel", dsel), ("dwin", dwin), ("dcmp", dcmp)):
                a, b = CONST_AT[name]
                sp.dma_start(dst[:], A["consts"][:, a:b]).then_inc(d_landed, 16)

            with nc.sync.Fori(0, LAST_PAIR) as j:
                for s in range(2):
                    load_unit(sp, K, s, j + (n0 + 1), wv[:, :, bass.ds(j * (2 * DK) + (C_NQ + (2 + s) * DK), DK)], DK)
            for s, (c0, width) in enumerate(next_units):
                load_unit(sp, K, s, n0 + NH // 2, w_in_unit(A["w_in"][0], c0, width), width)

        @block.scalar
        def _(act):
            def q_high_part(hh, h, done, scale):
                act.wait_ge(q_half0 if h == 0 else K.w_used[hh], done)
                nc.scalar.activation(q_hi[hh][:, h * HALF:(h + 1) * HALF], PQ, ACT.Copy, scale=scale).then_inc(q_high, 1)

            def exp(j, s, c):
                hh, br = SCORES[c]
                act.wait_ge(b_win if br == WIN else b_sel, at(j, 2 * NT, 2 * s + hh + 1))
                w, wide = sizes(s)
                e = E[s % 2]
                for b, a, size in (((WIN, E_WIN, w), (CMP, E_CMP, NB)) if br == WIN else ((SEL, E_SEL, wide),)):
                    m = nc.scalar.activation(e[:, hh, a:a + size], e[:, hh, a:a + size], ACT.Exp,
                                             bias=least[:, s % 2, b, hh:hh + 1], scale=-1.0,
                                             accum_out=total[:, s % 2, b, hh:hh + 1])
                m.then_inc(e_win if br == WIN else e_sel, 1)

            def scale(j, s, hh):
                act.wait_ge(w_win, at(j, NT, s + 1))
                e = E[s % 2][:, hh, E_WIN:E_WIN + sizes(s)[0]]
                nc.scalar.activation(e, e, ACT.Copy, scale=weight[:, s % 2, WIN, hh:hh + 1]).then_inc(c_win, 1)

            def copy_high(pair, step, k):
                w = len(batches(step)[k]) * 2 * P
                slot = (BEFORE[step] + k) % 2
                act.wait_ge(turned, batch_no(pair, step, k, 1))
                above_zero(act, added, batch_no(pair, step, k, -1))
                nc.scalar.activation(t_hi[:, slot, 0:w], K.ps[:, 4 + slot, 0:w], ACT.Copy).then_inc(high, 1)

            def fold(pair, step):
                act.wait_ge(added, batch_no(pair, step + 1, 0))
                above_zero(act, folded, at(pair, 2 * NT, 2 * step))
                nc.scalar.activation(o_low[:], O[DV:2 * DV, :], ACT.Copy).then_inc(o_low_out, 1)

            def take(step, t, n, pair):
                if step == "X":
                    exp(pair, t, n)
                elif step == "Z":
                    scale(pair, t, n)
                elif step == "H":
                    copy_high(pair, t, n)
                elif step == "F":
                    fold(pair, t)
                elif step == "q":
                    hh, h = Q_UNITS[t]
                    act.wait_ge(pair_set, at(pair, 1, 1))
                    q_high_part(hh, h, at(pair, 2, 3 + hh) if h == 0 else at(pair, 1, n0 + 1),
                                qscale[0:DK, 2 * (1 - h) + hh:2 * (1 - h) + hh + 1])
                elif step == "h":
                    split_hi(act, K, t, at(pair, 1, n0 + 1), at(pair, 1, n0 + 1), NK * DK)

            for g in range(NG):
                if g == 0:
                    for s in range(2):
                        split_hi(act, K, s, n0, n0, NK * DK)
                else:
                    act.wait_ge(added, GP * g * PER_PAIR)
                    nc.scalar.activation(C.k_hi[:], C.kraw, ACT.Copy).then_inc(k_high, 1)
                for dst, src in ((v_sel, C.vs), (v_win, C.vw)):
                    nc.scalar.activation(dst[:, :, 0:DV], both(src)[:, :, g, :], ACT.Copy).then_inc(k_high, 1)
                if g == 0:
                    act.wait_ge(zeroed, 3)
                    for hh in range(2):
                        q_high_part(hh, 0, 1 + hh, K.const("qscale")[0:DK, hh:hh + 1])
                pairs(nc.scalar, g, take)

        @block.gpsimd
        def _(pool):
            for e in E:
                nc.gpsimd.memset(e[:, :, E_CMP + NB:E_SEL], 0.0).then_inc(zeroed, 1)
            nc.gpsimd.memset(qscale[:], 0.0).then_inc(zeroed, 1)
            pool.wait_ge(zeroed, 3)

            def take(step, t, n, pair):
                slot = t % 2
                if step == "q" and t == 0:
                    above_zero(pool, q_out, at(pair, 4, 2))
                    w = 2 if is_last(pair) else 4
                    nc.gpsimd.tensor_copy(qscale[:, 0:w], K.const("qscale")[:, bass.ds(at(pair, 2, 0), w)])\
                        .then_inc(pair_set, 1)
                elif step == "Y" and t == 0 and n == 0:
                    above_zero(pool, c_sel, at(pair, 2 * NT, 0))
                    nc.gpsimd.tensor_copy(sel_gate[:], gates[:, :, SEL, bass.ds(at(pair, 2, 0), 2)]).then_inc(g_sel, 1)
                elif step == "P":
                    pool.wait_ge(e_win, at(pair, 2 * NT, 2 * t + 2))
                    nc.gpsimd.tensor_tensor(inv[:, slot, CMP::2, :], total[:, slot, CMP::2, :],
                                            K.mhalf[:, 4:8].rearrange("p (b h) -> p b h", h=2), ALU.pow).then_inc(i_win, 1)
                    pool.wait_ge(i_win, at(pair, NT, t + 1))
                    nc.gpsimd.tensor_tensor(weight[:, slot, CMP::2, :], inv[:, slot, CMP::2, :],
                                            gates[:, t, CMP::2, bass.ds(at(pair, 2, 0), 2)], ALU.mult).then_inc(w_win, 1)
                elif step == "C":
                    pool.wait_ge(w_win, at(pair, NT, t + 1))
                    e = E[slot][:, :, E_CMP:E_CMP + NB]
                    nc.gpsimd.tensor_tensor(e, e, weight[:, slot, CMP, :].unsqueeze(2).to_broadcast([P, 2, NB]), ALU.mult)\
                        .then_inc(c_cmp, 1)

            for g in range(NG):
                pairs(nc.gpsimd, g, take)

        @block.vector
        def _(dve):
            def q_low_part(hh, h, count, scale):
                dve.wait_ge(q_high, count)
                toks = slice(h * HALF, (h + 1) * HALF)
                nc.vector.scalar_tensor_tensor(out=q_lo[hh][:, toks], in0=PQ, scalar=scale, in1=q_hi[hh][:, toks].bitcast(F32),
                                               op0=ALU.mult, op1=ALU.subtract).then_inc(q_out, 1)

            def bias(j, s, c):
                hh, br = SCORES[c]
                w, wide = sizes(s)
                dve.wait_ge(s_win if br == WIN else s_sel, at(j, 2 * NT, 2 * s + hh + 1))
                nc.vector.nop(nofuse=True)
                parts = (((WIN, E_WIN, w, ps_win[:, 0:w], dwin[:, WINDOW + P - w:]),
                          (CMP, E_CMP, NB, ps_win[:, WINDOW + P:WINDOW + P + NB], dcmp[:, (NT - 1 - s) * 8:(NT - 1 - s) * 8 + NB]))
                         if br == WIN else ((SEL, E_SEL, wide, ps_sel[:, 0:wide], dsel[:, SEQ - wide:]),))
                for b, a, size, src, d in parts:
                    m = nc.vector.tensor_tensor_reduce(E[s % 2][:, hh, a:a + size], src, d, slope[:, hh:hh + 1], 3e38,
                                                       ALU.add, ALU.min, least[:, s % 2, b, hh:hh + 1])
                m.then_inc(b_win if br == WIN else b_sel, 1)

            def scale(pair, step, hh):
                dve.wait_ge(e_sel, at(pair, 2 * NT, 2 * step + hh + 1))
                nc.vector.reciprocal(inv[:, step % 2, SEL, hh:hh + 1], total[:, step % 2, SEL, hh:hh + 1]).then_inc(i_sel, 1)
                dve.wait_ge(i_sel, at(pair, 2 * NT, 2 * step + hh + 1))
                if step == 0 and hh == 0:
                    dve.wait_ge(g_sel, at(pair, 1, 1))
                e = E[step % 2][:, hh, E_SEL:E_SEL + sizes(step)[1]]
                nc.vector.tensor_scalar(e, e, inv[:, step % 2, SEL, hh:hh + 1], sel_gate[:, step, hh:hh + 1],
                                        ALU.mult, ALU.mult).then_inc(c_sel, 1)

            def copy_low(pair, step, k):
                w = len(batches(step)[k]) * 2 * P
                slot = (BEFORE[step] + k) % 2
                dve.wait_ge(high, batch_no(pair, step, k, 1))
                nc.vector.tensor_tensor(t_lo[:, slot, 0:w], K.ps[:, 4 + slot, 0:w], t_hi[:, slot, 0:w].bitcast(F32),
                                        ALU.subtract).then_inc(low, 1)

            def fold(pair, step):
                dve.wait_ge(o_low_out, at(pair, NT, step + 1))
                for hh in range(2):
                    cols = slice(hh * P, (hh + 1) * P)
                    out = K.mix[hh * DV:(hh + 1) * DV, bass.ds(pair, 1), step * P:(step + 1) * P].rearrange("p a n -> p (a n)")
                    nc.vector.tensor_tensor(out, O[0:DV, cols], o_low[:, cols], ALU.add).then_inc(folded, 1)

            def take(step, t, n, pair):
                if step == "B":
                    if t == 0 and n == 0:
                        if not (isinstance(pair, int) and pair == 0):
                            dve.wait_ge(b_sel, at(pair, 2 * NT, 0))
                            nc.vector.tensor_scalar(slope[:], slope[:], 0.5, None, ALU.mult).then_inc(slope_set, 1)
                        dve.wait_ge(slope_set, at(pair, 1, 1))
                    bias(pair, t, n)
                elif step == "Y":
                    scale(pair, t, n)
                elif step == "L":
                    copy_low(pair, t, n)
                elif step == "G":
                    fold(pair, t)
                elif step == "l":
                    hh, h = Q_UNITS[t]
                    q_low_part(hh, h, at(pair, 4, 3 + t), qscale[0:DK, 2 * (1 - h) + hh:2 * (1 - h) + hh + 1])
                elif step == "k":
                    split_lo(dve, K, t, at(pair, 1, n0 + 1), NK * DK)

            nc.vector.tensor_copy(slope[:], K.const("slope")[:, 0:2]).then_inc(slope_set, 1)
            for g in range(NG):
                k0 = 2 * g
                if g == 0:
                    for s in range(2):
                        split_lo(dve, K, s, n0, NK * DK)
                else:
                    dve.wait_ge(k_high, k0 + 1)
                    nc.vector.tensor_tensor(C.k_lo[:], C.kraw, C.k_hi[:].bitcast(F32), ALU.subtract).then_inc(k_split, 1)
                for n, (dst, src) in enumerate(((v_sel, C.vs), (v_win, C.vw))):
                    dve.wait_ge(k_high, k0 + (1 if g else 0) + n + 1)
                    nc.vector.tensor_tensor(dst[:, :, DV:2 * DV], both(src)[:, :, g, :], dst[:, :, 0:DV].bitcast(F32),
                                            ALU.subtract).then_inc(k_split, 1)
                if g == 0:
                    for hh in range(2):
                        q_low_part(hh, 0, 1 + hh, K.const("qscale")[0:DK, hh:hh + 1])
                    dve.wait_ge(d_landed, 48)
                pairs(nc.vector, g, take)

        @block.tensor
        def _(pe):
            def project(hh, h, c, n, out_before):
                if c == 0:
                    pe.wait_ge(K.lo_made[hh], n)
                    above_zero(pe, q_out, out_before)
                for k in range(2 * c, 2 * c + 2):
                    cols, toks = slice(k * DK, (k + 1) * DK), slice(h * HALF, (h + 1) * HALF)
                    m = mm3(nc, PQ, (K.w_hi[hh][:, cols], K.w_lo[hh][:, cols]), (K.h_hi[:, k, toks], K.h_lo[:, k, toks]),
                            k == 0, k == NK - 1)
                if c == 3:
                    m.then_inc(q_half0 if h == 0 else K.w_used[hh], 1)

            def score(j, s, c, g):
                hh, br = SCORES[c]
                w, wide = sizes(s)
                mine = (q_hi[hh][:, s * P:(s + 1) * P], q_lo[hh][:, s * P:(s + 1) * P])
                above_zero(pe, b_win if br == WIN else b_sel, at(j, 2 * NT, 2 * s + hh))
                if br == WIN:
                    for a in range(0, w, 512):
                        b = min(w, a + 512)
                        keys = slice((s + 1) * P - w + a, (s + 1) * P - w + b)
                        mm3(nc, ps_win[:, a:b], mine, (C.k_hi[:, 1, keys], C.k_lo[:, 1, keys]), True, True)
                    mm3(nc, ps_win[:, WINDOW + P:WINDOW + P + NB], mine, (C.kc_hi[:, g, :], C.kc_lo[:, g, :]), True, True)\
                        .then_inc(s_win, 1)
                else:
                    for a in range(0, wide, 512):
                        b = min(wide, a + 512)
                        m = mm3(nc, ps_sel[:, a:b], mine, (C.k_hi[:, 0, a:b], C.k_lo[:, 0, a:b]), True, True)
                    m.then_inc(s_sel, 1)

            def turn(pair, step, k):
                blocks, slot = batches(step)[k], (BEFORE[step] + k) % 2
                seen = {b[0] for part in batches(step)[:k] for b in part}
                new = {b[0] for b in blocks} - seen
                if WIN in new:
                    pe.wait_ge(c_win, at(pair, 2 * NT, 2 * step + 2))
                if CMP in new:
                    pe.wait_ge(c_cmp, at(pair, NT, step + 1))
                if SEL in new:
                    pe.wait_ge(c_sel, at(pair, 2 * NT, 2 * step + 2))
                above_zero(pe, low, batch_no(pair, step, k, -1))
                for c, (br, b, a) in enumerate(blocks):
                    for hh in range(2):
                        col = (2 * c + hh) * P
                        m = nc.tensor.transpose(K.ps[:, 4 + slot, col:col + P], E[step % 2][:, hh, a:a + P], K.ident[:])
                m.then_inc(turned, 1)

            def add(pair, step, k, g):
                blocks, slot = batches(step)[k], (BEFORE[step] + k) % 2
                pe.wait_ge(low, batch_no(pair, step, k, 1))
                if k == 0:
                    above_zero(pe, folded, at(pair, 2 * NT, 2 * step))
                for c, (br, b, a) in enumerate(blocks):
                    v = C.vcmp[:, g, :] if br == CMP else (v_sel if br == SEL else v_win)[:, b, :]
                    cols = slice(c * 2 * P, (c + 1) * 2 * P)
                    nc.tensor.matmul(O, v, t_hi[:, slot, cols], start=(k == 0 and c == 0), stop=False)
                    m = nc.tensor.matmul(O, v, t_lo[:, slot, cols], start=False,
                                         stop=(k == len(batches(step)) - 1 and c == len(blocks) - 1))
                m.then_inc(added, 1)

            for g in range(NG):
                def take(step, t, n, pair, g=g):
                    if step == "S":
                        if t % (NT // 2) == 0 and n == 0:
                            pe.wait_ge(q_out, at(pair, 4, 4 if t else 2))
                        score(pair, t, n, g)
                    elif step == "T":
                        turn(pair, t, n)
                    elif step == "A":
                        add(pair, t, n, g)
                    elif step == "Q":
                        hh, h = Q_UNITS[t]
                        project(hh, h, n, at(pair, 1, n0 + (2 if h == 0 else 1)), at(pair, 4, 2 + t))

                if g == 0:
                    for hh in range(2):
                        for c in range(4):
                            project(hh, 0, c, n0 + 1, hh)
                pe.wait_ge(k_split, 2 + 3 * g)
                pairs(nc.tensor, g, take)



def half_stream(K, ctx, tag):
    sem = lambda n: K.sem(f"{tag}_{n}")
    half0 = [sem(f"half0_{s}") for s in range(2)]
    out = [[sem(f"out{s}{h}") for h in range(2)] for s in range(2)]
    return half0, out


def phase_gate_nsa(K, ctx, A, n0, next_units):
    nc = K.nc
    half0, out = half_stream(K, ctx, "gb")
    sig = [[ctx.enter_context(nc.sbuf_tensor(f"gb_sig{s}{h}", [P, HALF], F32)) for h in range(2)] for s in range(2)]
    gated = [[K.sem(f"gb_gated{s}{h}") for h in range(2)] for s in range(2)]
    wv = A["w_in"][0].rearrange("(k p) n -> p k n", p=P)
    pairs = NK // 2

    def per_pair(engine, body):
        body(0)
        with engine.Fori(1, pairs) as r:
            body(r)

    with nc.Block() as block:
        @block.sync
        def _(sp):
            with nc.sync.Fori(0, pairs - 1) as r:
                for s in range(2):
                    load_unit(sp, K, s, r + (n0 + 1), wv[:, :, bass.ds(r * (2 * P) + (C_MB + (2 + s) * P), P)], P)
            for s, (c0, width) in enumerate(next_units):
                load_unit(sp, K, s, n0 + pairs, w_in_unit(A["w_in"][0], c0, width), width)

        @block.scalar
        def _(act):
            split_hi(act, K, 0, n0, n0, 1024)

            def body(r):
                for s in range(2):
                    split_hi(act, K, 1 - s, r + (n0 + s), r + (n0 + s), 1024)
                    for h in range(2):
                        act.wait_ge(half0[s] if h == 0 else K.w_used[s], r + (1 if h == 0 else n0 + 1))
                        above_zero(act, gated[s][h], r)
                        nc.scalar.activation(sig[s][h][:], K.ps[:, 2 * s + h, :], ACT.Sigmoid).then_inc(out[s][h], 1)
            per_pair(nc.scalar, body)

        @block.vector
        def _(dve):
            split_lo(dve, K, 0, n0, 1024)

            def body(r):
                for s in range(2):
                    split_lo(dve, K, 1 - s, r + (n0 + s), 1024)
                    for h in range(2):
                        dve.wait_ge(out[s][h], r + 1)
                        m = K.mix[:, bass.ds(r * 2 + s, 1), h * HALF:(h + 1) * HALF].rearrange("p a n -> p (a n)")
                        nc.vector.tensor_tensor(m, m, sig[s][h][:], ALU.mult).then_inc(gated[s][h], 1)
            per_pair(nc.vector, body)

        @block.tensor
        def _(pe):
            def body(r):
                for s in range(2):
                    pe.wait_ge(K.lo_made[s], r + (n0 + 1))
                    for h in range(2):
                        above_zero(pe, out[s][h], r)
                        project_half(K, 2 * s + h, s, P, h, K.h_hi, K.h_lo)\
                            .then_inc(half0[s] if h == 0 else K.w_used[s], 1)
            per_pair(nc.tensor, body)


HH = RH // 2
RP = HH // 2


def ret_units(half):
    return ([("q", C_RQ + (half * RP + i) * P, i) for i in range(RP)] + [("k", C_RK + (half * RP + i) * P, i) for i in range(RP)]
            + [("v", C_RV + (half * HH + i) * P, i) for i in range(HH)])


def phase_ret_project(K, ctx, A, R, half, n0, next_units):
    nc = K.nc
    units = ret_units(half)
    half0, out = half_stream(K, ctx, f"rp{half}")
    sem = lambda n: K.sem(f"rp{half}_{n}")
    tmp = [ctx.enter_context(nc.sbuf_tensor(f"ret{half}_tmp{i}", [P, SEQ], F32)) for i in range(2)]
    turned, turned_out = sem("turned"), sem("turned_out")
    turns = [u for u, unit in enumerate(units) if unit[0] in "kv"]

    def turn_source(u):
        kind, _, i = units[u]
        return R.k[:, i, :] if kind == "k" else tmp[i % 2][:]

    with nc.Block() as block:
        @block.sync
        def _(sp):
            for u in range(2, len(units)):
                load_unit(sp, K, u % 2, n0 + u // 2, w_in_unit(A["w_in"][0], units[u][1], P), P)
            for s, (c0, width) in enumerate(next_units):
                load_unit(sp, K, s, n0 + len(units) // 2, w_in_unit(A["w_in"][0], c0, width), width)

        @block.scalar
        def _(act):
            for u, (kind, c0, i) in enumerate(units):
                s, n = u % 2, n0 + (u + 1) // 2
                split_hi(act, K, (u + 1) % 2, n, n, 1024)
                for h in range(2):
                    act.wait_ge(half0[s] if h == 0 else K.w_used[s], u // 2 + 1 + (0 if h == 0 else n0))
                    toks = slice(h * HALF, (h + 1) * HALF)
                    if kind == "v":
                        above_zero(act, turned, 2 * (turns.index(u) - 1) if i >= 2 else 0)
                        dst = tmp[i % 2][:, toks]
                    else:
                        dst = (R.q if kind == "q" else R.k)[:, i, toks]
                    nc.scalar.activation(dst, K.ps[:, 2 * s + h, :], ACT.Copy).then_inc(out[s][h], 1)

        @block.vector
        def _(dve):
            def turn_out(u):
                kind, _, i = units[u]
                t = turns.index(u)
                for h in range(2):
                    dve.wait_ge(turned, 2 * t + h + 1)
                    src = K.ps[:, 4 + 2 * (t % 2) + h, :].rearrange("p (t c) -> p t c", t=4)
                    if kind == "v":
                        nc.vector.tensor_copy(R.v[:, 4 * h:4 * h + 4, i, :], src).then_inc(turned_out, 1)
                    else:
                        for a in range(2):
                            head = half * HH + 2 * i + a
                            nc.vector.tensor_scalar(R.kz[:, 4 * h:4 * h + 4, i, a * RDK:(a + 1) * RDK],
                                                    src[:, :, a * RDK:(a + 1) * RDK],
                                                    K.const("zeta")[:, head:head + 1], None, ALU.mult).then_inc(turned_out, 1)

            for u in range(len(units)):
                n = n0 + (u + 1) // 2
                split_lo(dve, K, (u + 1) % 2, n, 1024)
                if u - 1 in turns:
                    turn_out(u - 1)
            turn_out(len(units) - 1)

        @block.tensor
        def _(pe):
            counts = [0]
            for u in turns:
                counts.append(counts[-1] + (4 if units[u][0] == "k" else 2))

            def turn(u):
                t = turns.index(u)
                above_zero(pe, turned_out, counts[max(0, t - 1)])
                for h in range(2):
                    pe.wait_ge(out[u % 2][h], u // 2 + 1)
                    for i in range(4):
                        last = nc.tensor.transpose(K.ps[:, 4 + 2 * (t % 2) + h, i * P:(i + 1) * P],
                                                   turn_source(u)[:, (4 * h + i) * P:(4 * h + i + 1) * P], K.ident[:])
                    last.then_inc(turned, 1)

            for u in range(len(units)):
                s = u % 2
                pe.wait_ge(K.lo_made[s], n0 + u // 2 + 1)
                for h in range(2):
                    above_zero(pe, out[s][h], u // 2)
                    project_half(K, 2 * s + h, s, P, h, K.h_hi, K.h_lo).then_inc(half0[s] if h == 0 else K.w_used[s], 1)
                if u - 1 in turns:
                    turn(u - 1)
            turn(len(units) - 1)


def phase_ret_chunks(K, ctx, A, R, half):
    nc = K.nc
    sb = lambda n, s: ctx.enter_context(nc.sbuf_tensor(f"rc{half}_{n}", s, F32))
    sem = lambda n: K.sem(f"rc{half}_{n}")
    dmat = sb("dmat", [P, HH, P])
    inner = sb("inner", [P, 2, HH, P])
    state = sb("state", [P, RP, RDV])
    o, y = sb("o", [P, 2, HH, P]), sb("y", [P, 2, HH, P])
    stats, mv, rstd = sb("stats", [P, 2, HH, 6]), sb("mv", [P, 2, HH, 2]), sb("rstd", [P, 2, HH])
    d_landed, scores, decayed, summed, updated = sem("d_landed"), sem("scores"), sem("decayed"), sem("summed"), sem("updated")
    state_set, scaled, stat, agg = sem("state_set"), sem("scaled"), sem("stat"), sem("agg")
    var_eps, inv_std, normed, turned, turned_out = sem("var_eps"), sem("inv_std"), sem("normed"), sem("turned"), sem("turned_out")
    heads = [(a, a // 2, (a % 2) * RDK) for a in range(HH)]
    score_bank = lambda n, a: K.ps[:, 2 * (n % 2) + a % 2, (a // 2) * P:(a // 2 + 1) * P]
    o_bank = lambda a: K.ps[:, 4 + a % 2, (a // 2) * P:(a // 2 + 1) * P]
    gain = K.gains[:, 2, :]

    with nc.Block() as block:
        @block.sync
        def _(sp):
            a, b = CONST_AT["dmat"]
            w = (b - a) // 2
            sp.dma_start(dmat[:], A["consts"][:, a + half * w:a + (half + 1) * w].rearrange("p (h n) -> p h n", n=P))\
                .then_inc(d_landed, 16)

        @block.tensor
        def _(pe):
            def score(n):
                above_zero(pe, decayed, 2 * (n - 1))
                toks = slice(n * P, (n + 1) * P)
                for a, pair, row in sorted(heads, key=lambda x: x[2]):
                    rows = slice(row, row + RDK)
                    m = nc.tensor.matmul(score_bank(n, a), R.k[rows, pair, toks], R.q[rows, pair, toks], start=True, stop=True)
                m.then_inc(scores, 1)

            def turn(n):
                pe.wait_ge(normed, HH * (n + 1))
                above_zero(pe, turned_out, HH * n)
                for a in range(HH):
                    m = nc.tensor.transpose(K.ps[:, 7, a * P:(a + 1) * P], y[:, n % 2, a, :], K.ident[:])
                m.then_inc(turned, 1)

            score(0)
            for n in range(NT):
                toks = slice(n * P, (n + 1) * P)
                if n + 1 < NT:
                    score(n + 1)
                pe.wait_ge(decayed, 2 * (n + 1))
                above_zero(pe, scaled, 2 * n)
                if n:
                    pe.wait_ge(state_set, RP * n)
                for a, pair, row in sorted(heads, key=lambda x: x[2]):
                    rows = slice(row, row + RDK)
                    m = nc.tensor.matmul(o_bank(a), inner[:, n % 2, a, :], R.v[:, n, a, :], start=True, stop=(n == 0))
                    if n:
                        m = nc.tensor.matmul(o_bank(a), R.q[rows, pair, toks], state[rows, pair, :], start=False, stop=True)
                m.then_inc(summed, 1)
                if n + 1 < NT:
                    for a, pair, row in heads:
                        m = nc.tensor.matmul(K.ps[row:row + RDK, 6, pair * RDV:(pair + 1) * RDV],
                                             R.kz[:, n, pair, row:row + RDK], R.v[:, n, a, :], start=True, stop=True)
                    m.then_inc(updated, 1)
                if n:
                    turn(n - 1)
            turn(NT - 1)

        @block.vector
        def _(dve):
            def norm(n):
                for a in range(HH):
                    dve.wait_ge(scaled, 2 * (n + 1))
                    nc.vector.bn_stats(stats[:, n % 2, a, :], o[:, n % 2, a, :]).then_inc(stat, 1)
                for a in range(HH):
                    dve.wait_ge(stat, HH * n + a + 1)
                    nc.vector.bn_aggr(mv[:, n % 2, a, :], stats[:, n % 2, a, :]).then_inc(agg, 1)

            def normalise(n):
                dve.wait_ge(inv_std, n + 1)
                above_zero(dve, turned, n - 1)
                for a in range(HH):
                    nc.vector.tensor_scalar(y[:, n % 2, a, :], o[:, n % 2, a, :], mv[:, n % 2, a, 0:1],
                                            rstd[:, n % 2, a:a + 1], ALU.subtract, ALU.mult).then_inc(normed, 1)

            dve.wait_ge(d_landed, 16)
            for n in range(NT):
                dve.wait_ge(scores, n + 1)
                for odd in range(2):
                    nc.vector.tensor_tensor(inner[:, n % 2, odd::2, :],
                                            K.ps[:, 2 * (n % 2) + odd, 0:RP * P].rearrange("p (a c) -> p a c", c=P),
                                            dmat[:, odd::2, :], ALU.mult).then_inc(decayed, 1)
                dve.wait_ge(summed, n + 1)
                for odd in range(2):
                    xi = K.const("xi")[:, half * HH + odd:(half + 1) * HH:2].unsqueeze(2).to_broadcast([P, RP, P])
                    nc.vector.tensor_tensor(o[:, n % 2, odd::2, :],
                                            K.ps[:, 4 + odd, 0:RP * P].rearrange("p (a c) -> p a c", c=P), xi, ALU.mult)\
                        .then_inc(scaled, 1)
                if n + 1 < NT:
                    dve.wait_ge(updated, n + 1)
                    for pair in range(RP):
                        src = K.ps[:, 6, pair * RDV:(pair + 1) * RDV]
                        if n == 0:
                            nc.vector.tensor_copy(state[:, pair, :], src).then_inc(state_set, 1)
                        else:
                            c = half * RP + pair
                            nc.vector.scalar_tensor_tensor(out=state[:, pair, :], in0=state[:, pair, :],
                                                           scalar=K.const("decay")[:, c:c + 1], in1=src,
                                                           op0=ALU.mult, op1=ALU.add).then_inc(state_set, 1)
                norm(n)
                if n:
                    normalise(n - 1)
            normalise(NT - 1)

        @block.gpsimd
        def _(pool):
            for n in range(NT):
                pool.wait_ge(agg, HH * (n + 1))
                above_zero(pool, normed, HH * (n - 1))
                nc.gpsimd.tensor_scalar(rstd[:, n % 2, :], mv[:, n % 2, :, 1], GN_EPS, None, ALU.add).then_inc(var_eps, 1)
                pool.wait_ge(var_eps, n + 1)
                nc.gpsimd.tensor_tensor(rstd[:, n % 2, :], rstd[:, n % 2, :], K.mhalf[:, 0:HH], ALU.pow).then_inc(inv_std, 1)

        @block.scalar
        def _(act):
            for n in range(NT):
                act.wait_ge(turned, n + 1)
                for a in range(HH):
                    head = half * HH + a
                    nc.scalar.activation(R.out[:, a, n * P:(n + 1) * P], K.ps[:, 7, a * P:(a + 1) * P], ACT.Copy,
                                         scale=gain[:, head:head + 1]).then_inc(turned_out, 1)


def phase_gate_ret(K, ctx, A, R, half, n0, next_units):
    nc = K.nc
    half0, out = half_stream(K, ctx, f"gr{half}")
    sb = lambda n: [ctx.enter_context(nc.sbuf_tensor(f"gr{half}_{n}{h}", [P, HALF], F32)) for h in range(2)]
    sem = lambda n: [K.sem(f"gr{half}_{n}{h}") for h in range(2)]
    silu, sig = sb("silu"), sb("sig")
    silu_sig, sig_made, added = sem("silu_sig"), sem("sig_made"), sem("added")
    by_ret, by_sig = sem("by_ret"), sem("by_sig")
    wv = A["w_in"][0].rearrange("(k p) n -> p k n", p=P)
    first = [C_RG + half * HH * P, C_MA + half * HH * P]

    def per_head(engine, body):
        body(0)
        with engine.Fori(1, HH) as r:
            body(r)

    with nc.Block() as block:
        @block.sync
        def _(sp):
            with nc.sync.Fori(0, HH - 1) as r:
                for s in range(2):
                    load_unit(sp, K, s, r + (n0 + 1), wv[:, :, bass.ds(r * P + (first[s] + P), P)], P)
            for s, (src, width) in enumerate(next_units):
                load_unit(sp, K, s, n0 + HH, src, width)

        @block.scalar
        def _(act):
            def body(r):
                for s in range(2):
                    split_hi(act, K, 1 - s, r + (n0 + s), r + (n0 + s), 1024)
                    for h in range(2):
                        act.wait_ge(half0[s] if h == 0 else K.w_used[s], r + (1 if h == 0 else n0 + 1))
                        above_zero(act, added[h], r)
                        if s == 0:
                            nc.scalar.activation(silu[h][:], K.ps[:, h, :], ACT.Sigmoid).then_inc(silu_sig[h], 1)
                        else:
                            nc.scalar.activation(sig[h][:], K.ps[:, 2 + h, :], ACT.Sigmoid).then_inc(out[1][h], 1)
            per_head(nc.scalar, body)

        @block.vector
        def _(dve):
            def body(r):
                for s in range(2):
                    split_lo(dve, K, 1 - s, r + (n0 + s), 1024)
                    for h in range(2):
                        toks = slice(h * HALF, (h + 1) * HALF)
                        if s == 0:
                            dve.wait_ge(silu_sig[h], r + 1)
                            nc.vector.tensor_tensor(silu[h][:], K.ps[:, h, :], silu[h][:], ALU.mult).then_inc(out[0][h], 1)
                            dve.wait_ge(out[0][h], r + 1)
                            ret = R.out[:, bass.ds(r, 1), toks].rearrange("p a n -> p (a n)")
                            nc.vector.tensor_tensor(silu[h][:], silu[h][:], ret, ALU.mult).then_inc(by_ret[h], 1)
                        else:
                            dve.wait_ge(by_ret[h], r + 1)
                            dve.wait_ge(out[1][h], r + 1)
                            nc.vector.tensor_tensor(sig[h][:], sig[h][:], silu[h][:], ALU.mult).then_inc(by_sig[h], 1)
                            dve.wait_ge(by_sig[h], r + 1)
                            m = K.mix[:, bass.ds(r + half * HH, 1), toks].rearrange("p a n -> p (a n)")
                            nc.vector.tensor_tensor(m, m, sig[h][:], ALU.add).then_inc(added[h], 1)
            per_head(nc.vector, body)

        @block.tensor
        def _(pe):
            def body(r):
                for s in range(2):
                    pe.wait_ge(K.lo_made[s], r + (n0 + 1))
                    for h in range(2):
                        above_zero(pe, out[s][h], r)
                        project_half(K, 2 * s + h, s, P, h, K.h_hi, K.h_lo)\
                            .then_inc(half0[s] if h == 0 else K.w_used[s], 1)
            per_head(nc.tensor, body)



def wide_unit(W, m, ch):
    return W.rearrange("(k p) n -> p k n", p=P)[:, 2 * m:2 * m + 2, ch * HALF:(ch + 1) * HALF]


MIX_UNITS = [(ch, m) for ch in range(2) for m in range(NK // 2)]


def phase_mix_out(K, ctx, A, y, n0, next_units):
    nc = K.nc
    m_hi = ctx.enter_context(nc.sbuf_tensor("m_hi", [P, NK, SEQ], F32R))
    m_lo = ctx.enter_context(nc.sbuf_tensor("m_lo", [P, NK, SEQ], F32R))
    sem = K.sem
    m_high, m_made, done, out = sem("m_high"), sem("m_made"), sem("mo_done"), sem("mo_out")

    with nc.Block() as block:
        @block.sync
        def _(sp):
            for u in range(2, len(MIX_UNITS)):
                ch, m = MIX_UNITS[u]
                load_unit(sp, K, u % 2, n0 + u // 2, wide_unit(A["w_out"][0], m, ch), HALF)
            for s, (src, width) in enumerate(next_units):
                load_unit(sp, K, s, n0 + len(MIX_UNITS) // 2, src, width)

        @block.scalar
        def _(act):
            for u in range(len(MIX_UNITS)):
                if u < 4:
                    for k in (2 * u, 2 * u + 1):
                        nc.scalar.activation(m_hi[:, k, :], K.mix[:, k, :], ACT.Copy).then_inc(m_high, 1)
                n = n0 + (u + 1) // 2
                split_hi(act, K, (u + 1) % 2, n, n, 1024)

        @block.vector
        def _(dve):
            for u, (ch, m) in enumerate(MIX_UNITS):
                if u < 4:
                    for k in (2 * u, 2 * u + 1):
                        dve.wait_ge(m_high, k + 1)
                        nc.vector.tensor_tensor(m_lo[:, k, :], K.mix[:, k, :], m_hi[:, k, :].bitcast(F32), ALU.subtract)\
                            .then_inc(m_made, 1)
                split_lo(dve, K, (u + 1) % 2, n0 + (u + 1) // 2, 1024)
                if m == NK // 2 - 1:
                    for t in range(NT):
                        if t < NT - 1:
                            dve.wait_ge(done, ch * (NT - 1) + t + 1)
                        else:
                            dve.wait_ge(K.w_used[u % 2], n0 + u // 2 + 1)
                        nc.vector.tensor_copy(y[:, t, ch * HALF:(ch + 1) * HALF], K.ps[:, t, :]).then_inc(out, 1)

        @block.tensor
        def _(pe):
            for u, (ch, m) in enumerate(MIX_UNITS):
                s = u % 2
                pe.wait_ge(K.lo_made[s], n0 + u // 2 + 1)
                if ch == 0:
                    pe.wait_ge(m_made, 2 * m + 2)
                for t in range(NT):
                    toks = slice(t * P, (t + 1) * P)
                    if m == 0 and ch:
                        pe.wait_ge(out, t + 1)
                    for kk in range(2):
                        k, cols = 2 * m + kk, slice(kk * HALF, (kk + 1) * HALF)
                        last = mm3(nc, K.ps[:, t, :], (m_hi[:, k, toks], m_lo[:, k, toks]),
                                   (K.w_hi[s][:, cols], K.w_lo[s][:, cols]), k == 0, k == NK - 1)
                    if t == NT - 1:
                        last.then_inc(K.w_used[s], 1)
                    elif m == NK // 2 - 1:
                        last.then_inc(done, 1)


def phase_residual(K, ctx, A, tag, y, x, gain_row, hi, lo, gain, x_dram):
    nc = K.nc
    sem = lambda n: K.sem(f"{tag}_{n}")
    row = ctx.enter_context(nc.sbuf_tensor(f"{tag}_gain", [P, DM], F32))
    ss, rstd = (ctx.enter_context(nc.sbuf_tensor(f"{tag}_{n}", [P, NT], F32)) for n in ("ss", "rstd"))
    row_landed = sem("row_landed")
    x_landed = [sem(f"x_landed{t}") for t in range(NT)] if x_dram is not None else None
    squared, mean_made, rstd_made, scaled, added = sem("squared"), sem("mean_made"), sem("rstd_made"), sem("scaled"), sem("added")
    N = NormTranspose(K, ctx, f"{tag}n", x, y, hi, lo, gain)

    with nc.Block() as block:
        @block.sync
        def _(sp):
            sp.dma_start(row[:], gain_row.partition_broadcast(P)).then_inc(row_landed, 16)
            if x_dram is not None:
                for t in range(NT):
                    sp.dma_start(x[:, t, :], x_dram[:, t, :]).then_inc(x_landed[t], 16)

        @block.scalar
        def _(act):
            for t in range(NT + 2):
                if t < NT:
                    nc.scalar.activation(lo[:, t, :], y[:, t, :], ACT.Square, accum_out=ss[:, t:t + 1]).then_inc(squared, 1)
                if t >= 2:
                    act.wait_ge(added, t - 1)
                    N.scalar_stats(act, t - 2, hi)
            N.scalar_out(act)

        @block.gpsimd
        def _(pool):
            for t in range(NT):
                c = slice(t, t + 1)
                pool.wait_ge(squared, t + 1)
                nc.gpsimd.tensor_scalar(ss[:, c], ss[:, c], 1.0 / DM, EPS, ALU.mult, ALU.add).then_inc(mean_made, 1)
                pool.wait_ge(mean_made, t + 1)
                nc.gpsimd.tensor_tensor(rstd[:, c], ss[:, c], K.mhalf[:, 0:1], ALU.pow).then_inc(rstd_made, 1)
            N.pool(pool)

        @block.vector
        def _(dve):
            dve.wait_ge(row_landed, 16)
            for t in range(NT):
                dve.wait_ge(rstd_made, t + 1)
                nc.vector.scalar_tensor_tensor(out=y[:, t, :], in0=y[:, t, :], scalar=rstd[:, t:t + 1], in1=row[:],
                                               op0=ALU.mult, op1=ALU.mult).then_inc(scaled, 1)
                dve.wait_ge(scaled, t + 1)
                if x_dram is not None:
                    dve.wait_ge(x_landed[t], 16)
                nc.vector.tensor_tensor(x[:, t, :], x[:, t, :], y[:, t, :], ALU.add).then_inc(added, 1)
            N.vector(dve)

        @block.tensor
        def _(pe):
            N.tensor(pe)


FPI = 2
FIT = NF // FPI


def ffn_units(A, c):
    win = A["w_ffn_in"][0].rearrange("(k p) n -> p k n", p=P)
    return [(win[:, :, bass.ds(c * (FPI * P) + (b * P + part * DFF), P)], P) for b in range(FPI) for part in range(2)]


def phase_ffn(K, ctx, A, h_hi, h_lo, total, n0, next_units):
    nc = K.nc
    sb = lambda n, s, d=F32: ctx.enter_context(nc.sbuf_tensor(n, s, d))
    sem = K.sem
    a_hi, a_lo = sb("a_hi", [P, FPI, SEQ], F32R), sb("a_lo", [P, FPI, SEQ], F32R)
    gate = [sb(f"ffn_gate{h}", [P, HALF]) for h in range(2)]
    w2_in = [sb(f"w2_in{b}", [P, DM]) for b in range(FPI)]
    w2_hi = [sb(f"w2_hi{b}", [P, DM], F32R) for b in range(FPI)]
    w2_lo = [sb(f"w2_lo{b}", [P, DM], F32R) for b in range(FPI)]
    w2_landed = [sem(f"w2_landed{b}") for b in range(FPI)]
    w2_high, w2_low = [sem(f"w2_high{b}") for b in range(FPI)], [sem(f"w2_low{b}") for b in range(FPI)]
    half0 = [sem(f"ffn_half0_{s}") for s in range(2)]
    sig = [sem(f"ffn_sig{h}") for h in range(2)]
    u_out = [sem(f"ffn_u_out{h}") for h in range(2)]
    v_out = [sem(f"ffn_v_out{h}") for h in range(2)]
    high = [sem(f"ffn_high{h}") for h in range(2)]
    made = [sem(f"ffn_made{h}") for h in range(2)]
    done, out = sem("ffn_done"), sem("ffn_out")
    NO = 2 * NT

    def per_iteration(engine, body):
        body(0)
        with engine.Fori(1, FIT) as c:
            body(c)

    def half_ready(e, s, c, b, h):
        e.wait_ge(half0[s] if h == 0 else K.w_used[s], c * FPI + ((b if h == 0 else n0 + b) + 1))

    with nc.Block() as block:
        @block.sync
        def _(sp):
            def body(c, skip=0):
                for u, (src, width) in enumerate(ffn_units(A, c)):
                    if u >= skip:
                        load_unit(sp, K, u % 2, c * FPI + (n0 + u // 2), src, width)
                for b in range(FPI):
                    above_zero(sp, w2_high[b], c)
                    above_zero(sp, w2_low[b], c)
                    sp.dma_start(w2_in[b][:], A["w_ffn_out"][0][bass.ds(c * (FPI * P) + b * P, P), :])\
                        .then_inc(w2_landed[b], 16)
            body(0, skip=2)
            with nc.sync.Fori(1, FIT) as c:
                body(c)
            for s, (src, width) in enumerate(next_units):
                load_unit(sp, K, s, n0 + FIT * FPI, src, width)

        @block.scalar
        def _(act):
            def next_split(s, c, b):
                n = c * FPI + (n0 + b)
                split_hi(act, K, s, n, n, 1024)

            def body(c):
                next_split(1, c, 0)
                for b in range(FPI):
                    for h in range(2):
                        if h == 1:
                            next_split(0, c, b + 1)
                        half_ready(act, 0, c, b, h)
                        above_zero(act, made[h], c * FPI + b)
                        nc.scalar.activation(gate[h][:], K.ps[:, h, :], ACT.Sigmoid).then_inc(sig[h], 1)
                    if b == FPI - 1:
                        for i in range(FPI):
                            act.wait_ge(w2_landed[i], c * 16 + 16)
                            above_zero(act, done, c * NO)
                            nc.scalar.activation(w2_hi[i][:], w2_in[i][:], ACT.Copy).then_inc(w2_high[i], 1)
                    for h in range(2):
                        toks = slice(h * HALF, (h + 1) * HALF)
                        act.wait_ge(v_out[h], c * FPI + (b + 1))
                        nc.scalar.activation(a_hi[:, b, toks], gate[h][:], ACT.Copy).then_inc(high[h], 1)
                    if b < FPI - 1:
                        next_split(1, c, b + 1)
            per_iteration(nc.scalar, body)

        @block.vector
        def _(dve):
            def outputs(c):
                first = isinstance(c, int) and c == 0
                for o in range(NO):
                    t, ch = divmod(o, 2)
                    dve.wait_ge(done, c * NO + (o + 1))
                    dst, src = total[:, t, ch * HALF:(ch + 1) * HALF], K.ps[:, 4 + o % 4, :]
                    if first:
                        nc.vector.tensor_copy(dst, src).then_inc(out, 1)
                    else:
                        nc.vector.tensor_tensor(dst, src, dst, ALU.add).then_inc(out, 1)

            def next_split(s, c, b):
                split_lo(dve, K, s, c * FPI + (n0 + b), 1024)

            def body(c, before):
                next_split(1, c, 0)
                for b in range(FPI):
                    next_split(0, c, b + 1)
                    for h in range(2):
                        dve.wait_ge(sig[h], c * FPI + (b + 1))
                        nc.vector.tensor_tensor(gate[h][:], K.ps[:, h, :], gate[h][:], ALU.mult).then_inc(u_out[h], 1)
                    if b == 0 and before is not None:
                        outputs(before)
                    if b == FPI - 1:
                        for i in range(FPI):
                            dve.wait_ge(w2_high[i], c + 1)
                            nc.vector.tensor_tensor(w2_lo[i][:], w2_in[i][:], w2_hi[i][:].bitcast(F32), ALU.subtract)\
                                .then_inc(w2_low[i], 1)
                    for h in range(2):
                        toks = slice(h * HALF, (h + 1) * HALF)
                        half_ready(dve, 1, c, b, h)
                        dve.wait_ge(u_out[h], c * FPI + (b + 1))
                        nc.vector.tensor_tensor(gate[h][:], K.ps[:, 2 + h, :], gate[h][:], ALU.mult).then_inc(v_out[h], 1)
                        dve.wait_ge(high[h], c * FPI + (b + 1))
                        nc.vector.tensor_tensor(a_lo[:, b, toks], gate[h][:], a_hi[:, b, toks].bitcast(F32),
                                                ALU.subtract).then_inc(made[h], 1)
                    if b < FPI - 1:
                        next_split(1, c, b + 1)
            body(0, None)
            body(1, 0)
            with nc.vector.Fori(2, FIT) as c:
                body(c, c - 1)
            outputs(FIT - 1)

        @block.tensor
        def _(pe):
            def project(c, b, s):
                pe.wait_ge(K.lo_made[s], c * FPI + (n0 + b + 1))
                for h in range(2):
                    above_zero(pe, (u_out if s == 0 else v_out)[h], c * FPI + b)
                    project_half(K, 2 * s + h, s, P, h, h_hi, h_lo).then_inc(half0[s] if h == 0 else K.w_used[s], 1)

            def outputs(c):
                for b in range(FPI):
                    pe.wait_ge(w2_low[b], c + 1)
                for o in range(NO):
                    t, ch = divmod(o, 2)
                    toks, cols = slice(t * P, (t + 1) * P), slice(ch * HALF, (ch + 1) * HALF)
                    if o % NT == 0:
                        pe.wait_ge(made[o // NT], c * FPI + FPI)
                    above_zero(pe, out, c * NO + (o - 3))
                    for b in range(FPI):
                        m = mm3(nc, K.ps[:, 4 + o % 4, :], (a_hi[:, b, toks], a_lo[:, b, toks]),
                                (w2_hi[b][:, cols], w2_lo[b][:, cols]), b == 0, b == FPI - 1)
                    m.then_inc(done, 1)

            def body(c, before):
                project(c, 0, 0)
                if before is not None:
                    outputs(before)
                project(c, 0, 1)
                for b in range(1, FPI):
                    for s in range(2):
                        project(c, b, s)
            body(0, None)
            body(1, 0)
            with nc.tensor.Fori(2, FIT) as c:
                body(c, c - 1)
            outputs(FIT - 1)


PLE_UNITS = [(ch, m) for ch in range(2) for m in range(NK // 2 + 1)]


def ple_unit(A, u):
    ch, m = PLE_UNITS[u]
    return (wide_unit(A["w_ple_gate"][0], m, ch) if m < NK // 2 else wide_unit(A["w_ple"][0], 0, ch)), HALF


def phase_ple(K, ctx, A, x, x_hi, x_lo, spare, n0):
    nc = K.nc
    sem = K.sem
    p_in = spare[:, 0:2, :].rearrange("p a (t c) -> p (a t) c", c=PLE)
    p_hi = ctx.enter_context(nc.sbuf_tensor("p_hi", [P, PLE // P, SEQ], F32R))
    p_lo = ctx.enter_context(nc.sbuf_tensor("p_lo", [P, PLE // P, SEQ], F32R))
    sig = ctx.enter_context(nc.sbuf_tensor("ple_sig", [P, NT, HALF], F32))
    p_landed, p_turned, p_high, p_made = sem("p_landed"), sem("p_turned"), sem("p_high"), sem("p_made")
    gated, embedded = sem("ple_gated"), sem("ple_embedded")
    sig_made, scaled, added, stored = sem("ple_sig_made"), sem("ple_scaled"), sem("ple_added"), sem("ple_stored")
    ov = A["out"][0].rearrange("(t p) d -> p t d", p=P)
    G = NK // 2

    with nc.Block() as block:
        @block.sync
        def _(sp):
            sp.dma_start(p_in, A["p"][0, 0].rearrange("(t p) c -> p t c", p=P)).then_inc(p_landed, 16)
            for u in range(2, len(PLE_UNITS)):
                src, width = ple_unit(A, u)
                load_unit(sp, K, u % 2, n0 + u // 2, src, width)
            for n in range(2 * NT):
                ch, t = divmod(n, NT)
                sp.wait_ge(added, n + 1)
                cols = slice(ch * HALF, (ch + 1) * HALF)
                sp.dma_start(ov[:, t, cols], x[:, t, cols]).then_inc(stored, 16)
            sp.wait_ge(stored, 16 * 2 * NT)

        @block.scalar
        def _(act):
            for n in range(4):
                k, h = divmod(n, 2)
                act.wait_ge(p_turned, n + 1)
                nc.scalar.activation(p_hi[:, k, h * HALF:(h + 1) * HALF], K.ps[:, 4 + n, :], ACT.Copy).then_inc(p_high, 1)
            for u, (ch, m) in enumerate(PLE_UNITS):
                if u + 1 < len(PLE_UNITS):
                    n = n0 + (u + 1) // 2
                    split_hi(act, K, (u + 1) % 2, n, n, 1024)
                if m == G - 1:
                    for t in range(NT):
                        if t < NT - 1:
                            act.wait_ge(gated, ch * (NT - 1) + t + 1)
                        else:
                            act.wait_ge(K.w_used[u % 2], n0 + u // 2 + 1)
                        above_zero(act, scaled, (ch - 1) * NT + t + 1)
                        nc.scalar.activation(sig[:, t, :], K.ps[:, t, :], ACT.Sigmoid).then_inc(sig_made, 1)

        @block.vector
        def _(dve):
            for n in range(4):
                k, h = divmod(n, 2)
                dve.wait_ge(p_high, n + 1)
                toks = slice(h * HALF, (h + 1) * HALF)
                nc.vector.tensor_tensor(p_lo[:, k, toks], K.ps[:, 4 + n, :], p_hi[:, k, toks].bitcast(F32), ALU.subtract)\
                    .then_inc(p_made, 1)
            for u, (ch, m) in enumerate(PLE_UNITS):
                if u + 1 < len(PLE_UNITS):
                    split_lo(dve, K, (u + 1) % 2, n0 + (u + 1) // 2, 1024)
                if m == G:
                    for t in range(NT):
                        n = ch * NT + t
                        if t < NT - 1:
                            dve.wait_ge(embedded, ch * (NT - 1) + t + 1)
                        else:
                            dve.wait_ge(K.w_used[u % 2], n0 + u // 2 + 1)
                        dve.wait_ge(sig_made, n + 1)
                        cols = slice(ch * HALF, (ch + 1) * HALF)
                        nc.vector.tensor_tensor(sig[:, t, :], K.ps[:, t, :], sig[:, t, :], ALU.mult).then_inc(scaled, 1)
                        dve.wait_ge(scaled, n + 1)
                        nc.vector.tensor_tensor(x[:, t, cols], x[:, t, cols], sig[:, t, :], ALU.add).then_inc(added, 1)

        @block.tensor
        def _(pe):
            pe.wait_ge(p_landed, 16)
            for n in range(4):
                k, h = divmod(n, 2)
                for t in range(4):
                    last = nc.tensor.transpose(K.ps[:, 4 + n, t * P:(t + 1) * P], p_in[:, 4 * h + t, k * P:(k + 1) * P],
                                               K.ident[:])
                last.then_inc(p_turned, 1)
            for u, (ch, m) in enumerate(PLE_UNITS):
                s = u % 2
                pe.wait_ge(K.lo_made[s], n0 + u // 2 + 1)
                if u == 0 or m == G:
                    pe.wait_ge(p_made, 4)
                a_hi, a_lo = (x_hi, x_lo) if m < G else (p_hi, p_lo)
                for t in range(NT):
                    if m == G:
                        pe.wait_ge(sig_made, ch * NT + t + 1)
                    if m == 0 and ch:
                        pe.wait_ge(scaled, t + 1)
                    toks = slice(t * P, (t + 1) * P)
                    for kk in range(2):
                        k = 2 * m + kk if m < G else kk
                        cols = slice(kk * HALF, (kk + 1) * HALF)
                        last = mm3(nc, K.ps[:, t, :], (a_hi[:, k, toks], a_lo[:, k, toks]),
                                   (K.w_hi[s][:, cols], K.w_lo[s][:, cols]), k == 0, (k == NK - 1) or (m == G and kk == 1))
                    if t == NT - 1:
                        last.then_inc(K.w_used[s], 1)
                    elif m == G - 1:
                        last.then_inc(gated, 1)
                    elif m == G:
                        last.then_inc(embedded, 1)



def layer(nc, A):
    with ExitStack() as ctx:
        K, C = Core(), Core()
        setup(nc, ctx, K)
        small = lambda n, s: ctx.enter_context(nc.sbuf_tensor(n, s, F32))
        K.gains = small("gains", [P, 3, NK])
        K.small = small("consts", [P, SMALL_W])
        K.ss, K.rstd, K.mhalf = small("ss", [P, NT]), small("rstd", [P, NT]), small("mhalf", [P, 16])
        K.mix = ctx.enter_context(nc.sbuf_tensor("mix", [P, NK, SEQ], F32))
        with ExitStack() as proj:
            K.h_hi = proj.enter_context(nc.sbuf_tensor("h_hi", [P, NK, SEQ], F32R))
            K.h_lo = proj.enter_context(nc.sbuf_tensor("h_lo", [P, NK, SEQ], F32R))
            with ExitStack() as c:
                phase_norm1(K, c, A, [(u[1], u[2]) for u in kv_units()[:2]])
            with ExitStack() as attention:
                sb = lambda n, s, d=F32: attention.enter_context(nc.sbuf_tensor(n, s, d))
                C.k_hi, C.k_lo = sb("k_hi", [DK, 2, SEQ], F32R), sb("k_lo", [DK, 2, SEQ], F32R)
                C.kraw = K.mix[0:DK, 6:8, :]
                C.vs, C.vw = (K.mix[:, c, :].rearrange("p (t c) -> p t c", t=NT) for c in (4, 5))
                C.gate = sb("branch_gate", [P, NT, 3 * NH])
                C.kc_hi, C.kc_lo = sb("kc_hi", [DK, NG, NB], F32R), sb("kc_lo", [DK, NG, NB], F32R)
                C.vcmp = sb("v_cmp", [P, NG, P], F32R)
                with ExitStack() as c:
                    C.kc = c.enter_context(nc.sbuf_tensor("kc", [DK, NG, SEQ], F32))
                    C.vc = c.enter_context(nc.sbuf_tensor("vc", [P, SEQ], F32))
                    weight = lambda n, s: c.enter_context(nc.sbuf_tensor(n, s, F32))
                    C.cmp_weights = (weight("w1k", [DK, CMP_LEN, DK]), weight("w1v", [P, CMP_LEN, DV]),
                                     weight("w2k", [DK, DK]), weight("w2v", [DV, DV]),
                                     weight("pek", [DK, CMP_LEN]), weight("pev", [P, CMP_LEN]))
                    with ExitStack() as c2:
                        phase_kv(K, c2, A, C, [(C_NQ, DK), (C_NQ + DK, DK)])
                    with ExitStack() as c2:
                        phase_compress(K, c2, A, C)
                with ExitStack() as c:
                    phase_attention(K, c, A, C, len(kv_units()) // 2, [(C_MB, P), (C_MB + P, P)])
            n = len(kv_units()) // 2 + NH // 2
            K.renew()
            with ExitStack() as c:
                phase_gate_nsa(K, c, A, n, [(u[1], P) for u in ret_units(0)[:2]])
            n += NK // 2
            with ExitStack() as retention:
                R = Core()
                sb = lambda n, s: retention.enter_context(nc.sbuf_tensor(n, s, F32))
                R.q, R.k = sb("ret_q", [P, RP, SEQ]), sb("ret_k", [P, RP, SEQ])
                R.kz, R.v = sb("ret_kz", [P, NT, RP, P]), sb("ret_v", [P, NT, HH, P])
                R.out = sb("ret_out", [P, HH, SEQ])
                for half in range(2):
                    with ExitStack() as c:
                        phase_ret_project(K, c, A, R, half, n, [(C_RG + half * HH * P, P), (C_MA + half * HH * P, P)])
                    n += len(ret_units(half)) // 2
                    with ExitStack() as c:
                        phase_ret_chunks(K, c, A, R, half)
                    with ExitStack() as c:
                        if half == 0:
                            after = [(w_in_unit(A["w_in"][0], u[1], P), P) for u in ret_units(1)[:2]]
                        else:
                            after = [(wide_unit(A["w_out"][0], m, ch), HALF) for ch, m in MIX_UNITS[:2]]
                        phase_gate_ret(K, c, A, R, half, n, after)
                    n += HH
                K.renew()

        tail = ctx.enter_context(ExitStack())
        y = tail.enter_context(nc.sbuf_tensor("y", [P, NT, DM], F32))
        with ExitStack() as c:
            phase_mix_out(K, c, A, y, n, ffn_units(A, 0)[:2])
        n += len(MIX_UNITS) // 2
        x = K.mix
        h_hi = tail.enter_context(nc.sbuf_tensor("h2_hi", [P, NK, SEQ], F32R))
        h_lo = tail.enter_context(nc.sbuf_tensor("h2_lo", [P, NK, SEQ], F32R))
        xv = A["x"][0].rearrange("(t p) d -> p t d", p=P)
        with ExitStack() as c:
            phase_residual(K, c, A, "r1", y, x, A["norm_mix_post"][0], h_hi, h_lo, K.gains[:, 1, :], xv)
        K.renew()
        with ExitStack() as c:
            phase_ffn(K, c, A, h_hi, h_lo, y, n, [ple_unit(A, 0), ple_unit(A, 1)])
        n += FIT * FPI
        with ExitStack() as c:
            phase_residual(K, c, A, "r2", y, x, A["norm_ffn_post"][0], h_hi, h_lo, None, None)
        with ExitStack() as c:
            phase_ple(K, c, A, x, h_hi, h_lo, y, n)

_INS = ["x", "p", "norm_mix_pre", "norm_mix_post", "norm_ffn_pre", "norm_ffn_post", "w_in", "ret_gn_g",
        "cmp_pe_k", "cmp_w1_k", "cmp_w2_k", "cmp_pe_v", "cmp_w1_v", "cmp_w2_v",
        "w_out", "w_ffn_in", "w_ffn_out", "w_ple", "w_ple_gate"]


def kernel(**inputs):
    import concourse.bacc as _bacc
    from concourse.bass_utils import run_bass_kernel_spmd as _run

    nc = _bacc.Bacc("TRN2", target_bir_lowering=False, num_devices=1)
    given = {name: np.ascontiguousarray(inputs[name]) for name in _INS}
    given.update(laid_out(inputs))
    arrays, A = {}, {}
    for name, a in given.items():
        arrays[f"in_{name}"] = a
        A[name] = nc.dram_tensor(f"in_{name}", a.shape, mybir.dt.from_np(a.dtype), kind="ExternalInput").ap()
    A["out"] = nc.dram_tensor("out", (1, SEQ, DM), F32, kind="ExternalOutput").ap()
    layer(nc, A)
    return _run(nc, [arrays], core_ids=[0]).results[0]["out"]
```

```python
from contextlib import ExitStack

import numpy as np
import concourse.bass as bass
from concourse import mybir

F32 = mybir.dt.float32
F32R = mybir.dt.float32r
ALU = mybir.AluOpType
ACT = mybir.ActivationFunctionType

P = 128
SEQ, DM = 1024, 1024
NT, NK = SEQ // P, DM // P
HALF = 512
EPS, GN_EPS = 1e-6, 1e-5
RH, RDK, RDV = 8, 64, 128
NH, NG, DK, DV = 16, 2, 96, 64
HPG = NH // NG
CMP_LEN, CMP_STRIDE = 32, 16
NCMP = (SEQ - CMP_LEN) // CMP_STRIDE + 1
NB = SEQ // CMP_STRIDE
WINDOW = 512
WB = WINDOW // P
DFF = 2816
NF = DFF // P
PLE = 256
BIG = 1e30

C_RQ = 0
C_RK = C_RQ + RH * RDK
C_RV = C_RK + RH * RDK
C_RG = C_RV + RH * RDV
C_NQ = C_RG + RH * RDV
C_KC = C_NQ + NH * DK
C_VC = C_KC + NG * DK
C_KS = C_VC + NG * DV
C_VS = C_KS + NG * DK
C_KW = C_VS + NG * DV
C_VW = C_KW + NG * DK
C_NGATE = C_VW + NG * DV
C_MA = C_NGATE + 3 * NH
C_MB = C_MA + DM

_PARTS = [("slope", NH), ("qscale", NH), ("valid", 1), ("xi", RH), ("zeta", RH), ("decay", RH // 2),
          ("ident", P), ("dsel", SEQ), ("dwin", WINDOW + P), ("dcmp", NB + (NT - 1) * 8), ("dmat", RH * P)]
CONST_AT, _n = {}, 0
for _name, _w in _PARTS:
    CONST_AT[_name] = (_n, _n + _w)
    _n += _w
CONST_W = _n
SMALL_W = CONST_AT["ident"][0]


def shape_constants():
    c = np.zeros((P, CONST_W), np.float64)

    def put(name, value):
        a, b = CONST_AT[name]
        c[:, a:b] = value

    q = np.arange(P)[:, None]
    put("ident", np.eye(P))
    d = q + (SEQ - P) - np.arange(SEQ)[None, :]
    put("dsel", np.where(d >= 0, d, BIG))
    d = q + WINDOW - np.arange(WINDOW + P)[None, :]
    put("dwin", np.where((d >= 0) & (d < WINDOW), d, BIG))
    v = np.arange(NB + (NT - 1) * 8)[None, :] - (NT - 1) * 8
    d = q - CMP_STRIDE * v - (CMP_LEN - 1)
    put("dcmp", np.where(d >= 0, d, BIG))
    slope = 2.0 ** (-8.0 * (np.arange(NH) + 1.0) / NH)
    put("slope", slope[None, :])
    put("qscale", -(DK ** -0.5) / slope[None, :])
    put("valid", q >= CMP_LEN - 1)
    log_g = np.log1p(-(2.0 ** (-5.0 - np.arange(RH))))
    s, t = np.arange(P)[:, None, None], np.arange(P)[None, None, :]
    dmat = np.where(t >= s, np.exp(-log_g[None, :, None] * (s + 1.0)) * RDK ** -0.5, 0.0)
    put("dmat", np.broadcast_to(dmat, (P, RH, P)).reshape(P, RH * P))
    put("xi", np.exp(log_g[None, :] * (q + 1.0)))
    put("zeta", np.exp(log_g[None, :] * (P - 1.0 - q)) * RDK ** -0.5)
    decay = np.exp(log_g * P)
    put("decay", np.where(q < RDK, decay[None, 0::2], decay[None, 1::2]))
    return c.astype(np.float32)


def above_zero(engine, sem, value):
    if not (isinstance(value, int) and value <= 0):
        engine.wait_ge(sem, value)


class Core:

    def const(self, name):
        a, b = CONST_AT[name]
        return self.small[:, a:b]


def setup(nc, ctx, K):
    def sb(name, shape, dt=F32):
        return ctx.enter_context(nc.sbuf_tensor(name, shape, dt))

    sem = nc.alloc_semaphore
    K.own = []

    def phase_sem(name):
        K.own.append(nc.alloc_semaphore(name))
        return K.own[-1]

    def renew():
        nc.clear_and_free_semaphores(K.own)
        K.own = []
        nc.all_engine_barrier()

    K.sem, K.renew = phase_sem, renew

    K.nc = nc
    K.ps = ctx.enter_context(nc.psum_tensor("ps", [P, 8, 512], F32))
    K.stage = [sb(f"stage{s}", [P, 1024]) for s in range(2)]
    K.w_hi = [sb(f"w_hi{s}", [P, 1024], F32R) for s in range(2)]
    K.w_lo = [sb(f"w_lo{s}", [P, 1024], F32R) for s in range(2)]
    K.ident = sb("ident", [P, P])
    K.landed = [sem(f"w_landed{s}") for s in range(2)]
    K.hi_made = [sem(f"w_hi_made{s}") for s in range(2)]
    K.lo_made = [sem(f"w_lo_made{s}") for s in range(2)]
    K.w_used = [sem(f"w_used{s}") for s in range(2)]


def load_unit(sp, K, s, n, src, width):
    above_zero(sp, K.hi_made[s], n)
    above_zero(sp, K.lo_made[s], n)
    dst = K.stage[s][:, 0:src.shape[1] * width].rearrange("p (k c) -> p k c", c=width)
    sp.dma_start(dst, src).then_inc(K.landed[s], 16)


def split_hi(act, K, s, n, r, size, dst=None):
    act.wait_ge(K.landed[s], 16 * n + 16)
    if dst is None:
        above_zero(act, K.w_used[s], r)
        dst = K.w_hi[s][:, 0:size]
    K.nc.scalar.activation(dst, K.stage[s][:, 0:size], ACT.Copy).then_inc(K.hi_made[s], 1)


def split_lo(dve, K, s, n, size, dst=None, hi=None):
    dve.wait_ge(K.hi_made[s], n + 1)
    dst = K.w_lo[s][:, 0:size] if dst is None else dst
    hi = K.w_hi[s][:, 0:size] if hi is None else hi
    K.nc.vector.tensor_tensor(dst, K.stage[s][:, 0:size], hi.bitcast(F32), ALU.subtract).then_inc(K.lo_made[s], 1)


def mm3(nc, out, a, b, start, stop):
    nc.tensor.matmul(out, a[0], b[0], start=start, stop=False)
    nc.tensor.matmul(out, a[0], b[1], start=False, stop=False)
    return nc.tensor.matmul(out, a[1], b[0], start=False, stop=stop)


def project_half(K, bank, s, width, half, act_hi, act_lo):
    for k in range(NK):
        cols = slice(k * width, (k + 1) * width)
        toks = slice(half * HALF, (half + 1) * HALF)
        last = mm3(K.nc, K.ps[0:width, bank, :], (K.w_hi[s][:, cols], K.w_lo[s][:, cols]),
                   (act_hi[:, k, toks], act_lo[:, k, toks]), k == 0, k == NK - 1)
    return last


class NormTranspose:
    def __init__(self, K, tag, x, xn, hi, lo, gain, bank=4):
        sem = lambda n: K.sem(f"{tag}_{n}")
        self.bank = bank
        self.K, self.x, self.xn, self.hi, self.lo, self.gain = K, x, xn, hi, lo, gain
        self.ss, self.rstd, self.mhalf = K.ss, K.rstd, K.mhalf
        self.squared, self.rstd_made, self.mean_made = sem("squared"), sem("rstd_made"), sem("mean_made")
        self.scaled, self.turned = sem("scaled"), sem("turned")
        self.hi_out, self.lo_out = sem("hi_out"), sem("lo_out")

    def scalar_stats(self, act, t):
        self.K.nc.scalar.activation(self.lo[:, t, :], self.x[:, t, :], ACT.Square,
                                    accum_out=self.ss[:, t:t + 1]).then_inc(self.squared, 1)

    def scalar_scale(self, act, t):
        act.wait_ge(self.rstd_made, t + 1)
        self.K.nc.scalar.activation(self.xn[:, t, :], self.x[:, t, :], ACT.Copy, scale=self.rstd[:, t:t + 1])\
            .then_inc(self.scaled, 1)

    def scalar_out(self, act, half):
        for k in range(NK):
            n = half * NK + k
            act.wait_ge(self.turned, n + 1)
            dst = self.hi[:, k, half * HALF:(half + 1) * HALF]
            src = self.K.ps[:, self.bank + n % 4, :]
            if self.gain is None:
                i = self.K.nc.scalar.activation(dst, src, ACT.Copy)
            else:
                i = self.K.nc.scalar.activation(dst, src, ACT.Copy, scale=self.gain[:, k:k + 1])
            i.then_inc(self.hi_out, 1)

    def pool_rstd(self, pool, t):
        nc, c = self.K.nc, slice(t, t + 1)
        pool.wait_ge(self.squared, t + 1)
        nc.gpsimd.tensor_scalar(self.ss[:, c], self.ss[:, c], 1.0 / DM, EPS, ALU.mult, ALU.add).then_inc(self.mean_made, 1)
        pool.wait_ge(self.mean_made, t + 1)
        nc.gpsimd.tensor_tensor(self.rstd[:, c], self.ss[:, c], self.mhalf[:, 0:1], ALU.pow).then_inc(self.rstd_made, 1)

    def vector_scale(self, dve, t):
        dve.wait_ge(self.rstd_made, t + 1)
        self.K.nc.vector.tensor_scalar(self.xn[:, t, :], self.x[:, t, :], self.rstd[:, t:t + 1], None, ALU.mult)\
            .then_inc(self.scaled, 1)

    def vector_out(self, dve, half, ks=range(NK)):
        nc = self.K.nc
        for k in ks:
            n = half * NK + k
            dve.wait_ge(self.hi_out, n + 1)
            toks = slice(half * HALF, (half + 1) * HALF)
            src, hi = self.K.ps[:, self.bank + n % 4, :], self.hi[:, k, toks].bitcast(F32)
            if self.gain is None:
                i = nc.vector.tensor_tensor(self.lo[:, k, toks], src, hi, ALU.subtract)
            else:
                i = nc.vector.scalar_tensor_tensor(out=self.lo[:, k, toks], in0=src, scalar=self.gain[:, k:k + 1],
                                                   in1=hi, op0=ALU.mult, op1=ALU.subtract)
            i.then_inc(self.lo_out, 1)

    def tensor(self, pe, half):
        pe.wait_ge(self.scaled, 4 * half + 4)
        for k in range(NK):
            n = half * NK + k
            above_zero(pe, self.lo_out, n - 3)
            for t in range(4):
                last = self.K.nc.tensor.transpose(self.K.ps[:, self.bank + n % 4, t * P:(t + 1) * P],
                                                  self.xn[:, 4 * half + t, k * P:(k + 1) * P], self.K.ident[:])
            last.then_inc(self.turned, 1)


def w_in_unit(W, c0, width):
    return W.rearrange("(k p) n -> p k n", p=P)[:, :, c0:c0 + width]


def phase_norm1(K, ctx, A, first_units):
    nc = K.nc
    x = ctx.enter_context(nc.sbuf_tensor("x_in", [P, NT, DM], F32))
    x_landed = [K.sem(f"x_landed{t}") for t in range(NT)]
    c_landed = K.sem("c_landed")
    one = K.sem("mhalf_set")
    N = NormTranspose(K, "n1", x, x, K.h_hi, K.h_lo, K.gains[:, 0, :])
    xv = A["x"][0].rearrange("(t p) d -> p t d", p=P)

    with nc.Block() as block:
        @block.sync
        def _(sp):
            for t in range(NT):
                sp.dma_start(x[:, t, :], xv[:, t, :]).then_inc(x_landed[t], 16)
            for s, (c0, width) in enumerate(first_units):
                load_unit(sp, K, s, 0, w_in_unit(A["w_kv"], c0, width), width)

        @block.scalar
        def _(act):
            a, b = CONST_AT["ident"]
            act.dma_start(K.ident[:], A["consts"][:, a:b]).then_inc(c_landed, 16)
            act.dma_start(K.small[:], A["consts"][:, 0:SMALL_W]).then_inc(c_landed, 16)
            act.dma_start(K.gains[:], A["gains"]).then_inc(c_landed, 16)
            for t in range(NT):
                act.wait_ge(x_landed[t], 16)
                N.scalar_stats(act, t)
            act.wait_ge(c_landed, 48)
            N.scalar_out(act, 0)
            split_hi(act, K, 0, 0, 0, 1024)
            N.scalar_out(act, 1)

        @block.gpsimd
        def _(pool):
            nc.gpsimd.memset(K.mhalf[:, 0:4], -0.5).then_inc(one, 1)
            nc.gpsimd.memset(K.mhalf[:, 4:16], -1.0).then_inc(one, 1)
            pool.wait_ge(one, 2)
            for t in range(NT):
                N.pool_rstd(pool, t)

        @block.vector
        def _(dve):
            for t in range(4):
                N.vector_scale(dve, t)
            dve.wait_ge(c_landed, 48)
            for t in range(4):
                N.vector_out(dve, 0, range(2 * t, 2 * t + 2))
                N.vector_scale(dve, 4 + t)
            split_lo(dve, K, 0, 0, 1024)
            N.vector_out(dve, 1)

        @block.tensor
        def _(pe):
            pe.wait_ge(c_landed, 48)
            for half in range(2):
                N.tensor(pe, half)


KV_UNITS = [
    [(0, DK, C_KC, "kc", 0, 0), (DK, P - DK, C_KC + DK + DV, "kc", 1, DV)],
    [(0, DV, C_KC + DK, "kc", 1, 0), (DV, 3 * NH, C_NGATE, "gate", 0, 0)],
    [(0, P, C_VC, "vc", 0, 0)],
    [(0, P, C_VS, "vs", 0, 0)],
    [(0, P, C_VW, "vw", 0, 0)],
    [(0, DK, C_KS, "k0", 0, 0), (DK, P - DK, C_KW + DV, "k0", 1, DV)],
    [(0, DV, C_KW, "k0", 1, 0), (DV, DV, C_KS + DK, "k1", 0, 0)],
    [(0, DK, C_KW + DK, "k1", 1, 0), (DK, P - DK, C_KS + DK + DV, "k1", 0, DV)],
]


def kv_columns():
    columns = []
    for unit in KV_UNITS:
        mine = [c for piece in unit for c in range(piece[2], piece[2] + piece[1])]
        columns += mine + [mine[-1]] * (P - len(mine))
    return columns


def compress_sources(K, C):
    return ([K.mix[0:DK, 2 * i:2 * i + 2, :].rearrange("p g (n l) -> p g n l", l=CMP_STRIDE) for i in range(2)],
            [C.vtmp[:, i, :].rearrange("p (n l) -> p n l", l=CMP_STRIDE) for i in range(2)])


def phase_kv(K, ctx, A, C, next_units):
    nc = K.nc
    units = KV_UNITS
    tmp = [ctx.enter_context(nc.sbuf_tensor(f"kv_tmp{i}", [P, SEQ], F32)) for i in range(2)]
    sem = K.sem
    half0 = [sem(f"kv_half0_{s}") for s in range(2)]
    out = [[sem(f"kv_out{s}{h}") for h in range(2)] for s in range(2)]
    turned, turned_out = sem("kv_turned"), sem("kv_turned_out")
    masked = sem("kv_gate_out")
    turns = [u for u, unit in enumerate(units) if unit[-1][3] in ("gate", "vs", "vw")]
    copies = lambda u: sum(len(units[v]) for v in range(u % 2, u + 1, 2))
    place = {"kc": C.kc, "vc": C.vc[:].unsqueeze(1), "k0": C.kfirst, "k1": C.kraw}
    half_ready = lambda e, u, h: e.wait_ge(half0[u % 2] if h == 0 else K.w_used[u % 2], u // 2 + 1)
    cmp_loaded = sem("cmp_weights_loaded")
    w1k, w1v, w2k, w2v, pek, pev = C.cmp_weights
    ksrc, vsrc = compress_sources(K, C)
    summed = sem("cmp_sources_summed")
    SUMS_AT = 4

    with nc.Block() as block:
        @block.gpsimd
        def _(pool):
            pool.dma_start(w1k[:], A["cmp_w1_k"][0].rearrange("(l d) j -> d l j", d=DK)).then_inc(cmp_loaded, 16)
            for g in range(NG):
                rows = slice(g * DV, (g + 1) * DV)
                pool.dma_start(w1v[rows], A["cmp_w1_v"][0].rearrange("(l d) j -> d l j", d=DV)).then_inc(cmp_loaded, 16)
                pool.dma_start(pev[rows], A["pe_v"]).then_inc(cmp_loaded, 16)
            pool.dma_start(pek[:], A["pe_k"]).then_inc(cmp_loaded, 16)
            pool.dma_start(w2k[:], A["cmp_w2_k"][0]).then_inc(cmp_loaded, 16)
            pool.dma_start(w2v[:], A["cmp_w2_v"][0]).then_inc(cmp_loaded, 16)
            pool.wait_ge(cmp_loaded, 16 * 8)

        @block.sync
        def _(sp):
            for u in range(2, len(units)):
                load_unit(sp, K, u % 2, u // 2, w_in_unit(A["w_kv"], u * P, P), P)
            for s, (c0, width) in enumerate(next_units):
                load_unit(sp, K, s, len(units) // 2, w_in_unit(A["w_in"][0], c0, width), width)

        @block.scalar
        def _(act):
            for u, unit in enumerate(units):
                if u + 1 < len(units):
                    split_hi(act, K, (u + 1) % 2, (u + 1) // 2, (u + 1) // 2, 1024)
                s = u % 2
                for h in range(2):
                    half_ready(act, u, h)
                    toks = slice(h * HALF, (h + 1) * HALF)
                    for row, n, c0, kind, which, at in unit:
                        if kind in place:
                            dst = place[kind][at:at + n, which, toks]
                            nc.scalar.activation(dst, K.ps[row:row + n, 2 * s + h, :], ACT.Copy).then_inc(out[s][h], 1)
                        else:
                            i = turns.index(u)
                            above_zero(act, turned, 2 * (i - 1))
                            nc.scalar.activation(tmp[i % 2][:, toks], K.ps[:, 2 * s + h, :],
                                                 ACT.Sigmoid if kind == "gate" else ACT.Copy).then_inc(out[s][h], 1)

        @block.vector
        def _(dve):
            def turn_out(u):
                row, which, i = units[u][-1][0], units[u][-1][3], turns.index(u)
                for h in range(2):
                    dve.wait_ge(turned, 2 * i + h + 1)
                    src = K.ps[:, 4 + 2 * (i % 2) + h, :].rearrange("p (t c) -> p t c", t=4)
                    if which == "gate":
                        nc.vector.tensor_copy(C.gate[:, 4 * h:4 * h + 4, :], src[:, :, row:row + 3 * NH]).then_inc(turned_out, 1)
                    else:
                        dst = C.vs if which == "vs" else C.vw
                        nc.vector.tensor_copy(dst[:, 4 * h:4 * h + 4, :], src).then_inc(turned_out, 1)

            for u in range(len(units)):
                if u + 1 < len(units):
                    split_lo(dve, K, (u + 1) % 2, (u + 1) // 2, 1024)
                if u - 1 in turns:
                    turn_out(u - 1)
                if u == SUMS_AT:
                    dve.wait_ge(cmp_loaded, 16 * 8)
                    for s in range(2):
                        for h in range(2):
                            dve.wait_ge(out[s][h], copies(2 - s))
                    for i in range(2):
                        part = slice(i * CMP_STRIDE, (i + 1) * CMP_STRIDE)
                        for g in range(NG):
                            nc.vector.tensor_tensor(ksrc[i][:, g], C.kc[:, g, :].rearrange("p (n l) -> p n l", l=CMP_STRIDE),
                                                    pek[:, part].unsqueeze(1).to_broadcast([DK, NB, CMP_STRIDE]), ALU.add)\
                                .then_inc(summed, 1)
                        nc.vector.tensor_tensor(vsrc[i], C.vc[:].rearrange("p (n l) -> p n l", l=CMP_STRIDE),
                                                pev[:, part].unsqueeze(1).to_broadcast([P, NB, CMP_STRIDE]), ALU.add)\
                            .then_inc(summed, 1)
            dve.wait_ge(summed, 6)
            dve.wait_ge(turned_out, 2 * len(turns))
            first = C.gate[:, 0, 0:NH]
            nc.vector.tensor_scalar(first, first, K.const("valid"), None, ALU.mult).then_inc(masked, 1)
            dve.wait_ge(masked, 1)

        @block.tensor
        def _(pe):
            for u in range(len(units)):
                s = u % 2
                pe.wait_ge(K.lo_made[s], u // 2 + 1)
                for h in range(2):
                    above_zero(pe, out[s][h], copies(u - 2))
                    project_half(K, 2 * s + h, s, P, h, K.h_hi, K.h_lo)\
                        .then_inc(half0[s] if h == 0 else K.w_used[s], 1)
                if u - 1 in turns:
                    i = turns.index(u - 1)
                    above_zero(pe, turned_out, 2 * (i - 1))
                    for h in range(2):
                        pe.wait_ge(out[(u - 1) % 2][h], copies(u - 1))
                        for t in range(4):
                            last = nc.tensor.transpose(K.ps[:, 4 + 2 * (i % 2) + h, t * P:(t + 1) * P],
                                                       tmp[i % 2][:, (4 * h + t) * P:(4 * h + t + 1) * P], K.ident[:])
                        last.then_inc(turned, 1)


def phase_compress(K, ctx, A, C):
    nc = K.nc
    sb = lambda n, s, d=F32: ctx.enter_context(nc.sbuf_tensor(n, s, d))
    sem = K.sem
    w1k, w1v, w2k, w2v, pek, pev = C.cmp_weights
    ksrc, vsrc = compress_sources(K, C)
    gk, gv = sb("gelu_k", [DK, NG * NCMP]), sb("gelu_v", [DV, NG * NCMP])
    k_high = sem("cw_k_high")
    hidden, active = sem("cw_hidden"), sem("cw_active")
    mapped, zeroed, high, written = sem("cw_mapped"), sem("cw_zeroed"), sem("cw_high"), sem("cw_written")
    hid_k = K.ps[0:DK, 0, 0:NG * NCMP]
    hid_v = [K.ps[0:DV, 1, 0:NCMP], K.ps[0:DV, 4, 0:NCMP]]
    out_k, out_v = K.ps[0:DK, 2, 0:NG * NCMP], K.ps[0:NCMP, 3, 0:NG * DV]

    with nc.Block() as block:
        @block.gpsimd
        def _(pool):
            nc.gpsimd.memset(C.kc_hi[:].bitcast(F32), 0.0).then_inc(zeroed, 1)
            nc.gpsimd.memset(C.kc_lo[:].bitcast(F32), 0.0).then_inc(zeroed, 1)
            nc.gpsimd.memset(C.vcmp[:].bitcast(F32), 0.0).then_inc(zeroed, 1)

        @block.vector
        def _(dve):
            dve.wait_ge(k_high, 1)
            nc.vector.tensor_tensor(C.k_lo[:], C.kfirst[:], C.k_hi[:].bitcast(F32), ALU.subtract)\
                .then_inc(written, 1)
            dve.wait_ge(mapped, 1)
            dve.wait_ge(high, 1)
            nc.vector.tensor_tensor(C.kc_lo[:, :, 0:NCMP], out_k.rearrange("p (g n) -> p g n", g=NG),
                                    C.kc_hi[:, :, 0:NCMP].bitcast(F32), ALU.subtract).then_inc(written, 1)
            dve.wait_ge(mapped, 2)
            dve.wait_ge(high, 2)
            nc.vector.tensor_tensor(C.vcmp[0:NCMP, :, DV:2 * DV], out_v.rearrange("p (g n) -> p g n", g=NG),
                                    C.vcmp[0:NCMP, :, 0:DV].bitcast(F32), ALU.subtract).then_inc(written, 1)

        @block.tensor
        def _(pe):
            for l in range(CMP_LEN):
                i, c = divmod(l, CMP_STRIDE)
                last = nc.tensor.matmul(hid_k.rearrange("p (g n) -> p g n", g=NG), w1k[:, l, :],
                                        ksrc[i][:, :, i:i + NCMP, c], start=(l == 0), stop=(l == CMP_LEN - 1))
            last.then_inc(hidden, 1)
            for g in range(NG):
                rows = slice(g * DV, (g + 1) * DV)
                for l in range(CMP_LEN):
                    i, c = divmod(l, CMP_STRIDE)
                    last = nc.tensor.matmul(hid_v[g], w1v[rows, l, :],
                                            vsrc[i][rows, i:i + NCMP, c], start=(l == 0), stop=(l == CMP_LEN - 1))
            last.then_inc(hidden, 1)
            pe.wait_ge(active, 1)
            nc.tensor.matmul(out_k, w2k[:], gk[:], start=True, stop=True).then_inc(mapped, 1)
            pe.wait_ge(active, 3)
            for g in range(NG):
                last = nc.tensor.matmul(out_v[:, g * DV:(g + 1) * DV], gv[:, g * NCMP:(g + 1) * NCMP], w2v[:],
                                        start=True, stop=True)
            last.then_inc(mapped, 1)

        @block.scalar
        def _(act):
            nc.scalar.activation(C.k_hi[:], C.kfirst[:], ACT.Copy).then_inc(k_high, 1)
            act.wait_ge(hidden, 1)
            nc.scalar.activation(gk[:], hid_k, ACT.Gelu_apprx_tanh).then_inc(active, 1)
            act.wait_ge(hidden, 2)
            for g in range(NG):
                nc.scalar.activation(gv[:, g * NCMP:(g + 1) * NCMP], hid_v[g], ACT.Gelu_apprx_tanh).then_inc(active, 1)
            act.wait_ge(mapped, 1)
            act.wait_ge(zeroed, 3)
            nc.scalar.activation(C.kc_hi[:, :, 0:NCMP], out_k.rearrange("p (g n) -> p g n", g=NG), ACT.Copy)\
                .then_inc(high, 1)
            act.wait_ge(mapped, 2)
            nc.scalar.activation(C.vcmp[0:NCMP, :, 0:DV], out_v.rearrange("p (g n) -> p g n", g=NG), ACT.Copy)\
                .then_inc(high, 1)


def laid_out(inputs):
    column = lambda a: np.asarray(a)[0].reshape(NK, P).T
    gains = np.stack([column(inputs[n]) for n in ("norm_mix_pre", "norm_ffn_pre", "ret_gn_g")], axis=1)
    w_kv = np.ascontiguousarray(np.asarray(inputs["w_in"])[0][:, kv_columns()])
    return {"consts": shape_constants(), "w_kv": w_kv, "gains": np.ascontiguousarray(gains),
            "pe_k": np.ascontiguousarray(np.asarray(inputs["cmp_pe_k"])[0].T),
            "pe_v": np.ascontiguousarray(np.asarray(inputs["cmp_pe_v"])[0].T)}



CMP, SEL, WIN = 0, 1, 2
E_WIN, E_CMP, E_SEL = 0, WINDOW + P, WINDOW + 2 * P
LAST_PAIR = NH // 2 - 1
GP = NH // NG // 2


def key_blocks(i):
    first = max(0, i - WB)
    return ([(WIN, b, E_WIN + (b - first) * P) for b in range(first, i + 1)] + [(CMP, 0, E_CMP)]
            + [(SEL, b, E_SEL + b * P) for b in range(i + 1)])


def batches(i):
    blocks = key_blocks(i)
    return [blocks[n:n + 2] for n in range(0, len(blocks), 2)]


BEFORE = [sum(len(batches(i)) for i in range(s)) for s in range(NT + 1)]
PER_PAIR = BEFORE[NT]
assert PER_PAIR % 2 == 0
ORDER = """
Q00 T64- A62- H64- T65- A63- H65- Q01 Z70- L64- L65- Z71- Y70- T66- u4 C7- A64- H66- S00 A65- L66- T70- B00
S02 A66- U4 T71- H70- S01 B02 S03 F6- L70- G6- B03 T72- H71- L71- A70- X73- H72- X02 Q02 Y71- L72- X00 A71-
T73- A72- H73- T74- u5 X03 B01 H74- X01 Y00 L73- Q03 L74- T75- A73- Y01 A74- T76- q0 l0 S12 P0 H75- L75- S10
H76- C0 B12 B10 Z00 A75- L76- Z01 h0 U5 S13 T00 S11 B13 X12 H00 X10 B11 T01 A76- X11 S22 Y10 F7- H01 P1 B22
Q10 S20 k0 X13 X22 C1 Z10 S23 G7- Q11 B20 L00 Z11 S21 A00 X20 L01 Y11 T10 H10 A01 B23 B21 T11 L10 X23 F0 Q12
H11 G0 Q13 A10 X21 q1 Y20 Y21 T12 H12 S30 L11 P2 Z20 L12 C2 Z21 B30 S32 A11 A12 S31 T20 l1 X30 T21 F1 B32 Q20
H20 B31 H21 G1 S33 L20 A20 X31 T22 L21 P3 X32 H22 T23 B33 Y30 A21 S42 H23 L22 B42 L23 Z30 S40 B40 C3 Z31 X33
A22 T30 H30 A23 S43 L30 F2 T31 X42 S41 Y31 G2 H31 Y40 X40 Q21 h1 A30 T32 B41 L31 Q22 T33 A31 H32 Q23 B43 X41
L32 H33 X43 k1 T34 L33 P4 A32 S50 Y41 Z40 S52 H34 Z41 U6 L34 q2 T40 A33 H40 B50 A34 B52 T41 S51 L40 F3 S53 H41
G3 L41 X50 X52 C4 l2 T42 B51 A40 T43 H42 L42 A41 Q30 H43 L43 T44 A42 T45 X51 P5 H44 A43 u6 C5 S60 U7 B53 L44
H45 L45 S62 B60 X53 A44 Z50 A45 S61 Y50 Z51 T50 X60 F4 B62 T51 B61 H50 G4 Q31 Q32 L50 S63 H51 X62 X61 A50 Y51
T52 L51 H52 Y60 u7 A51 T53 L52 H53 L53 Q33 B63 T54 P6 A52 Z60 q3 T55 A53 H54 l3 S70 H55 Z61 L54 L55 B70 C6 A54
T60 H60 A55 L60 S72 F5 T61 T62 G5 X63 A60 B72 H61 L61 H62 S71 Y61 S73 A61 B71 X70 T63 L62 X72 H63 L63 X71 B73
P7
"""

SCORES = [(0, WIN), (1, WIN), (0, SEL), (1, SEL)]
Q_UNITS = [(0, 1), (1, 1), (0, 0), (1, 0)]


def entries():
    for word in ORDER.split():
        back = word.endswith("-")
        word = word.rstrip("-")
        yield word[0], int(word[1]), int(word[2:] or 0), back


FILL = (8, 20)


def phase_attention(K, ctx, A, C, n0, next_units, next_half0):
    nc = K.nc
    sb = lambda n, s, d=F32: ctx.enter_context(nc.sbuf_tensor(n, s, d))
    sem = K.sem
    dsel, dwin, dcmp = sb("d_sel", [P, SEQ]), sb("d_win", [P, WINDOW + P]), sb("d_cmp", [P, NB + (NT - 1) * 8])
    q_hi = [sb(f"q_hi{i}", [DK, SEQ], F32R) for i in range(2)]
    q_lo = [sb(f"q_lo{i}", [DK, SEQ], F32R) for i in range(2)]
    v_sel, v_win = sb("v_sel", [P, NT, P], F32R), sb("v_win", [P, NT, P], F32R)
    E = [sb("probs0", [P, 2, E_SEL + SEQ - P]), sb("probs1", [P, 2, E_SEL + SEQ])]
    t_hi, t_lo = sb("probs_t_hi", [P, 2, 512], F32R), sb("probs_t_lo", [P, 2, 512], F32R)
    o_low = sb("o_low", [DV, 2 * P])
    least, total = sb("least", [P, 2, 3, 2]), sb("total", [P, 2, 3, 2])
    inv, weight = sb("inv_total", [P, 2, 3, 2]), sb("weight", [P, 2, 3, 2])
    sel_gate = sb("sel_gate", [P, NT, 2])
    slope, qscale = sb("slope", [P, 2]), sb("q_scale", [P, 4])
    d_landed = sem("d_landed")
    q_half0, q_high, q_out = sem("q_half0"), sem("q_high"), sem("q_out")
    s_win, s_sel = sem("win_scores"), sem("sel_scores")
    b_win, b_sel = sem("win_biased"), sem("sel_biased")
    e_win, e_sel = sem("win_probs"), sem("sel_probs")
    i_win, w_win = sem("win_inv"), sem("win_weights")
    i_sel, g_sel = sem("sel_inv"), sem("sel_gates_set")
    c_win, c_cmp, c_sel = sem("win_scaled"), sem("cmp_scaled"), sem("sel_scaled")
    turned, high, low, added = sem("turned"), sem("turned_high"), sem("turned_low"), sem("values_added")
    o_low_out, folded = sem("o_low_out"), sem("folded")
    slope_set, pair_set, zeroed = sem("slope_set"), sem("pair_set"), sem("pad_zeroed")
    k_high, k_split = sem("group_keys_high"), sem("group_keys_split")
    v_high, v_split = sem("group_values_high"), sem("group_values_split")
    ps_sel = K.ps[:, 0:2, :].rearrange("p b n -> p (b n)")
    ps_win = K.ps[:, 2:4, :].rearrange("p b n -> p (b n)")
    O, PQ = K.ps[:, 6, 0:2 * P], K.ps[0:DK, 7, :]
    kx_hi = [w[0:DK, NK * DK:NK * DK + P + NB] for w in K.w_hi]
    kx_lo = [w[0:DK, NK * DK:NK * DK + P + NB] for w in K.w_lo]
    x_high, x_low = sem("own_keys_high"), sem("own_keys_low")
    wv = A["w_in"][0].rearrange("(k p) n -> p k n", p=P)
    gates = C.gate[:].rearrange("p i (b h) -> p i b h", b=3)
    both = lambda ap: ap.rearrange("p t (g e) -> p t g e", g=NG)

    def is_last(j):
        return isinstance(j, int) and j == LAST_PAIR

    def own_keys_free(engine, pair, t):
        above_zero(engine, s_win, at(pair, 2 * NT, 2 * (t - 2) + 2 if t >= WB + 2 else 2 * (t + 2) + 2 - 2 * NT))

    def pairs(engine, g, take, between=None):
        def body(j, first=False):
            for step, t, n, back in entries():
                if not (back and first):
                    one(step, t, n, j - 1 if back else j)

        def one(step, t, n, pair):
            if not (is_last(pair) and ((step in "Qql" and t >= 2) or step in "hk")):
                take(step, t, n, pair)

        body(GP * g, True)
        if g == NG - 1:
            with engine.Fori(GP * g + 1, LAST_PAIR) as j:
                body(j)
            body(LAST_PAIR)
        else:
            with engine.Fori(GP * g + 1, GP * g + GP) as j:
                body(j)
        late = [entry for entry in entries() if entry[3]]
        for m, (step, t, n, back) in enumerate(late):
            if between is not None:
                between(g, m)
            one(step, t, n, GP * (g + 1) - 1)

    def at(j, per, n):
        return j * per + n

    def batch_no(pair, step, k, extra=0):
        return at(pair, PER_PAIR, BEFORE[step] + k + extra)

    def sizes(i):
        return (min(i, WB) + 1) * P, (i + 1) * P

    with nc.Block() as block:
        @block.sync
        def _(sp):
            for name, dst in (("dsel", dsel), ("dwin", dwin), ("dcmp", dcmp)):
                a, b = CONST_AT[name]
                sp.dma_start(dst[:], A["consts"][:, a:b]).then_inc(d_landed, 16)

            with nc.sync.Fori(0, LAST_PAIR) as j:
                for s in range(2):
                    load_unit(sp, K, s, j + (n0 + 1), wv[:, :, bass.ds(j * (2 * DK) + (C_NQ + (2 + s) * DK), DK)], DK)
            for s, (c0, width) in enumerate(next_units):
                load_unit(sp, K, s, n0 + NH // 2, w_in_unit(A["w_in"][0], c0, width), width)

        @block.scalar
        def _(act):
            def q_high_part(hh, h, done, scale):
                act.wait_ge(q_half0 if h == 0 else K.w_used[hh], done)
                nc.scalar.activation(q_hi[hh][:, h * HALF:(h + 1) * HALF], PQ, ACT.Copy, scale=scale).then_inc(q_high, 1)

            def exp(j, s, c):
                hh, br = SCORES[c]
                act.wait_ge(b_win if br == WIN else b_sel, at(j, 2 * NT, 2 * s + hh + 1))
                w, wide = sizes(s)
                e = E[s % 2]
                for b, a, size in (((WIN, E_WIN, w), (CMP, E_CMP, NB)) if br == WIN else ((SEL, E_SEL, wide),)):
                    m = nc.scalar.activation(e[:, hh, a:a + size], e[:, hh, a:a + size], ACT.Exp,
                                             bias=least[:, s % 2, b, hh:hh + 1], scale=-1.0,
                                             accum_out=total[:, s % 2, b, hh:hh + 1])
                m.then_inc(e_win if br == WIN else e_sel, 1)

            def scale(j, s, hh):
                act.wait_ge(w_win, at(j, NT, s + 1))
                e = E[s % 2][:, hh, E_WIN:E_WIN + sizes(s)[0]]
                nc.scalar.activation(e, e, ACT.Copy, scale=weight[:, s % 2, WIN, hh:hh + 1]).then_inc(c_win, 1)

            def copy_high(pair, step, k):
                w = len(batches(step)[k]) * 2 * P
                slot = (BEFORE[step] + k) % 2
                act.wait_ge(turned, batch_no(pair, step, k, 1))
                above_zero(act, added, batch_no(pair, step, k, -1))
                nc.scalar.activation(t_hi[:, slot, 0:w], K.ps[:, 4 + slot, 0:w], ACT.Copy).then_inc(high, 1)

            def fold(pair, step):
                act.wait_ge(added, batch_no(pair, step + 1, 0))
                above_zero(act, folded, at(pair, 2 * NT, 2 * step))
                nc.scalar.activation(o_low[:], O[DV:2 * DV, :], ACT.Copy).then_inc(o_low_out, 1)

            def take(step, t, n, pair):
                if step == "X":
                    exp(pair, t, n)
                elif step == "Z":
                    scale(pair, t, n)
                elif step == "H":
                    copy_high(pair, t, n)
                elif step == "F":
                    fold(pair, t)
                elif step == "q":
                    hh, h = Q_UNITS[t]
                    act.wait_ge(pair_set, at(pair, 1, 1))
                    q_high_part(hh, h, at(pair, 2, 3 + hh) if h == 0 else at(pair, 1, n0 + 1),
                                qscale[0:DK, 2 * (1 - h) + hh:2 * (1 - h) + hh + 1])
                elif step == "U":
                    own_keys_free(act, pair, t)
                    nc.scalar.activation(kx_hi[t % 2][:, 0:P], C.k_hi[:, 1, t * P:(t + 1) * P].bitcast(F32), ACT.Copy)\
                        .then_inc(x_high, 1)
                elif step == "h":
                    split_hi(act, K, t, at(pair, 1, n0 + 1), at(pair, 1, n0 + 1), NK * DK)

            def own_compressed(g):
                for slot in range(2):
                    nc.scalar.activation(kx_hi[slot][:, P:], C.kc_hi[:, g, :].bitcast(F32), ACT.Copy).then_inc(k_high, 1)

            def before_next(g, m):
                if g == NG - 1 and m == FILL[1]:
                    split_hi(act, K, 1, n0 + NH // 2, n0 + NH // 2, 1024)
                if m > 0:
                    return
                act.wait_ge(s_win, (g + 1) * GP * 2 * NT)
                act.wait_ge(s_sel, (g + 1) * GP * 2 * NT)
                if g == NG - 1:
                    split_hi(act, K, 0, n0 + NH // 2, n0 + NH // 2, 1024)
                else:
                    nc.scalar.activation(C.k_hi[:], C.kraw, ACT.Copy).then_inc(k_high, 1)
                    own_compressed(g + 1)
                    act.wait_ge(k_high, 5)

            for g in range(NG):
                if g == 0:
                    for s in range(2):
                        split_hi(act, K, s, n0, n0, NK * DK)
                    own_compressed(0)
                above_zero(act, added, GP * g * PER_PAIR)
                for dst, src in ((v_sel, C.vs), (v_win, C.vw)):
                    nc.scalar.activation(dst[:, :, 0:DV], both(src)[:, :, g, :], ACT.Copy).then_inc(v_high, 1)
                if g == 0:
                    act.wait_ge(zeroed, 3)
                    for hh in range(2):
                        q_high_part(hh, 0, 1 + hh, K.const("qscale")[0:DK, hh:hh + 1])
                pairs(nc.scalar, g, take, before_next)

        @block.gpsimd
        def _(pool):
            for e in E:
                nc.gpsimd.memset(e[:, :, E_CMP + NB:E_SEL], 0.0).then_inc(zeroed, 1)
            nc.gpsimd.memset(qscale[:], 0.0).then_inc(zeroed, 1)
            pool.wait_ge(zeroed, 3)

            def take(step, t, n, pair):
                slot = t % 2
                if step == "q" and t == 0:
                    above_zero(pool, q_out, at(pair, 4, 2))
                    w = 2 if is_last(pair) else 4
                    nc.gpsimd.tensor_copy(qscale[:, 0:w], K.const("qscale")[:, bass.ds(at(pair, 2, 0), w)])\
                        .then_inc(pair_set, 1)
                elif step == "Y" and t == 0 and n == 0:
                    above_zero(pool, c_sel, at(pair, 2 * NT, 0))
                    nc.gpsimd.tensor_copy(sel_gate[:], gates[:, :, SEL, bass.ds(at(pair, 2, 0), 2)]).then_inc(g_sel, 1)
                elif step == "P":
                    pool.wait_ge(e_win, at(pair, 2 * NT, 2 * t + 2))
                    nc.gpsimd.tensor_tensor(inv[:, slot, CMP::2, :], total[:, slot, CMP::2, :],
                                            K.mhalf[:, 4:8].rearrange("p (b h) -> p b h", h=2), ALU.pow).then_inc(i_win, 1)
                    pool.wait_ge(i_win, at(pair, NT, t + 1))
                    nc.gpsimd.tensor_tensor(weight[:, slot, CMP::2, :], inv[:, slot, CMP::2, :],
                                            gates[:, t, CMP::2, bass.ds(at(pair, 2, 0), 2)], ALU.mult).then_inc(w_win, 1)
                elif step == "C":
                    pool.wait_ge(w_win, at(pair, NT, t + 1))
                    e = E[slot][:, :, E_CMP:E_CMP + NB]
                    nc.gpsimd.tensor_tensor(e, e, weight[:, slot, CMP, :].unsqueeze(2).to_broadcast([P, 2, NB]), ALU.mult)\
                        .then_inc(c_cmp, 1)

            for g in range(NG):
                pairs(nc.gpsimd, g, take)

        @block.vector
        def _(dve):
            def q_low_part(hh, h, count, scale):
                dve.wait_ge(q_high, count)
                toks = slice(h * HALF, (h + 1) * HALF)
                nc.vector.scalar_tensor_tensor(out=q_lo[hh][:, toks], in0=PQ, scalar=scale, in1=q_hi[hh][:, toks].bitcast(F32),
                                               op0=ALU.mult, op1=ALU.subtract).then_inc(q_out, 1)

            def bias(j, s, c):
                hh, br = SCORES[c]
                w, wide = sizes(s)
                dve.wait_ge(s_win if br == WIN else s_sel, at(j, 2 * NT, 2 * s + hh + 1))
                nc.vector.nop(nofuse=True)
                parts = (((WIN, E_WIN, w, ps_win[:, 0:w], dwin[:, WINDOW + P - w:]),
                          (CMP, E_CMP, NB, ps_win[:, WINDOW + P:WINDOW + P + NB], dcmp[:, (NT - 1 - s) * 8:(NT - 1 - s) * 8 + NB]))
                         if br == WIN else ((SEL, E_SEL, wide, ps_sel[:, 0:wide], dsel[:, SEQ - wide:]),))
                for b, a, size, src, d in parts:
                    m = nc.vector.tensor_tensor_reduce(E[s % 2][:, hh, a:a + size], src, d, slope[:, hh:hh + 1], 3e38,
                                                       ALU.add, ALU.min, least[:, s % 2, b, hh:hh + 1])
                m.then_inc(b_win if br == WIN else b_sel, 1)

            def scale(pair, step, hh):
                dve.wait_ge(e_sel, at(pair, 2 * NT, 2 * step + hh + 1))
                nc.vector.reciprocal(inv[:, step % 2, SEL, hh:hh + 1], total[:, step % 2, SEL, hh:hh + 1]).then_inc(i_sel, 1)
                dve.wait_ge(i_sel, at(pair, 2 * NT, 2 * step + hh + 1))
                if step == 0 and hh == 0:
                    dve.wait_ge(g_sel, at(pair, 1, 1))
                e = E[step % 2][:, hh, E_SEL:E_SEL + sizes(step)[1]]
                nc.vector.tensor_scalar(e, e, inv[:, step % 2, SEL, hh:hh + 1], sel_gate[:, step, hh:hh + 1],
                                        ALU.mult, ALU.mult).then_inc(c_sel, 1)

            def copy_low(pair, step, k):
                w = len(batches(step)[k]) * 2 * P
                slot = (BEFORE[step] + k) % 2
                dve.wait_ge(high, batch_no(pair, step, k, 1))
                nc.vector.tensor_tensor(t_lo[:, slot, 0:w], K.ps[:, 4 + slot, 0:w], t_hi[:, slot, 0:w].bitcast(F32),
                                        ALU.subtract).then_inc(low, 1)

            def fold(pair, step):
                dve.wait_ge(o_low_out, at(pair, NT, step + 1))
                for hh in range(2):
                    cols = slice(hh * P, (hh + 1) * P)
                    out = K.mix[hh * DV:(hh + 1) * DV, bass.ds(pair, 1), step * P:(step + 1) * P].rearrange("p a n -> p (a n)")
                    nc.vector.tensor_tensor(out, O[0:DV, cols], o_low[:, cols], ALU.add).then_inc(folded, 1)

            def take(step, t, n, pair):
                if step == "B":
                    if t == 0 and n == 0:
                        if not (isinstance(pair, int) and pair == 0):
                            dve.wait_ge(b_sel, at(pair, 2 * NT, 0))
                            nc.vector.tensor_scalar(slope[:], slope[:], 0.5, None, ALU.mult).then_inc(slope_set, 1)
                        dve.wait_ge(slope_set, at(pair, 1, 1))
                    bias(pair, t, n)
                elif step == "Y":
                    scale(pair, t, n)
                elif step == "L":
                    copy_low(pair, t, n)
                elif step == "G":
                    fold(pair, t)
                elif step == "l":
                    hh, h = Q_UNITS[t]
                    q_low_part(hh, h, at(pair, 4, 3 + t), qscale[0:DK, 2 * (1 - h) + hh:2 * (1 - h) + hh + 1])
                elif step == "u":
                    own_keys_free(dve, pair, t)
                    nc.vector.tensor_copy(kx_lo[t % 2][:, 0:P], C.k_lo[:, 1, t * P:(t + 1) * P].bitcast(F32)).then_inc(x_low, 1)
                elif step == "k":
                    split_lo(dve, K, t, at(pair, 1, n0 + 1), NK * DK)

            def own_compressed(g):
                for slot in range(2):
                    nc.vector.tensor_copy(kx_lo[slot][:, P:], C.kc_lo[:, g, :].bitcast(F32)).then_inc(k_split, 1)

            def before_next(g, m):
                if g == NG - 1 and m == FILL[1]:
                    split_lo(dve, K, 1, n0 + NH // 2, 1024)
                if m > 0:
                    return
                if g == NG - 1:
                    split_lo(dve, K, 0, n0 + NH // 2, 1024)
                else:
                    dve.wait_ge(k_high, 3)
                    nc.vector.tensor_tensor(C.k_lo[:], C.kraw, C.k_hi[:].bitcast(F32), ALU.subtract).then_inc(k_split, 1)
                    own_compressed(g + 1)
                    dve.wait_ge(k_split, 5)

            nc.vector.tensor_copy(slope[:], K.const("slope")[:, 0:2]).then_inc(slope_set, 1)
            for g in range(NG):
                if g == 0:
                    for s in range(2):
                        split_lo(dve, K, s, n0, NK * DK)
                    own_compressed(0)
                for n, (dst, src) in enumerate(((v_sel, C.vs), (v_win, C.vw))):
                    dve.wait_ge(v_high, 2 * g + n + 1)
                    nc.vector.tensor_tensor(dst[:, :, DV:2 * DV], both(src)[:, :, g, :], dst[:, :, 0:DV].bitcast(F32),
                                            ALU.subtract).then_inc(v_split, 1)
                if g == 0:
                    for hh in range(2):
                        q_low_part(hh, 0, 1 + hh, K.const("qscale")[0:DK, hh:hh + 1])
                    dve.wait_ge(d_landed, 48)
                pairs(nc.vector, g, take, before_next)

        @block.tensor
        def _(pe):
            def project(hh, h, c, n, out_before):
                if c == 0:
                    pe.wait_ge(K.lo_made[hh], n)
                    above_zero(pe, q_out, out_before)
                for k in range(2 * c, 2 * c + 2):
                    cols, toks = slice(k * DK, (k + 1) * DK), slice(h * HALF, (h + 1) * HALF)
                    m = mm3(nc, PQ, (K.w_hi[hh][:, cols], K.w_lo[hh][:, cols]), (K.h_hi[:, k, toks], K.h_lo[:, k, toks]),
                            k == 0, k == NK - 1)
                if c == 3:
                    m.then_inc(q_half0 if h == 0 else K.w_used[hh], 1)

            def score(j, s, c, g):
                hh, br = SCORES[c]
                w, wide = sizes(s)
                mine = (q_hi[hh][:, s * P:(s + 1) * P], q_lo[hh][:, s * P:(s + 1) * P])
                above_zero(pe, b_win if br == WIN else b_sel, at(j, 2 * NT, 2 * s + hh))
                if br == WIN:
                    full = s >= WB
                    keys = slice((s + 1) * P - w, s * P if full else (s + 1) * P)
                    mm3(nc, ps_win[:, 0:min(w, WINDOW)], mine, (C.k_hi[:, 1, keys], C.k_lo[:, 1, keys]), True, True)
                    if full:
                        if hh == 0:
                            pe.wait_ge(x_high, at(j, NT - WB, s - WB + 1))
                            pe.wait_ge(x_low, at(j, NT - WB, s - WB + 1))
                        m = mm3(nc, ps_win[:, WINDOW:WINDOW + P + NB], mine, (kx_hi[s % 2], kx_lo[s % 2]), True, True)
                    else:
                        m = mm3(nc, ps_win[:, WINDOW + P:WINDOW + P + NB], mine, (C.kc_hi[:, g, :], C.kc_lo[:, g, :]), True, True)
                    m.then_inc(s_win, 1)
                else:
                    for a in range(0, wide, 512):
                        b = min(wide, a + 512)
                        m = mm3(nc, ps_sel[:, a:b], mine, (C.k_hi[:, 0, a:b], C.k_lo[:, 0, a:b]), True, True)
                    m.then_inc(s_sel, 1)

            def turn(pair, step, k):
                blocks, slot = batches(step)[k], (BEFORE[step] + k) % 2
                seen = {b[0] for part in batches(step)[:k] for b in part}
                new = {b[0] for b in blocks} - seen
                if WIN in new:
                    pe.wait_ge(c_win, at(pair, 2 * NT, 2 * step + 2))
                if CMP in new:
                    pe.wait_ge(c_cmp, at(pair, NT, step + 1))
                if SEL in new:
                    pe.wait_ge(c_sel, at(pair, 2 * NT, 2 * step + 2))
                above_zero(pe, low, batch_no(pair, step, k, -1))
                for c, (br, b, a) in enumerate(blocks):
                    for hh in range(2):
                        col = (2 * c + hh) * P
                        m = nc.tensor.transpose(K.ps[:, 4 + slot, col:col + P], E[step % 2][:, hh, a:a + P], K.ident[:])
                m.then_inc(turned, 1)

            def add(pair, step, k, g):
                blocks, slot = batches(step)[k], (BEFORE[step] + k) % 2
                pe.wait_ge(low, batch_no(pair, step, k, 1))
                if isinstance(pair, int) and pair == g * GP and step == k == 0:
                    pe.wait_ge(v_split, 2 * g + 2)
                if k == 0:
                    above_zero(pe, folded, at(pair, 2 * NT, 2 * step))
                for c, (br, b, a) in enumerate(blocks):
                    v = C.vcmp[:, g, :] if br == CMP else (v_sel if br == SEL else v_win)[:, b, :]
                    cols = slice(c * 2 * P, (c + 1) * 2 * P)
                    nc.tensor.matmul(O, v, t_hi[:, slot, cols], start=(k == 0 and c == 0), stop=False)
                    m = nc.tensor.matmul(O, v, t_lo[:, slot, cols], start=False,
                                         stop=(k == len(batches(step)) - 1 and c == len(blocks) - 1))
                m.then_inc(added, 1)

            def before_next(g, m):
                for h in range(2):
                    if g == NG - 1 and m == FILL[h]:
                        pe.wait_ge(K.lo_made[0], n0 + NH // 2 + 1)
                        pe.wait_ge(b_sel, LAST_PAIR * 2 * NT + 2 * NT)
                        project_half(K, h, 0, P, h, K.h_hi, K.h_lo)\
                            .then_inc(next_half0 if h == 0 else K.w_used[0], 1)

            for g in range(NG):
                def take(step, t, n, pair, g=g):
                    if step == "S":
                        if t % (NT // 2) == 0 and n == 0:
                            pe.wait_ge(q_out, at(pair, 4, 4 if t else 2))
                        score(pair, t, n, g)
                    elif step == "T":
                        turn(pair, t, n)
                    elif step == "A":
                        add(pair, t, n, g)
                    elif step == "Q":
                        hh, h = Q_UNITS[t]
                        project(hh, h, n, at(pair, 1, n0 + (2 if h == 0 else 1)), at(pair, 4, 2 + t))

                if g == 0:
                    for hh in range(2):
                        for c in range(4):
                            project(hh, 0, c, n0 + 1, hh)
                pe.wait_ge(k_high, 2 + 3 * g)
                pe.wait_ge(k_split, 2 + 3 * g)
                pairs(nc.tensor, g, take, before_next)



def half_stream(K, tag):
    return [K.sem(f"{tag}_half0_{s}") for s in range(2)], bank_out(K, tag)


def bank_out(K, tag):
    return [[K.sem(f"{tag}_out{s}{h}") for h in range(2)] for s in range(2)]


def phase_gate_nsa(K, ctx, A, n0, half0, next_units):
    nc = K.nc
    out = bank_out(K, "gb")
    sig = [[ctx.enter_context(nc.sbuf_tensor(f"gb_sig{s}{h}", [P, HALF], F32)) for h in range(2)] for s in range(2)]
    gated = [[K.sem(f"gb_gated{s}{h}") for h in range(2)] for s in range(2)]
    wv = A["w_in"][0].rearrange("(k p) n -> p k n", p=P)
    pairs = NK // 2

    def per_pair(engine, body):
        body(0)
        with engine.Fori(1, pairs) as r:
            body(r)

    with nc.Block() as block:
        @block.sync
        def _(sp):
            with nc.sync.Fori(0, pairs - 1) as r:
                for s in range(2):
                    load_unit(sp, K, s, r + (n0 + 1), wv[:, :, bass.ds(r * (2 * P) + (C_MB + (2 + s) * P), P)], P)
            for s, (c0, width) in enumerate(next_units):
                load_unit(sp, K, s, n0 + pairs, w_in_unit(A["w_in"][0], c0, width), width)

        @block.scalar
        def _(act):
            def body(r):
                for s in range(2):
                    if s or not isinstance(r, int):
                        split_hi(act, K, 1 - s, r + (n0 + s), r + (n0 + s), 1024)
                    for h in range(2):
                        act.wait_ge(half0[s] if h == 0 else K.w_used[s], r + (1 if h == 0 else n0 + 1))
                        above_zero(act, gated[s][h], r)
                        nc.scalar.activation(sig[s][h][:], K.ps[:, 2 * s + h, :], ACT.Sigmoid).then_inc(out[s][h], 1)
            per_pair(nc.scalar, body)

        @block.vector
        def _(dve):
            def body(r):
                for s in range(2):
                    if s or not isinstance(r, int):
                        split_lo(dve, K, 1 - s, r + (n0 + s), 1024)
                    for h in range(2):
                        dve.wait_ge(out[s][h], r + 1)
                        m = K.mix[:, bass.ds(r * 2 + s, 1), h * HALF:(h + 1) * HALF].rearrange("p a n -> p (a n)")
                        nc.vector.tensor_tensor(m, m, sig[s][h][:], ALU.mult).then_inc(gated[s][h], 1)
            per_pair(nc.vector, body)

        @block.tensor
        def _(pe):
            def body(r):
                for s in range(2):
                    if s == 0 and isinstance(r, int):
                        continue
                    pe.wait_ge(K.lo_made[s], r + (n0 + 1))
                    for h in range(2):
                        above_zero(pe, out[s][h], r)
                        project_half(K, 2 * s + h, s, P, h, K.h_hi, K.h_lo)\
                            .then_inc(half0[s] if h == 0 else K.w_used[s], 1)
            per_pair(nc.tensor, body)


HH = RH // 2
RP = HH // 2


def ret_units(half):
    return ([("q", C_RQ + (half * RP + i) * P, i) for i in range(RP)] + [("k", C_RK + (half * RP + i) * P, i) for i in range(RP)]
            + [("v", C_RV + (half * HH + i) * P, i) for i in range(HH)])


def phase_ret_project(K, ctx, A, R, half, n0, next_units):
    nc = K.nc
    units = ret_units(half)
    half0, out = half_stream(K, f"rp{half}")
    sem = lambda n: K.sem(f"rp{half}_{n}")
    tmp = [ctx.enter_context(nc.sbuf_tensor(f"ret{half}_tmp{i}", [P, SEQ], F32)) for i in range(2)]
    turned, turned_out = sem("turned"), sem("turned_out")
    zeroed, spread = sem("q_zeroed"), sem("q_spread")
    turns = [u for u, unit in enumerate(units) if unit[0] in "kv"]

    def turn_source(u):
        kind, _, i = units[u]
        return R.k[:, i, :] if kind == "k" else tmp[i % 2][:]

    with nc.Block() as block:
        @block.gpsimd
        def _(pool):
            for row in range(2):
                nc.gpsimd.memset(R.out[row * RDK:(row + 1) * RDK, 1 - row::2, :], 0.0).then_inc(zeroed, 1)

        @block.sync
        def _(sp):
            for u in range(2, len(units)):
                load_unit(sp, K, u % 2, n0 + u // 2, w_in_unit(A["w_in"][0], units[u][1], P), P)
            for s, (c0, width) in enumerate(next_units):
                load_unit(sp, K, s, n0 + len(units) // 2, w_in_unit(A["w_in"][0], c0, width), width)

        @block.scalar
        def _(act):
            for u, (kind, c0, i) in enumerate(units):
                s, n = u % 2, n0 + (u + 1) // 2
                split_hi(act, K, (u + 1) % 2, n, n, 1024)
                for h in range(2):
                    act.wait_ge(half0[s] if h == 0 else K.w_used[s], u // 2 + 1 + (0 if h == 0 else n0))
                    toks = slice(h * HALF, (h + 1) * HALF)
                    if kind == "v":
                        above_zero(act, turned, 2 * (turns.index(u) - 1) if i >= 2 else 0)
                        dst = tmp[i % 2][:, toks]
                    else:
                        dst = (R.q if kind == "q" else R.k)[:, i, toks]
                    nc.scalar.activation(dst, K.ps[:, 2 * s + h, :], ACT.Copy).then_inc(out[s][h], 1)

        @block.vector
        def _(dve):
            def turn_out(u):
                kind, _, i = units[u]
                t = turns.index(u)
                for h in range(2):
                    dve.wait_ge(turned, 2 * t + h + 1)
                    src = K.ps[:, 4 + 2 * (t % 2) + h, :].rearrange("p (t c) -> p t c", t=4)
                    if kind == "v":
                        nc.vector.tensor_copy(R.v[:, 4 * h:4 * h + 4, i, :], src).then_inc(turned_out, 1)
                    else:
                        for a in range(2):
                            head = half * HH + 2 * i + a
                            nc.vector.tensor_scalar(R.kz[:, 4 * h:4 * h + 4, i, a * RDK:(a + 1) * RDK],
                                                    src[:, :, a * RDK:(a + 1) * RDK],
                                                    K.const("zeta")[:, head:head + 1], None, ALU.mult).then_inc(turned_out, 1)

            for u in range(len(units)):
                n = n0 + (u + 1) // 2
                split_lo(dve, K, (u + 1) % 2, n, 1024)
                if units[u][0] == "q":
                    i = units[u][2]
                    for h in range(2):
                        toks = slice(h * HALF, (h + 1) * HALF)
                        dve.wait_ge(out[u % 2][h], u // 2 + 1)
                        for a in range(2):
                            rows = slice(a * RDK, (a + 1) * RDK)
                            nc.vector.tensor_copy(R.out[rows, 2 * i + a, toks], R.q[rows, i, toks]).then_inc(spread, 1)
                if u - 1 in turns:
                    turn_out(u - 1)
            turn_out(len(units) - 1)

        @block.tensor
        def _(pe):
            counts = [0]
            for u in turns:
                counts.append(counts[-1] + (4 if units[u][0] == "k" else 2))

            def turn(u):
                t = turns.index(u)
                above_zero(pe, turned_out, counts[max(0, t - 1)])
                for h in range(2):
                    pe.wait_ge(out[u % 2][h], u // 2 + 1)
                    for i in range(4):
                        last = nc.tensor.transpose(K.ps[:, 4 + 2 * (t % 2) + h, i * P:(i + 1) * P],
                                                   turn_source(u)[:, (4 * h + i) * P:(4 * h + i + 1) * P], K.ident[:])
                    last.then_inc(turned, 1)

            for u in range(len(units)):
                s = u % 2
                pe.wait_ge(K.lo_made[s], n0 + u // 2 + 1)
                for h in range(2):
                    above_zero(pe, out[s][h], u // 2)
                    project_half(K, 2 * s + h, s, P, h, K.h_hi, K.h_lo).then_inc(half0[s] if h == 0 else K.w_used[s], 1)
                if u - 1 in turns:
                    turn(u - 1)
            turn(len(units) - 1)


def phase_ret_chunks(K, ctx, A, R, half, n0, gates):
    nc = K.nc
    sb = lambda n, s: ctx.enter_context(nc.sbuf_tensor(f"rc{half}_{n}", s, F32))
    sem = lambda n: K.sem(f"rc{half}_{n}")
    dmat = sb("dmat", [P, HH, P])
    inner = sb("inner", [P, 2, HH, P])
    state = sb("state", [P, HH, RDV])
    o, y = sb("o", [P, 2, HH, P]), sb("y", [P, 2, HH, P])
    stats, mv, rstd = sb("stats", [P, 2, HH, 6]), sb("mv", [P, 2, HH, 2]), sb("rstd", [P, 2, HH])
    d_landed, zeroed, scores, decayed = sem("d_landed"), sem("zeroed"), sem("scores"), sem("decayed")
    summed, updated, queried = sem("summed"), sem("updated"), sem("queried")
    state_set, scaled, stat, agg = sem("state_set"), sem("scaled"), sem("stat"), sem("agg")
    var_eps, inv_std, normed, turned, turned_out = sem("var_eps"), sem("inv_std"), sem("normed"), sem("turned"), sem("turned_out")
    heads = [(a, a // 2, (a % 2) * RDK) for a in range(HH)]
    bank = lambda b: K.ps[:, b, :].rearrange("p (a c) -> p a c", c=P)
    score_bank, o_bank = lambda n: bank(n % 2), lambda n: bank(2 + n % 2)
    update_bank, turn_bank = lambda n: bank(4 + n % 2), lambda n: bank(6 + n % 2)
    gain = K.gains[:, 2, :]

    with nc.Block() as block:
        @block.sync
        def _(sp):
            a, b = CONST_AT["dmat"]
            w = (b - a) // 2
            sp.dma_start(dmat[:], A["consts"][:, a + half * w:a + (half + 1) * w].rearrange("p (h n) -> p h n", n=P))\
                .then_inc(d_landed, 16)

        @block.tensor
        def _(pe):
            def score(n):
                above_zero(pe, decayed, n - 1)
                toks = slice(n * P, (n + 1) * P)
                for pair in range(RP):
                    m = nc.tensor.matmul(score_bank(n)[:, 2 * pair:2 * pair + 2, :], R.k[:, pair, toks],
                                         R.out[:, 2 * pair:2 * pair + 2, toks], start=True, stop=True)
                m.then_inc(scores, 1)

            def turn(n):
                pe.wait_ge(normed, HH * (n + 1))
                above_zero(pe, turned_out, HH * (n - 1))
                for a in range(HH):
                    m = nc.tensor.transpose(turn_bank(n)[:, a, :], y[:, n % 2, a, :], K.ident[:])
                m.then_inc(turned, 1)

            score(0)
            for n in range(NT):
                toks = slice(n * P, (n + 1) * P)
                above_zero(pe, scaled, HH * (n - 1))
                if n:
                    pe.wait_ge(state_set, HH * n)
                    for pair in range(RP):
                        m = nc.tensor.matmul(o_bank(n)[:, 2 * pair:2 * pair + 2, :], R.q[:, pair, toks],
                                             state[:, 2 * pair:2 * pair + 2, :], start=(pair == 0), stop=False)
                    m.then_inc(queried, 1)
                if n + 1 < NT:
                    for pair in range(RP):
                        m = nc.tensor.matmul(update_bank(n)[:, 2 * pair:2 * pair + 2, :], R.kz[:, n, pair, :],
                                             R.v[:, n, 2 * pair:2 * pair + 2, :], start=True, stop=True)
                    m.then_inc(updated, 1)
                    score(n + 1)
                pe.wait_ge(decayed, n + 1)
                for a in range(HH):
                    m = nc.tensor.matmul(o_bank(n)[:, a, :], inner[:, n % 2, a, :], R.v[:, n, a, :],
                                         start=(n == 0 and a == 0), stop=(a == HH - 1))
                m.then_inc(summed, 1)
                if n >= 3:
                    turn(n - 3)
            pe.wait_ge(K.lo_made[0], n0 + 1)
            pe.wait_ge(decayed, NT)
            project_half(K, 0, 0, P, 0, K.h_hi, K.h_lo).then_inc(gates[0][0], 1)
            for n in range(NT - 3, NT):
                turn(n)
                if n == NT - 3:
                    project_half(K, 1, 0, P, 1, K.h_hi, K.h_lo).then_inc(K.w_used[0], 1)

        @block.vector
        def _(dve):
            def decay(n):
                dve.wait_ge(scores, n + 1)
                nc.vector.tensor_tensor(inner[:, n % 2], score_bank(n), dmat[:], ALU.mult).then_inc(decayed, 1)

            def norm(n):
                for a in range(HH):
                    dve.wait_ge(scaled, HH * n + a + 1)
                    nc.vector.bn_stats(stats[:, n % 2, a, :], o[:, n % 2, a, :]).then_inc(stat, 1)
                for a in range(HH):
                    dve.wait_ge(stat, HH * n + a + 1)
                    nc.vector.bn_aggr(mv[:, n % 2, a, :], stats[:, n % 2, a, :]).then_inc(agg, 1)

            def normalise(n):
                dve.wait_ge(inv_std, n + 1)
                above_zero(dve, turned, n - 1)
                for a in range(HH):
                    nc.vector.tensor_scalar(y[:, n % 2, a, :], o[:, n % 2, a, :], mv[:, n % 2, a, 0:1],
                                            rstd[:, n % 2, a:a + 1], ALU.subtract, ALU.mult).then_inc(normed, 1)

            dve.wait_ge(d_landed, 16)
            dve.wait_ge(zeroed, 1)
            decay(0)
            split_lo(dve, K, 1, n0, 1024)
            for n in range(NT + 2):
                if n + 1 < NT:
                    dve.wait_ge(updated, n + 1)
                    above_zero(dve, queried, n)
                    for a, pair, row in heads:
                        rows = slice(row, row + RDK)
                        src = update_bank(n)[rows, a, :]
                        if n == 0:
                            nc.vector.tensor_copy(state[rows, a, :], src).then_inc(state_set, 1)
                        else:
                            c = half * RP + pair
                            nc.vector.scalar_tensor_tensor(out=state[rows, a, :], in0=state[rows, a, :],
                                                           scalar=K.const("decay")[rows, c:c + 1], in1=src,
                                                           op0=ALU.mult, op1=ALU.add).then_inc(state_set, 1)
                    decay(n + 1)
                if 1 <= n <= NT:
                    norm(n - 1)
                if n >= 2:
                    normalise(n - 2)

        @block.gpsimd
        def _(pool):
            nc.gpsimd.memset(state[:], 0.0).then_inc(zeroed, 1)
            for n in range(NT):
                pool.wait_ge(agg, HH * (n + 1))
                above_zero(pool, normed, HH * (n - 1))
                nc.gpsimd.tensor_scalar(rstd[:, n % 2, :], mv[:, n % 2, :, 1], GN_EPS, None, ALU.add).then_inc(var_eps, 1)
                pool.wait_ge(var_eps, n + 1)
                nc.gpsimd.tensor_tensor(rstd[:, n % 2, :], rstd[:, n % 2, :], K.mhalf[:, 0:HH], ALU.pow).then_inc(inv_std, 1)

        @block.scalar
        def _(act):
            split_hi(act, K, 1, n0, n0, 1024)
            for n in range(NT + 3):
                if n < NT:
                    act.wait_ge(summed, n + 1)
                    above_zero(act, normed, HH * (n - 1))
                    for a in range(HH):
                        head = half * HH + a
                        nc.scalar.activation(o[:, n % 2, a, :], o_bank(n)[:, a, :], ACT.Copy,
                                             scale=K.const("xi")[:, head:head + 1]).then_inc(scaled, 1)
                if n >= 3:
                    c = n - 3
                    act.wait_ge(turned, c + 1)
                    for a in range(HH):
                        head = half * HH + a
                        nc.scalar.activation(R.out[:, a, c * P:(c + 1) * P], turn_bank(c)[:, a, :], ACT.Copy,
                                             scale=gain[:, head:head + 1]).then_inc(turned_out, 1)


def phase_gate_ret(K, ctx, A, R, half, n0, gates, next_units):
    nc = K.nc
    half0, out = gates
    sb = lambda n: [ctx.enter_context(nc.sbuf_tensor(f"gr{half}_{n}{h}", [P, HALF], F32)) for h in range(2)]
    sem = lambda n: [K.sem(f"gr{half}_{n}{h}") for h in range(2)]
    silu, sig = sb("silu"), sb("sig")
    silu_sig, sig_made, added = sem("silu_sig"), sem("sig_made"), sem("added")
    by_ret, by_sig = sem("by_ret"), sem("by_sig")
    wv = A["w_in"][0].rearrange("(k p) n -> p k n", p=P)
    first = [C_RG + half * HH * P, C_MA + half * HH * P]

    def per_head(engine, body):
        body(0)
        with engine.Fori(1, HH) as r:
            body(r)

    with nc.Block() as block:
        @block.sync
        def _(sp):
            with nc.sync.Fori(0, HH - 1) as r:
                for s in range(2):
                    load_unit(sp, K, s, r + (n0 + 1), wv[:, :, bass.ds(r * P + (first[s] + P), P)], P)
            for s, (src, width) in enumerate(next_units):
                load_unit(sp, K, s, n0 + HH, src, width)

        @block.scalar
        def _(act):
            def body(r):
                for s in range(2):
                    if s or not isinstance(r, int):
                        split_hi(act, K, 1 - s, r + (n0 + s), r + (n0 + s), 1024)
                    for h in range(2):
                        act.wait_ge(half0[s] if h == 0 else K.w_used[s], r + (1 if h == 0 else n0 + 1))
                        above_zero(act, added[h], r)
                        if s == 0:
                            nc.scalar.activation(silu[h][:], K.ps[:, h, :], ACT.Sigmoid).then_inc(silu_sig[h], 1)
                        else:
                            nc.scalar.activation(sig[h][:], K.ps[:, 2 + h, :], ACT.Sigmoid).then_inc(out[1][h], 1)
            per_head(nc.scalar, body)

        @block.vector
        def _(dve):
            def body(r):
                for s in range(2):
                    if s or not isinstance(r, int):
                        split_lo(dve, K, 1 - s, r + (n0 + s), 1024)
                    for h in range(2):
                        toks = slice(h * HALF, (h + 1) * HALF)
                        if s == 0:
                            dve.wait_ge(silu_sig[h], r + 1)
                            nc.vector.tensor_tensor(silu[h][:], K.ps[:, h, :], silu[h][:], ALU.mult).then_inc(out[0][h], 1)
                            dve.wait_ge(out[0][h], r + 1)
                            ret = R.out[:, bass.ds(r, 1), toks].rearrange("p a n -> p (a n)")
                            nc.vector.tensor_tensor(silu[h][:], silu[h][:], ret, ALU.mult).then_inc(by_ret[h], 1)
                        else:
                            dve.wait_ge(by_ret[h], r + 1)
                            dve.wait_ge(out[1][h], r + 1)
                            nc.vector.tensor_tensor(sig[h][:], sig[h][:], silu[h][:], ALU.mult).then_inc(by_sig[h], 1)
                            dve.wait_ge(by_sig[h], r + 1)
                            m = K.mix[:, bass.ds(r + half * HH, 1), toks].rearrange("p a n -> p (a n)")
                            nc.vector.tensor_tensor(m, m, sig[h][:], ALU.add).then_inc(added[h], 1)
            per_head(nc.vector, body)

        @block.tensor
        def _(pe):
            def body(r):
                for s in range(2):
                    if s == 0 and isinstance(r, int):
                        continue
                    pe.wait_ge(K.lo_made[s], r + (n0 + 1))
                    for h in range(2):
                        above_zero(pe, out[s][h], r)
                        project_half(K, 2 * s + h, s, P, h, K.h_hi, K.h_lo)\
                            .then_inc(half0[s] if h == 0 else K.w_used[s], 1)
            per_head(nc.tensor, body)



def wide_unit(W, m, ch):
    return W.rearrange("(k p) n -> p k n", p=P)[:, 2 * m:2 * m + 2, ch * HALF:(ch + 1) * HALF]


MIX_UNITS = [(ch, m) for ch in range(2) for m in range(NK // 2)]


class Residual:

    def __init__(self, K, ctx, tag, y, x, x_landed, row, row_landed, hi, lo, gain, spare, bank=4):
        self.K, self.y, self.x, self.x_landed, self.row, self.row_landed = K, y, x, x_landed, row, row_landed
        self.spare = spare
        sem = lambda n: K.sem(f"{tag}_{n}")
        self.squared, self.mean_made, self.rstd_made = sem("y_squared"), sem("y_mean_made"), sem("y_rstd_made")
        self.scaled, self.added = sem("y_scaled"), sem("x_added")
        self.ss, self.rstd = (ctx.enter_context(K.nc.sbuf_tensor(f"{tag}_{n}", [P, NT], F32)) for n in ("ss", "rstd"))
        self.N = NormTranspose(K, f"{tag}_n", x, y, hi, lo, gain, bank)

    def scalar(self, act, t, y_ready):
        nc, N = self.K.nc, self.N
        if t < NT:
            y_ready(act, t)
            above_zero(act, self.squared, t)
            nc.scalar.activation(self.spare[0], self.y[:, t, :], ACT.Square, accum_out=self.ss[:, t:t + 1])\
                .then_inc(self.squared, 1)
        if t >= 2:
            N.scalar_scale(act, t - 2)
        if 1 <= t <= NT:
            act.wait_ge(self.added, t)
            above_zero(act, N.squared, t - 1)
            nc.scalar.activation(self.spare[1], self.x[:, t - 1, :], ACT.Square, accum_out=N.ss[:, t - 1:t])\
                .then_inc(N.squared, 1)

    def pool(self, pool, t):
        nc, c = self.K.nc, slice(t, t + 1)
        if t < NT:
            pool.wait_ge(self.squared, t + 1)
            nc.gpsimd.tensor_scalar(self.ss[:, c], self.ss[:, c], 1.0 / DM, EPS, ALU.mult, ALU.add).then_inc(self.mean_made, 1)
            pool.wait_ge(self.mean_made, t + 1)
            nc.gpsimd.tensor_tensor(self.rstd[:, c], self.ss[:, c], self.K.mhalf[:, 0:1], ALU.pow).then_inc(self.rstd_made, 1)
        if t >= 1:
            self.N.pool_rstd(pool, t - 1)

    def vector(self, dve, t):
        nc = self.K.nc
        if t == 0:
            dve.wait_ge(self.row_landed, 16)
        dve.wait_ge(self.rstd_made, t + 1)
        nc.vector.scalar_tensor_tensor(out=self.y[:, t, :], in0=self.y[:, t, :], scalar=self.rstd[:, t:t + 1],
                                       in1=self.row[:], op0=ALU.mult, op1=ALU.mult).then_inc(self.scaled, 1)
        dve.wait_ge(self.scaled, t + 1)
        if self.x_landed is not None:
            dve.wait_ge(self.x_landed[t], 16)
        nc.vector.tensor_tensor(self.x[:, t, :], self.x[:, t, :], self.y[:, t, :], ALU.add).then_inc(self.added, 1)


def phase_mix_out(K, ctx, A, y, m_hi, m_lo, n0, next_units, ffn_half0):
    nc = K.nc
    sb = lambda n, s, d=F32: ctx.enter_context(nc.sbuf_tensor(n, s, d))
    kept_hi, kept_lo = sb("w_out_hi", [P, NK, HALF], F32R), sb("w_out_lo", [P, NK, HALF], F32R)
    row = sb("mix_gain", [P, DM])
    sem = K.sem
    m_high, m_made, done, out = sem("m_high"), sem("m_made"), sem("mo_done"), sem("mo_out")
    ended, y_out = sem("mo_ended"), sem("mo_y_out")
    x_landed, row_landed = [sem(f"mo_x_landed{t}") for t in range(NT)], sem("mo_row_landed")
    R = Residual(K, ctx, "mo_r", y, K.mix, x_landed, row, row_landed, m_hi, m_lo, K.gains[:, 1, :],
                 [sb(f"squares{i}", [P, DM])[:] for i in range(2)])
    xv = A["x"][0].rearrange("(t p) d -> p t d", p=P)
    NU = NK // 2
    LAST = NT - 2

    def kept(place, u):
        return place[:, 2 * (u - NU):2 * (u - NU) + 2, :].rearrange("p k n -> p (k n)")

    with nc.Block() as block:
        @block.sync
        def _(sp):
            sp.dma_start(row[:], A["norm_mix_post"][0].partition_broadcast(P)).then_inc(row_landed, 16)
            for u in range(2, 2 * NU):
                ch, m = MIX_UNITS[u]
                load_unit(sp, K, u % 2, n0 + u // 2, wide_unit(A["w_out"][0], m, ch), HALF)
            for t in range(NT):
                sp.wait_ge(m_made, t + 1)
                sp.dma_start(K.mix[:, t, :], xv[:, t, :]).then_inc(x_landed[t], 16)
            for s, (src, width) in enumerate(next_units):
                load_unit(sp, K, s, n0 + NU, src, width)

        @block.scalar
        def _(act):
            for u in range(NU):
                for k in (2 * u, 2 * u + 1):
                    nc.scalar.activation(m_hi[:, k, :], K.mix[:, k, :], ACT.Copy).then_inc(m_high, 1)
                if u + 1 < NU:
                    split_hi(act, K, (u + 1) % 2, n0 + (u + 1) // 2, n0 + (u + 1) // 2, 1024)
            for u in range(NU, 2 * NU):
                split_hi(act, K, u % 2, n0 + u // 2, None, 1024, kept(kept_hi, u))
            for s in range(2):
                split_hi(act, K, s, n0 + NU, n0 + NU // 2, 1024)

            def y_ready(act, t):
                act.wait_ge(y_out, t + 1)
                act.wait_ge(out, t + 1)

            for t in range(NT + 2):
                if t < NT:
                    act.wait_ge(*((ended, t + 1) if t < NT - 1 else (K.w_used[1], n0 + NU)))
                    nc.scalar.activation(y[:, t, HALF:], K.ps[:, t % 4, :], ACT.Copy).then_inc(y_out, 1)
                R.scalar(act, t, y_ready)
                if t == LAST:
                    R.N.scalar_out(act, 0)
            R.N.scalar_out(act, 1)

        @block.gpsimd
        def _(pool):
            for t in range(NT + 1):
                R.pool(pool, t)

        @block.vector
        def _(dve):
            for u in range(NU):
                for k in (2 * u, 2 * u + 1):
                    dve.wait_ge(m_high, k + 1)
                    nc.vector.tensor_tensor(m_lo[:, k, :], K.mix[:, k, :], m_hi[:, k, :].bitcast(F32), ALU.subtract)\
                        .then_inc(m_made, 1)
                if u + 1 < NU:
                    split_lo(dve, K, (u + 1) % 2, n0 + (u + 1) // 2, 1024)
            for u in range(NU, 2 * NU):
                split_lo(dve, K, u % 2, n0 + u // 2, 1024, kept(kept_lo, u), kept(kept_hi, u))
            for t in range(NT):
                dve.wait_ge(*((done, t + 1) if t < NT - 1 else (K.w_used[1], n0 + NU // 2)))
                nc.vector.tensor_copy(y[:, t, 0:HALF], K.ps[:, t, :]).then_inc(out, 1)
            for s in range(2):
                split_lo(dve, K, s, n0 + NU, 1024)
            for t in range(NT):
                R.vector(dve, t)
                if t == LAST:
                    R.N.vector_out(dve, 0)
            R.N.vector_out(dve, 1)

        @block.tensor
        def _(pe):
            for u in range(NU):
                s = u % 2
                pe.wait_ge(K.lo_made[s], n0 + u // 2 + 1)
                for kk in range(2):
                    k, cols = 2 * u + kk, slice(kk * HALF, (kk + 1) * HALF)
                    pe.wait_ge(m_made, k + 1)
                    for t in range(NT):
                        toks = slice(t * P, (t + 1) * P)
                        last = mm3(nc, K.ps[:, t, :], (m_hi[:, k, toks], m_lo[:, k, toks]),
                                   (K.w_hi[s][:, cols], K.w_lo[s][:, cols]), k == 0, k == NK - 1)
                        if k == NK - 1 and t < NT - 1:
                            last.then_inc(done, 1)
                last.then_inc(K.w_used[s], 1)
            for s in range(2):
                pe.wait_ge(K.lo_made[s], n0 + NU)
            for t in range(NT):
                toks = slice(t * P, (t + 1) * P)
                pe.wait_ge(out, t + 1)
                above_zero(pe, y_out, t - 3)
                for k in range(NK):
                    last = mm3(nc, K.ps[:, t % 4, :], (m_hi[:, k, toks], m_lo[:, k, toks]),
                               (kept_hi[:, k, :], kept_lo[:, k, :]), k == 0, k == NK - 1)
                    if t == NT - 1 and k % 2:
                        last.then_inc(K.w_used[k // 2 % 2], 1)
                if t < NT - 1:
                    last.then_inc(ended, 1)
                if t == LAST:
                    pe.wait_ge(out, NT)
                    R.N.tensor(pe, 0)
            for s in range(2):
                pe.wait_ge(K.lo_made[s], n0 + NU + 1)
                pe.wait_ge(R.N.lo_out, NK)
                pe.wait_ge(y_out, NT if s else 5)
                project_half(K, 2 * s, s, P, 0, m_hi, m_lo).then_inc(ffn_half0[s], 1)
                if s == 0:
                    R.N.tensor(pe, 1)


FPI = 2
FIT = NF // FPI


def ffn_units(A, c):
    win = A["w_ffn_in"][0].rearrange("(k p) n -> p k n", p=P)
    return [(win[:, :, bass.ds(c * (FPI * P) + (b * P + part * DFF), P)], P) for b in range(FPI) for part in range(2)]


def phase_ffn(K, ctx, A, h_hi, h_lo, total, x, n0, half0, next_units):
    nc = K.nc
    sb = lambda n, s, d=F32: ctx.enter_context(nc.sbuf_tensor(n, s, d))
    sem = K.sem
    a_hi, a_lo = sb("a_hi", [P, FPI, SEQ], F32R), sb("a_lo", [P, FPI, SEQ], F32R)
    gate = [sb(f"ffn_gate{h}", [P, HALF]) for h in range(2)]
    w2_in = [sb(f"w2_in{b}", [P, DM]) for b in range(FPI)]
    w2_hi = [sb(f"w2_hi{b}", [P, DM], F32R) for b in range(FPI)]
    w2_lo = [sb(f"w2_lo{b}", [P, DM], F32R) for b in range(FPI)]
    w2_landed = [sem(f"w2_landed{b}") for b in range(FPI)]
    w2_high, w2_low = [sem(f"w2_high{b}") for b in range(FPI)], [sem(f"w2_low{b}") for b in range(FPI)]
    sig = [sem(f"ffn_sig{h}") for h in range(2)]
    u_out = [sem(f"ffn_u_out{h}") for h in range(2)]
    v_out = [sem(f"ffn_v_out{h}") for h in range(2)]
    high = [sem(f"ffn_high{h}") for h in range(2)]
    made = [sem(f"ffn_made{h}") for h in range(2)]
    done, out = sem("ffn_done"), sem("ffn_out")
    NO = 2 * NT
    LAST = NT - 2
    row, row_landed = sb("ffn_gain", [P, DM]), sem("ffn_row_landed")
    R = Residual(K, ctx, "ffn_r", total, x, None, row, row_landed, h_hi, h_lo, None, [w[:] for w in w2_in], 0)

    def per_iteration(engine, body):
        body(0)
        with engine.Fori(1, FIT) as c:
            body(c)

    def half_ready(e, s, c, b, h):
        e.wait_ge(half0[s] if h == 0 else K.w_used[s], c * FPI + ((b if h == 0 else n0 + b) + 1))

    with nc.Block() as block:
        @block.sync
        def _(sp):
            def body(c, skip=0):
                for u, (src, width) in enumerate(ffn_units(A, c)):
                    if u >= skip:
                        load_unit(sp, K, u % 2, c * FPI + (n0 + u // 2), src, width)
                for b in range(FPI):
                    above_zero(sp, w2_high[b], c)
                    above_zero(sp, w2_low[b], c)
                    sp.dma_start(w2_in[b][:], A["w_ffn_out"][0][bass.ds(c * (FPI * P) + b * P, P), :])\
                        .then_inc(w2_landed[b], 16)
            sp.dma_start(row[:], A["norm_ffn_post"][0].partition_broadcast(P)).then_inc(row_landed, 16)
            body(0, skip=2)
            with nc.sync.Fori(1, FIT) as c:
                body(c)
            for s, (src, width) in enumerate(next_units):
                load_unit(sp, K, s, n0 + FIT * FPI, src, width)

        @block.scalar
        def _(act):
            def next_split(s, c, b):
                n = c * FPI + (n0 + b)
                split_hi(act, K, s, n, n, 1024)

            def body(c):
                if not isinstance(c, int):
                    next_split(1, c, 0)
                for b in range(FPI):
                    for h in range(2):
                        if h == 1:
                            next_split(0, c, b + 1)
                        half_ready(act, 0, c, b, h)
                        above_zero(act, made[h], c * FPI + b)
                        nc.scalar.activation(gate[h][:], K.ps[:, h, :], ACT.Sigmoid).then_inc(sig[h], 1)
                    if b == FPI - 1:
                        for i in range(FPI):
                            act.wait_ge(w2_landed[i], c * 16 + 16)
                            above_zero(act, done, c * NO)
                            nc.scalar.activation(w2_hi[i][:], w2_in[i][:], ACT.Copy).then_inc(w2_high[i], 1)
                    for h in range(2):
                        toks = slice(h * HALF, (h + 1) * HALF)
                        act.wait_ge(v_out[h], c * FPI + (b + 1))
                        nc.scalar.activation(a_hi[:, b, toks], gate[h][:], ACT.Copy).then_inc(high[h], 1)
                    if b < FPI - 1:
                        next_split(1, c, b + 1)
            per_iteration(nc.scalar, body)
            next_split(1, FIT - 1, FPI)

            def y_ready(act, t):
                if t == 0:
                    for b in range(FPI):
                        act.wait_ge(w2_low[b], FIT)
                act.wait_ge(out, (FIT - 1) * NO + 2 * t + 2)

            for t in range(NT + 2):
                R.scalar(act, t, y_ready)
                if t == LAST:
                    R.N.scalar_out(act, 0)
            R.N.scalar_out(act, 1)

        @block.gpsimd
        def _(pool):
            for t in range(NT + 1):
                R.pool(pool, t)

        @block.vector
        def _(dve):
            def outputs(c, tiles=range(NT)):
                first = isinstance(c, int) and c == 0
                for o in range(2 * tiles[0], 2 * tiles[-1] + 2):
                    t, ch = divmod(o, 2)
                    dve.wait_ge(done, c * NO + (o + 1))
                    dst, src = total[:, t, ch * HALF:(ch + 1) * HALF], K.ps[:, 4 + o % 4, :]
                    if first:
                        nc.vector.tensor_copy(dst, src).then_inc(out, 1)
                    else:
                        nc.vector.tensor_tensor(dst, src, dst, ALU.add).then_inc(out, 1)

            def next_split(s, c, b):
                split_lo(dve, K, s, c * FPI + (n0 + b), 1024)

            def body(c, before):
                if before is not None:
                    next_split(1, c, 0)
                for b in range(FPI):
                    next_split(0, c, b + 1)
                    for h in range(2):
                        dve.wait_ge(sig[h], c * FPI + (b + 1))
                        nc.vector.tensor_tensor(gate[h][:], K.ps[:, h, :], gate[h][:], ALU.mult).then_inc(u_out[h], 1)
                    if b == 0 and before is not None:
                        outputs(before)
                    if b == FPI - 1:
                        for i in range(FPI):
                            dve.wait_ge(w2_high[i], c + 1)
                            nc.vector.tensor_tensor(w2_lo[i][:], w2_in[i][:], w2_hi[i][:].bitcast(F32), ALU.subtract)\
                                .then_inc(w2_low[i], 1)
                    for h in range(2):
                        toks = slice(h * HALF, (h + 1) * HALF)
                        half_ready(dve, 1, c, b, h)
                        dve.wait_ge(u_out[h], c * FPI + (b + 1))
                        nc.vector.tensor_tensor(gate[h][:], K.ps[:, 2 + h, :], gate[h][:], ALU.mult).then_inc(v_out[h], 1)
                        dve.wait_ge(high[h], c * FPI + (b + 1))
                        nc.vector.tensor_tensor(a_lo[:, b, toks], gate[h][:], a_hi[:, b, toks].bitcast(F32),
                                                ALU.subtract).then_inc(made[h], 1)
                    if b < FPI - 1:
                        next_split(1, c, b + 1)
            body(0, None)
            body(1, 0)
            with nc.vector.Fori(2, FIT) as c:
                body(c, c - 1)
            next_split(1, FIT - 1, FPI)
            for t in range(NT + 1):
                if t < NT:
                    outputs(FIT - 1, [t])
                if t:
                    R.vector(dve, t - 1)
                if t == LAST:
                    R.N.vector_out(dve, 0)
            R.N.vector_out(dve, 1)

        @block.tensor
        def _(pe):
            def project(c, b, s, halves=(0, 1)):
                pe.wait_ge(K.lo_made[s], c * FPI + (n0 + b + 1))
                for h in halves:
                    above_zero(pe, (u_out if s == 0 else v_out)[h], c * FPI + b)
                    project_half(K, 2 * s + h, s, P, h, h_hi, h_lo).then_inc(half0[s] if h == 0 else K.w_used[s], 1)

            def outputs(c):
                for b in range(FPI):
                    pe.wait_ge(w2_low[b], c + 1)
                for o in range(NO):
                    t, ch = divmod(o, 2)
                    toks, cols = slice(t * P, (t + 1) * P), slice(ch * HALF, (ch + 1) * HALF)
                    if o % NT == 0:
                        pe.wait_ge(made[o // NT], c * FPI + FPI)
                    above_zero(pe, out, c * NO + (o - 3))
                    for b in range(FPI):
                        m = mm3(nc, K.ps[:, 4 + o % 4, :], (a_hi[:, b, toks], a_lo[:, b, toks]),
                                (w2_hi[b][:, cols], w2_lo[b][:, cols]), b == 0, b == FPI - 1)
                    m.then_inc(done, 1)

            def body(c, before):
                halves = (0, 1) if before is not None else (1,)
                project(c, 0, 0, halves)
                if before is not None:
                    outputs(before)
                project(c, 0, 1, halves)
                for b in range(1, FPI):
                    for s in range(2):
                        project(c, b, s)
            body(0, None)
            body(1, 0)
            with nc.tensor.Fori(2, FIT) as c:
                body(c, c - 1)
            outputs(FIT - 1)
            R.N.tensor(pe, 0)
            pe.wait_ge(out, FIT * NO)
            pe.wait_ge(R.N.lo_out, NK)
            for s in range(2):
                pe.wait_ge(K.lo_made[s], n0 + FIT * FPI + 1)
                for t in range(NT // 2):
                    ple_gate_tile(K, h_hi, h_lo, s, s, t)
            R.N.tensor(pe, 1)


PLE_UNITS = [(ch, m) for ch in range(2) for m in range(NK // 2 + 1)]


def ple_unit(A, u):
    ch, m = PLE_UNITS[u]
    return (wide_unit(A["w_ple_gate"][0], m, ch) if m < NK // 2 else wide_unit(A["w_ple"][0], 0, ch)), HALF


def ple_bank(t):
    return (t + 4) % 8


def ple_gate_tile(K, x_hi, x_lo, s, m, t):
    toks = slice(t * P, (t + 1) * P)
    for kk in range(2):
        k, cols = 2 * m + kk, slice(kk * HALF, (kk + 1) * HALF)
        last = mm3(K.nc, K.ps[:, ple_bank(t), :], (x_hi[:, k, toks], x_lo[:, k, toks]),
                   (K.w_hi[s][:, cols], K.w_lo[s][:, cols]), k == 0, k == NK - 1)
    return last


def phase_ple(K, ctx, A, x, x_hi, x_lo, spare, n0):
    nc = K.nc
    sem = K.sem
    p_in = spare[:, 0:2, :].rearrange("p a (t c) -> p (a t) c", c=PLE)
    p_hi = ctx.enter_context(nc.sbuf_tensor("p_hi", [P, PLE // P, SEQ], F32R))
    p_lo = ctx.enter_context(nc.sbuf_tensor("p_lo", [P, PLE // P, SEQ], F32R))
    sig = ctx.enter_context(nc.sbuf_tensor("ple_sig", [P, NT, HALF], F32))
    p_landed, p_turned, p_high, p_made = sem("p_landed"), sem("p_turned"), sem("p_high"), sem("p_made")
    gated, embedded = sem("ple_gated"), sem("ple_embedded")
    sig_made, scaled, added, stored = sem("ple_sig_made"), sem("ple_scaled"), sem("ple_added"), sem("ple_stored")
    ov = A["out"][0].rearrange("(t p) d -> p t d", p=P)
    G = NK // 2
    P_BANK = K.ps[:, ple_bank(NT - 1), :]

    with nc.Block() as block:
        @block.sync
        def _(sp):
            sp.dma_start(p_in, A["p"][0, 0].rearrange("(t p) c -> p t c", p=P)).then_inc(p_landed, 16)
            for u in range(2, len(PLE_UNITS)):
                src, width = ple_unit(A, u)
                load_unit(sp, K, u % 2, n0 + u // 2, src, width)
            for n in range(2 * NT):
                ch, t = divmod(n, NT)
                sp.wait_ge(added, n + 1)
                cols = slice(ch * HALF, (ch + 1) * HALF)
                sp.dma_start(ov[:, t, cols], x[:, t, cols]).then_inc(stored, 16)
            sp.wait_ge(stored, 16 * 2 * NT)

        @block.scalar
        def _(act):
            for n in range(4):
                k, h = divmod(n, 2)
                act.wait_ge(p_turned, n + 1)
                nc.scalar.activation(p_hi[:, k, h * HALF:(h + 1) * HALF], P_BANK, ACT.Copy).then_inc(p_high, 1)
            for u, (ch, m) in enumerate(PLE_UNITS):
                if 1 < u + 1 < len(PLE_UNITS):
                    n = n0 + (u + 1) // 2
                    split_hi(act, K, (u + 1) % 2, n, n, 1024)
                if m == G - 1:
                    for t in range(NT):
                        if t < NT - 1:
                            act.wait_ge(gated, ch * (NT - 1) + t + 1)
                        else:
                            act.wait_ge(K.w_used[u % 2], n0 + u // 2 + 1)
                        above_zero(act, scaled, (ch - 1) * NT + t + 1)
                        nc.scalar.activation(sig[:, t, :], K.ps[:, ple_bank(t), :], ACT.Sigmoid).then_inc(sig_made, 1)

        @block.vector
        def _(dve):
            for n in range(4):
                k, h = divmod(n, 2)
                dve.wait_ge(p_high, n + 1)
                toks = slice(h * HALF, (h + 1) * HALF)
                nc.vector.tensor_tensor(p_lo[:, k, toks], P_BANK, p_hi[:, k, toks].bitcast(F32), ALU.subtract)\
                    .then_inc(p_made, 1)
            for u, (ch, m) in enumerate(PLE_UNITS):
                if 1 < u + 1 < len(PLE_UNITS):
                    split_lo(dve, K, (u + 1) % 2, n0 + (u + 1) // 2, 1024)
                if m == G:
                    for t in range(NT):
                        n = ch * NT + t
                        if t < NT - 1:
                            dve.wait_ge(embedded, ch * (NT - 1) + t + 1)
                        else:
                            dve.wait_ge(K.w_used[u % 2], n0 + u // 2 + 1)
                        dve.wait_ge(sig_made, n + 1)
                        cols = slice(ch * HALF, (ch + 1) * HALF)
                        nc.vector.tensor_tensor(sig[:, t, :], K.ps[:, ple_bank(t), :], sig[:, t, :], ALU.mult).then_inc(scaled, 1)
                        dve.wait_ge(scaled, n + 1)
                        nc.vector.tensor_tensor(x[:, t, cols], x[:, t, cols], sig[:, t, :], ALU.add).then_inc(added, 1)

        @block.tensor
        def _(pe):
            def turn_p(n):
                k, h = divmod(n, 2)
                above_zero(pe, p_made, n)
                for i in range(4):
                    last = nc.tensor.transpose(P_BANK[:, i * P:(i + 1) * P], p_in[:, 4 * h + i, k * P:(k + 1) * P], K.ident[:])
                last.then_inc(p_turned, 1)

            pe.wait_ge(p_landed, 16)
            for u, (ch, m) in enumerate(PLE_UNITS):
                s = u % 2
                pe.wait_ge(K.lo_made[s], n0 + u // 2 + 1)
                for t in range(NT // 2 if u < 2 else 0, NT):
                    if u == 0:
                        turn_p(t - NT // 2)
                        if t == NT - 1:
                            pe.wait_ge(p_made, 4)
                    if m == G:
                        pe.wait_ge(sig_made, ch * NT + t + 1)
                    if m == 0 and ch:
                        pe.wait_ge(scaled, t + 1)
                    if m < G:
                        last = ple_gate_tile(K, x_hi, x_lo, s, m, t)
                    else:
                        toks = slice(t * P, (t + 1) * P)
                        for k in range(2):
                            cols = slice(k * HALF, (k + 1) * HALF)
                            last = mm3(nc, K.ps[:, ple_bank(t), :], (p_hi[:, k, toks], p_lo[:, k, toks]),
                                       (K.w_hi[s][:, cols], K.w_lo[s][:, cols]), k == 0, k == 1)
                    if t == NT - 1:
                        last.then_inc(K.w_used[s], 1)
                    elif m == G - 1:
                        last.then_inc(gated, 1)
                    elif m == G:
                        last.then_inc(embedded, 1)



def layer(nc, A):
    with ExitStack() as ctx:
        K, C = Core(), Core()
        setup(nc, ctx, K)
        small = lambda n, s: ctx.enter_context(nc.sbuf_tensor(n, s, F32))
        K.gains = small("gains", [P, 3, NK])
        K.small = small("consts", [P, SMALL_W])
        K.ss, K.rstd, K.mhalf = small("ss", [P, NT]), small("rstd", [P, NT]), small("mhalf", [P, 16])
        gb_half0 = [nc.alloc_semaphore(f"gb_first_half{s}") for s in range(2)]
        K.mix = ctx.enter_context(nc.sbuf_tensor("mix", [P, NK, SEQ], F32))
        with ExitStack() as proj:
            K.h_hi = proj.enter_context(nc.sbuf_tensor("h_hi", [P, NK, SEQ], F32R))
            K.h_lo = proj.enter_context(nc.sbuf_tensor("h_lo", [P, NK, SEQ], F32R))
            with ExitStack() as c:
                phase_norm1(K, c, A, [(0, P), (P, P)])
            with ExitStack() as attention:
                sb = lambda n, s, d=F32: attention.enter_context(nc.sbuf_tensor(n, s, d))
                C.k_hi, C.k_lo = sb("k_hi", [DK, 2, SEQ], F32R), sb("k_lo", [DK, 2, SEQ], F32R)
                C.kraw = K.mix[0:DK, 6:8, :]
                C.vs, C.vw = (K.mix[:, c, :].rearrange("p (t c) -> p t c", t=NT) for c in (4, 5))
                C.gate = sb("branch_gate", [P, NT, 3 * NH])
                C.kc_hi, C.kc_lo = sb("kc_hi", [DK, NG, NB], F32R), sb("kc_lo", [DK, NG, NB], F32R)
                C.vcmp = sb("v_cmp", [P, NG, P], F32R)
                with ExitStack() as c:
                    C.kc = c.enter_context(nc.sbuf_tensor("kc", [DK, NG, SEQ], F32))
                    C.vc = c.enter_context(nc.sbuf_tensor("vc", [P, SEQ], F32))
                    C.vtmp = c.enter_context(nc.sbuf_tensor("cmp_values", [P, 2, SEQ], F32))
                    C.kfirst = c.enter_context(nc.sbuf_tensor("k_first", [DK, 2, SEQ], F32))
                    weight = lambda n, s: c.enter_context(nc.sbuf_tensor(n, s, F32))
                    C.cmp_weights = (weight("w1k", [DK, CMP_LEN, DK]), weight("w1v", [P, CMP_LEN, DV]),
                                     weight("w2k", [DK, DK]), weight("w2v", [DV, DV]),
                                     weight("pek", [DK, CMP_LEN]), weight("pev", [P, CMP_LEN]))
                    with ExitStack() as c2:
                        phase_kv(K, c2, A, C, [(C_NQ, DK), (C_NQ + DK, DK)])
                    with ExitStack() as c2:
                        phase_compress(K, c2, A, C)
                with ExitStack() as c:
                    phase_attention(K, c, A, C, len(KV_UNITS) // 2, [(C_MB, P), (C_MB + P, P)], gb_half0[0])
            n = len(KV_UNITS) // 2 + NH // 2
            K.renew()
            with ExitStack() as c:
                phase_gate_nsa(K, c, A, n, gb_half0, [(u[1], P) for u in ret_units(0)[:2]])
            n += NK // 2
            with ExitStack() as retention:
                R = Core()
                sb = lambda n, s: retention.enter_context(nc.sbuf_tensor(n, s, F32))
                R.q, R.k = sb("ret_q", [P, RP, SEQ]), sb("ret_k", [P, RP, SEQ])
                R.kz, R.v = sb("ret_kz", [P, NT, RP, P]), sb("ret_v", [P, NT, HH, P])
                R.out = sb("ret_out", [P, HH, SEQ])
                for half in range(2):
                    with ExitStack() as c:
                        phase_ret_project(K, c, A, R, half, n, [(C_RG + half * HH * P, P), (C_MA + half * HH * P, P)])
                    n += len(ret_units(half)) // 2
                    gates = half_stream(K, f"gr{half}")
                    with ExitStack() as c:
                        phase_ret_chunks(K, c, A, R, half, n, gates)
                    with ExitStack() as c:
                        if half == 0:
                            after = [(w_in_unit(A["w_in"][0], u[1], P), P) for u in ret_units(1)[:2]]
                        else:
                            after = [(wide_unit(A["w_out"][0], m, ch), HALF) for ch, m in MIX_UNITS[:2]]
                        phase_gate_ret(K, c, A, R, half, n, gates, after)
                    n += HH
                K.renew()

        tail = ctx.enter_context(ExitStack())
        y = tail.enter_context(nc.sbuf_tensor("y", [P, NT, DM], F32))
        m_hi = tail.enter_context(nc.sbuf_tensor("m_hi", [P, NK, SEQ], F32R))
        m_lo = tail.enter_context(nc.sbuf_tensor("m_lo", [P, NK, SEQ], F32R))
        ffn_half0 = [K.sem(f"ffn_half0_{s}") for s in range(2)]
        with ExitStack() as c:
            phase_mix_out(K, c, A, y, m_hi, m_lo, n, ffn_units(A, 0)[:2], ffn_half0)
        n += len(MIX_UNITS) // 2
        x = K.mix
        with ExitStack() as c:
            phase_ffn(K, c, A, m_hi, m_lo, y, x, n, ffn_half0, [ple_unit(A, 0), ple_unit(A, 1)])
        n += FIT * FPI
        with ExitStack() as c:
            phase_ple(K, c, A, x, m_hi, m_lo, y, n)

_INS = ["x", "p", "norm_mix_pre", "norm_mix_post", "norm_ffn_pre", "norm_ffn_post", "w_in", "ret_gn_g",
        "cmp_pe_k", "cmp_w1_k", "cmp_w2_k", "cmp_pe_v", "cmp_w1_v", "cmp_w2_v",
        "w_out", "w_ffn_in", "w_ffn_out", "w_ple", "w_ple_gate"]


def kernel(**inputs):
    import concourse.bacc as _bacc
    from concourse.bass_utils import run_bass_kernel_spmd as _run

    nc = _bacc.Bacc("TRN2", target_bir_lowering=False, num_devices=1)
    given = {name: np.ascontiguousarray(inputs[name]) for name in _INS}
    given.update(laid_out(inputs))
    arrays, A = {}, {}
    for name, a in given.items():
        arrays[f"in_{name}"] = a
        A[name] = nc.dram_tensor(f"in_{name}", a.shape, mybir.dt.from_np(a.dtype), kind="ExternalInput").ap()
    A["out"] = nc.dram_tensor("out", (1, SEQ, DM), F32, kind="ExternalOutput").ap()
    layer(nc, A)
    return _run(nc, [arrays], core_ids=[0]).results[0]["out"]
```
